# Optimizing a Trainium2 kernel written in Bass

```python
import math
import jax, jax.numpy as jnp
from jax import lax
import numpy as np

D_MODEL = 2048
BATCH = 1
SEQ = 256
DEPTH = 2

CHUNK = 64
Q_BLOCK = 128
HA = 8
A_NOPE = 128
A_ROPE = 64
A_V = 128
Q_RANK = 384
KV_RANK = 128
ROPE_THETA = 10000.0
HB = 4
B_DH = 64
HC = 4
C_DH = 128
LEFT_CHUNKS = 8
REL_CLIP = 256
REL_SIZE = REL_CLIP + CHUNK
MIX_WIDTH = HA * A_V + HB * 2 * B_DH + HC * C_DH
IN_SIZES = (Q_RANK, KV_RANK, A_ROPE,
            HB * 2 * B_DH, HB * 2 * B_DH, HB * 2 * B_DH,
            HC * C_DH, HC * C_DH, HC * C_DH)
IN_WIDTH = sum(IN_SIZES)
D_FF = 4 * D_MODEL
EPS = 1e-6
NEG = -1e30


def rms_norm(x, g):
    xf = x.astype(jnp.float32)
    y = xf * lax.rsqrt(jnp.mean(xf * xf, axis=-1, keepdims=True) + EPS)
    return (y * g.astype(jnp.float32)).astype(x.dtype)

def apply_rope(x, pos):
    half = x.shape[-1] // 2
    inv_freq = ROPE_THETA ** (-jnp.arange(half, dtype=jnp.float32) / half)
    ang = pos.astype(jnp.float32)[:, None] * inv_freq[None, :]
    cos = jnp.cos(ang)[:, None, :]
    sin = jnp.sin(ang)[:, None, :]
    xf = x.astype(jnp.float32)
    x1, x2 = xf[..., :half], xf[..., half:]
    return jnp.concatenate([x1 * cos - x2 * sin, x2 * cos + x1 * sin], axis=-1).astype(x.dtype)

def chunk_causal_mask(q_pos, seq):
    k_chunk = jnp.arange(seq) // CHUNK
    return k_chunk[None, :] <= (q_pos // CHUNK)[:, None]

def sweep_query_blocks(block_fn, q):
    b, h, s = q.shape[:3]
    nblk = s // Q_BLOCK
    qb = jnp.moveaxis(q.reshape((b, h, nblk, Q_BLOCK) + q.shape[3:]), 2, 0)
    out = lax.map(lambda a: block_fn(a[0], a[1]), (qb, jnp.arange(nblk)))
    return out.transpose(1, 0, 3, 2, 4).reshape(b, s, h * out.shape[-1])

def mla_mixer(c_q, c_kv, k_rope, q_norm, kv_norm, w_uq, w_ukv):
    b, s, _ = c_q.shape
    pos = jnp.arange(s)
    q = (rms_norm(c_q, q_norm) @ w_uq).reshape(b, s, HA, A_NOPE + A_ROPE)
    q = jnp.concatenate([q[..., :A_NOPE], apply_rope(q[..., A_NOPE:], pos)], axis=-1)
    kv = (rms_norm(c_kv, kv_norm) @ w_ukv).reshape(b, s, HA, A_NOPE + A_V)
    kr = apply_rope(k_rope[:, :, None, :], pos)
    k = jnp.concatenate([kv[..., :A_NOPE], jnp.broadcast_to(kr, (b, s, HA, A_ROPE))], axis=-1)
    q = q.transpose(0, 2, 1, 3)
    k = k.transpose(0, 2, 1, 3)
    v = kv[..., A_NOPE:].transpose(0, 2, 1, 3)
    scale = (A_NOPE + A_ROPE) ** -0.5

    def block(qb, blk):
        q_pos = blk * Q_BLOCK + jnp.arange(Q_BLOCK)
        sc = jnp.einsum('bhqd,bhkd->bhqk', qb, k).astype(jnp.float32) * scale
        sc = jnp.where(chunk_causal_mask(q_pos, s), sc, NEG)
        p = jax.nn.softmax(sc, axis=-1).astype(v.dtype)
        return jnp.einsum('bhqk,bhkd->bhqd', p, v)

    return sweep_query_blocks(block, q)

def diff_mixer(q, k, v, lq1, lk1, lq2, lk2, subln, lam_init):
    b, s, _ = q.shape
    q = q.reshape(b, s, HB, 2, B_DH).transpose(0, 2, 1, 3, 4)
    k = k.reshape(b, s, HB, 2, B_DH).transpose(0, 2, 1, 3, 4)
    v = v.reshape(b, s, HB, 2 * B_DH).transpose(0, 2, 1, 3)
    f32 = jnp.float32
    lam = (jnp.exp(jnp.sum(lq1.astype(f32) * lk1.astype(f32)))
           - jnp.exp(jnp.sum(lq2.astype(f32) * lk2.astype(f32))) + lam_init)
    slopes = 2.0 ** (-8.0 * (jnp.arange(HB, dtype=f32) + 1.0) / HB)
    k_pos = jnp.arange(s)
    scale = B_DH ** -0.5

    def block(qb, blk):
        q_pos = blk * Q_BLOCK + jnp.arange(Q_BLOCK)
        sc = jnp.einsum('bhqnd,bhknd->nbhqk', qb, k).astype(f32) * scale
        dist = jnp.abs(q_pos[:, None] - k_pos[None, :]).astype(f32)
        sc = sc - slopes[:, None, None] * dist
        sc = jnp.where(chunk_causal_mask(q_pos, s), sc, NEG)
        p = jax.nn.softmax(sc, axis=-1)
        w = (p[0] - lam * p[1]).astype(v.dtype)
        o = jnp.einsum('bhqk,bhkd->bhqd', w, v)
        return rms_norm(o, subln) * (1.0 - lam_init)

    return sweep_query_blocks(block, q)

def chunk_band_mixer(q, k, v, rel_bias):
    b, s, _ = q.shape
    nc = s // CHUNK
    win = LEFT_CHUNKS + 1
    idx = jnp.arange(nc)[:, None] + jnp.arange(win)[None, :]

    def band(t):
        t = t.reshape(b, nc, CHUNK, HC, C_DH)
        t = jnp.pad(t, ((0, 0), (LEFT_CHUNKS, 0), (0, 0), (0, 0), (0, 0)))
        return t[:, idx].reshape(b, nc, win * CHUNK, HC, C_DH)

    qc = q.reshape(b, nc, CHUNK, HC, C_DH)
    kb, vb = band(k), band(v)
    valid = (jnp.arange(nc)[:, None] - LEFT_CHUNKS + jnp.arange(win)[None, :]) >= 0
    valid = jnp.repeat(valid, CHUNK, axis=1)
    rel = LEFT_CHUNKS * CHUNK + jnp.arange(CHUNK)[:, None] - jnp.arange(win * CHUNK)[None, :]
    rel_idx = jnp.clip(rel, -(CHUNK - 1), REL_CLIP) + (CHUNK - 1)
    bias = rel_bias[:, rel_idx].astype(jnp.float32)
    sc = jnp.einsum('bcqhd,bckhd->bchqk', qc, kb).astype(jnp.float32) * (C_DH ** -0.5)
    sc = sc + bias[None, None]
    sc = jnp.where(valid[None, :, None, None, :], sc, NEG)
    p = jax.nn.softmax(sc, axis=-1).astype(vb.dtype)
    o = jnp.einsum('bchqk,bckhd->bcqhd', p, vb)
    return o.reshape(b, s, HC * C_DH)

def first_inputs(seed: int = 0) -> dict:
    key = jax.random.key(seed)
    ks = jax.random.split(key, 20)
    f32 = jnp.float32
    nrm = lambda k, shape, s: jax.random.normal(k, shape, f32) * s
    gain = lambda k, shape: 1.0 + 0.02 * jax.random.normal(k, shape, f32)
    return {
        "x": nrm(ks[0], (BATCH, SEQ, D_MODEL), 1.0),
        "attn_norm": gain(ks[1], (DEPTH, D_MODEL)),
        "w_in": nrm(ks[2], (DEPTH, D_MODEL, IN_WIDTH), D_MODEL ** -0.5),
        "q_a_norm": gain(ks[3], (DEPTH, Q_RANK)),
        "kv_a_norm": gain(ks[4], (DEPTH, KV_RANK)),
        "w_uq": nrm(ks[5], (DEPTH, Q_RANK, HA * (A_NOPE + A_ROPE)), Q_RANK ** -0.5),
        "w_ukv": nrm(ks[6], (DEPTH, KV_RANK, HA * (A_NOPE + A_V)), KV_RANK ** -0.5),
        "lambda_q1": nrm(ks[7], (DEPTH, B_DH), 0.1),
        "lambda_k1": nrm(ks[8], (DEPTH, B_DH), 0.1),
        "lambda_q2": nrm(ks[9], (DEPTH, B_DH), 0.1),
        "lambda_k2": nrm(ks[10], (DEPTH, B_DH), 0.1),
        "diff_subln": gain(ks[11], (DEPTH, 2 * B_DH)),
        "rel_bias": nrm(ks[12], (DEPTH, HC, REL_SIZE), 0.1),
        "w_o": nrm(ks[13], (DEPTH, MIX_WIDTH, D_MODEL), MIX_WIDTH ** -0.5),
        "mlp_norm": gain(ks[14], (DEPTH, D_MODEL)),
        "w_up": nrm(ks[15], (DEPTH, D_MODEL, D_FF), D_MODEL ** -0.5),
        "w_down": nrm(ks[16], (DEPTH, D_FF, D_MODEL), D_FF ** -0.5),
        "final_norm": gain(ks[17], (D_MODEL,)),
    }

def first_block(x, attn_norm, w_in, q_a_norm, kv_a_norm, w_uq, w_ukv,
              lambda_q1, lambda_k1, lambda_q2, lambda_k2, diff_subln, rel_bias,
              w_o, mlp_norm, w_up, w_down, final_norm):
    split_points = np.cumsum(np.array(IN_SIZES))[:-1]
    for l in range(DEPTH):
        h = rms_norm(x, attn_norm[l])
        proj = h @ w_in[l]
        (c_q, c_kv, k_rope, qb, kb, vb, qc, kc, vc) = jnp.split(proj, split_points, axis=-1)
        out_a = mla_mixer(c_q, c_kv, k_rope, q_a_norm[l], kv_a_norm[l], w_uq[l], w_ukv[l])
        lam_init = 0.8 - 0.6 * math.exp(-0.3 * l)
        out_b = diff_mixer(qb, kb, vb, lambda_q1[l], lambda_k1[l], lambda_q2[l],
                           lambda_k2[l], diff_subln[l], lam_init)
        out_c = chunk_band_mixer(qc, kc, vc, rel_bias[l])
        mixed = jnp.concatenate([out_a, out_b, out_c], axis=-1)
        x = x + mixed @ w_o[l]
        h = rms_norm(x, mlp_norm[l])
        x = x + jnp.square(jax.nn.relu(h @ w_up[l])) @ w_down[l]
    return rms_norm(x, final_norm)


DEPTH_2 = 1

N_META = 16
HEAD_DIM = 64
ATTN_WIDTH = D_MODEL // 2
N_HEADS = ATTN_WIDTH // HEAD_DIM
N_KV_HEADS = N_HEADS // 4
KV_GROUP = N_HEADS // N_KV_HEADS
KV_WIDTH = N_KV_HEADS * HEAD_DIM
SSM_WIDTH = D_MODEL - ATTN_WIDTH
SSM_GROUP_CH = 16
SSM_GROUPS = SSM_WIDTH // SSM_GROUP_CH
SSM_STATE = 64
WINDOW = 128
BLOCK = 128
PAD = BLOCK - N_META
D_FF_2 = 4 * D_MODEL
IN_WIDTH_2 = ATTN_WIDTH + 2 * KV_WIDTH + SSM_WIDTH
NORM_EPS = 1e-6
NEG_INF = -1e30
STEP_MIN = 1e-3
STEP_MAX = 1e-1


def _rmsnorm(x, g):
    xf = x.astype(jnp.float32)
    y = xf * lax.rsqrt(jnp.mean(xf * xf, axis=-1, keepdims=True) + NORM_EPS)
    return (y * g.astype(jnp.float32)).astype(x.dtype)

def _alibi_slopes():
    h = jnp.arange(1, N_HEADS + 1, dtype=jnp.float32)
    return jnp.exp2(-8.0 * h / N_HEADS)

def _sliding_window_attention(q, k, v, sinks):
    b, L = q.shape[0], q.shape[1]
    dtype = q.dtype
    Lp = L + PAD
    nb = Lp // BLOCK
    qf = q.astype(jnp.float32)
    kf = k.astype(jnp.float32)
    vf = v.astype(jnp.float32)
    pad4 = ((0, 0), (PAD, 0), (0, 0), (0, 0))
    qp = jnp.pad(qf, pad4).reshape(b, nb, BLOCK, N_KV_HEADS, KV_GROUP, HEAD_DIM)
    kp = jnp.pad(kf, pad4).reshape(b, nb, BLOCK, N_KV_HEADS, HEAD_DIM)
    vp = jnp.pad(vf, pad4).reshape(b, nb, BLOCK, N_KV_HEADS, HEAD_DIM)
    pad5 = ((0, 0), (1, 0), (0, 0), (0, 0), (0, 0))
    k_band = jnp.concatenate([jnp.pad(kp, pad5)[:, :-1], kp], axis=2)
    v_band = jnp.concatenate([jnp.pad(vp, pad5)[:, :-1], vp], axis=2)
    k_meta = kf[:, :N_META]
    v_meta = vf[:, :N_META]

    n_idx = jnp.arange(nb)[:, None, None]
    i_idx = jnp.arange(BLOCK)[None, :, None]
    j_idx = jnp.arange(2 * BLOCK)[None, None, :]
    t_pos = n_idx * BLOCK + i_idx - PAD
    s_pos = (n_idx - 1) * BLOCK + j_idx - PAD
    band_mask = (s_pos >= N_META) & (s_pos <= t_pos) & (t_pos - s_pos < WINDOW)
    band_dist = jnp.abs(t_pos - s_pos).astype(jnp.float32)
    m_pos = jnp.arange(N_META)[None, None, :]
    meta_mask = m_pos <= t_pos
    meta_dist = jnp.abs(t_pos - m_pos).astype(jnp.float32)

    slopes = _alibi_slopes().reshape(N_KV_HEADS, KV_GROUP, 1, 1)
    scale = 1.0 / math.sqrt(HEAD_DIM)
    s_band = jnp.einsum('bnqkgd,bnskd->bnkgqs', qp, k_band) * scale
    s_band = s_band - slopes * band_dist[:, None, None]
    s_band = jnp.where(band_mask[:, None, None], s_band, NEG_INF)
    s_meta = jnp.einsum('bnqkgd,bmkd->bnkgqm', qp, k_meta) * scale
    s_meta = s_meta - slopes * meta_dist[:, None, None]
    s_meta = jnp.where(meta_mask[:, None, None], s_meta, NEG_INF)
    sink = jnp.broadcast_to(sinks.astype(jnp.float32).reshape(N_KV_HEADS, KV_GROUP, 1, 1),
                            s_band.shape[:-1] + (1,))
    probs = jax.nn.softmax(jnp.concatenate([s_band, s_meta, sink], axis=-1), axis=-1)
    p_band = probs[..., :2 * BLOCK]
    p_meta = probs[..., 2 * BLOCK:2 * BLOCK + N_META]
    out = (jnp.einsum('bnkgqs,bnskd->bnqkgd', p_band, v_band)
           + jnp.einsum('bnkgqm,bmkd->bnqkgd', p_meta, v_meta))
    out = out.reshape(b, Lp, ATTN_WIDTH)[:, PAD:]
    return out.astype(dtype)

def _ssm_combine(e_i, e_j):
    a_i, b_i = e_i
    a_j, b_j = e_j
    return a_j * a_i, a_j * b_i + b_j

def _s5_mixer(u, lam_re, lam_im, log_step, b_re, b_im, c_re, c_im, d, w_glu, b_glu):
    dtype = u.dtype
    b, L = u.shape[0], u.shape[1]
    ul = jnp.moveaxis(u.astype(jnp.float32).reshape(b, L, SSM_GROUPS, SSM_GROUP_CH), 1, 0)
    lam = lax.complex(lam_re.astype(jnp.float32), lam_im.astype(jnp.float32))
    delta = jnp.exp(log_step.astype(jnp.float32))[:, None]
    lam_bar = jnp.exp(lam * delta)
    b_c = lax.complex(b_re.astype(jnp.float32), b_im.astype(jnp.float32))
    b_bar = ((lam_bar - 1.0) / lam)[..., None] * b_c
    c_c = lax.complex(c_re.astype(jnp.float32), c_im.astype(jnp.float32))
    bu = jnp.einsum('lbgh,gph->lbgp', ul.astype(jnp.complex64), b_bar)
    a = jnp.broadcast_to(lam_bar, (L, 1, SSM_GROUPS, SSM_STATE))
    _, states = lax.associative_scan(_ssm_combine, (a, bu), axis=0)
    y = jnp.real(jnp.einsum('lbgp,ghp->lbgh', states, c_c))
    y = y + d.astype(jnp.float32).reshape(SSM_GROUPS, SSM_GROUP_CH) * ul
    y = jnp.moveaxis(y, 0, 1).reshape(b, L, SSM_WIDTH)
    g = jax.nn.gelu(y)
    out = g * jax.nn.sigmoid(g @ w_glu.astype(jnp.float32) + b_glu.astype(jnp.float32))
    return out.astype(dtype)

def second_inputs(seed: int = 0) -> dict:
    key = jax.random.key(seed)
    ks = jax.random.split(key, 24)
    f32 = jnp.float32
    nrm = lambda k, shape, s: jax.random.normal(k, shape, f32) * s
    x = jax.random.normal(ks[0], (BATCH, SEQ, D_MODEL), f32)
    meta_tokens = nrm(ks[1], (N_META, D_MODEL), 1.0)
    norm_mix_g = 1.0 + nrm(ks[2], (DEPTH_2, D_MODEL), 0.02)
    w_in = nrm(ks[3], (DEPTH_2, D_MODEL, IN_WIDTH_2), D_MODEL ** -0.5)
    q_norm_g = 1.0 + nrm(ks[4], (DEPTH_2, HEAD_DIM), 0.02)
    k_norm_g = 1.0 + nrm(ks[5], (DEPTH_2, HEAD_DIM), 0.02)
    attn_sinks = nrm(ks[6], (DEPTH_2, N_HEADS), 0.5)
    n = jnp.arange(SSM_STATE, dtype=f32)
    ssm_lambda_re = -0.5 + nrm(ks[7], (DEPTH_2, SSM_GROUPS, SSM_STATE), 1e-3)
    ssm_lambda_im = math.pi * n + nrm(ks[8], (DEPTH_2, SSM_GROUPS, SSM_STATE), 1e-3)
    ssm_log_step = jax.random.uniform(ks[9], (DEPTH_2, SSM_GROUPS), f32,
                                      math.log(STEP_MIN), math.log(STEP_MAX))
    bs = (SSM_GROUP_CH ** -0.5) / math.sqrt(2.0)
    cs = (SSM_STATE ** -0.5) / math.sqrt(2.0)
    ssm_b_re = nrm(ks[10], (DEPTH_2, SSM_GROUPS, SSM_STATE, SSM_GROUP_CH), bs)
    ssm_b_im = nrm(ks[11], (DEPTH_2, SSM_GROUPS, SSM_STATE, SSM_GROUP_CH), bs)
    ssm_c_re = nrm(ks[12], (DEPTH_2, SSM_GROUPS, SSM_GROUP_CH, SSM_STATE), cs)
    ssm_c_im = nrm(ks[13], (DEPTH_2, SSM_GROUPS, SSM_GROUP_CH, SSM_STATE), cs)
    ssm_d = nrm(ks[14], (DEPTH_2, SSM_WIDTH), 1.0)
    w_glu = nrm(ks[15], (DEPTH_2, SSM_WIDTH, SSM_WIDTH), SSM_WIDTH ** -0.5)
    b_glu = nrm(ks[16], (DEPTH_2, SSM_WIDTH), 0.01)
    attn_out_g = 1.0 + nrm(ks[17], (DEPTH_2, ATTN_WIDTH), 0.02)
    ssm_out_g = 1.0 + nrm(ks[18], (DEPTH_2, SSM_WIDTH), 0.02)
    w_out = nrm(ks[19], (DEPTH_2, D_MODEL, D_MODEL), D_MODEL ** -0.5)
    norm_mlp_g = 1.0 + nrm(ks[20], (DEPTH_2, D_MODEL), 0.02)
    w_up = nrm(ks[21], (DEPTH_2, D_MODEL, D_FF_2), D_MODEL ** -0.5)
    w_down = nrm(ks[22], (DEPTH_2, D_FF_2, D_MODEL), D_FF_2 ** -0.5)
    return {"x": x, "meta_tokens": meta_tokens, "norm_mix_g": norm_mix_g, "w_in": w_in,
            "q_norm_g": q_norm_g, "k_norm_g": k_norm_g, "attn_sinks": attn_sinks,
            "ssm_lambda_re": ssm_lambda_re, "ssm_lambda_im": ssm_lambda_im,
            "ssm_log_step": ssm_log_step, "ssm_b_re": ssm_b_re, "ssm_b_im": ssm_b_im,
            "ssm_c_re": ssm_c_re, "ssm_c_im": ssm_c_im, "ssm_d": ssm_d,
            "w_glu": w_glu, "b_glu": b_glu, "attn_out_g": attn_out_g, "ssm_out_g": ssm_out_g,
            "w_out": w_out, "norm_mlp_g": norm_mlp_g, "w_up": w_up, "w_down": w_down}

def second_block(x, meta_tokens, norm_mix_g, w_in, q_norm_g, k_norm_g, attn_sinks,
              ssm_lambda_re, ssm_lambda_im, ssm_log_step, ssm_b_re, ssm_b_im,
              ssm_c_re, ssm_c_im, ssm_d, w_glu, b_glu, attn_out_g, ssm_out_g,
              w_out, norm_mlp_g, w_up, w_down):
    b = x.shape[0]
    meta = jnp.broadcast_to(meta_tokens.astype(x.dtype)[None], (b, N_META, D_MODEL))
    h_res = jnp.concatenate([meta, x], axis=1)
    L = h_res.shape[1]
    for l in range(DEPTH_2):
        h = _rmsnorm(h_res, norm_mix_g[l])
        proj = h @ w_in[l]
        q = proj[..., :ATTN_WIDTH].reshape(b, L, N_HEADS, HEAD_DIM)
        k = proj[..., ATTN_WIDTH:ATTN_WIDTH + KV_WIDTH].reshape(b, L, N_KV_HEADS, HEAD_DIM)
        v = proj[..., ATTN_WIDTH + KV_WIDTH:ATTN_WIDTH + 2 * KV_WIDTH].reshape(b, L, N_KV_HEADS, HEAD_DIM)
        u = proj[..., ATTN_WIDTH + 2 * KV_WIDTH:]
        q = _rmsnorm(q, q_norm_g[l])
        k = _rmsnorm(k, k_norm_g[l])
        attn = _sliding_window_attention(q, k, v, attn_sinks[l])
        ssm = _s5_mixer(u, ssm_lambda_re[l], ssm_lambda_im[l], ssm_log_step[l],
                        ssm_b_re[l], ssm_b_im[l], ssm_c_re[l], ssm_c_im[l], ssm_d[l],
                        w_glu[l], b_glu[l])
        mix = jnp.concatenate([_rmsnorm(attn, attn_out_g[l]), _rmsnorm(ssm, ssm_out_g[l])], axis=-1)
        h_res = h_res + mix @ w_out[l]
        h2 = _rmsnorm(h_res, norm_mlp_g[l])
        h_res = h_res + jnp.square(jax.nn.relu(h2 @ w_up[l])) @ w_down[l]
    return h_res[:, N_META:]


_first_inputs = second_inputs


def second_inputs(seed=0):
    import zlib

    import numpy as np

    out = dict(_first_inputs(seed))
    spreads = {}
    factors = {}
    for name, (base, spread) in spreads.items():
        noise = np.random.default_rng([zlib.crc32(name.encode()), seed]).standard_normal(out[name].shape)
        drawn = base * np.exp(spread * noise) if base else spread * noise
        out[name] = __import__('jax').numpy.asarray(drawn.astype(out[name].dtype))
    for name, factor in factors.items():
        out[name] = (out[name] * factor).astype(out[name].dtype)
    return out


_narrow_inputs = second_inputs


def second_inputs(seed=0):

    out = dict(_narrow_inputs(seed))
    wider = {'norm_mix_g': 3.13,
     'q_norm_g': 7.95,
     'k_norm_g': 6.8,
     'ssm_lambda_re': 12.0,
     'b_glu': 12.0,
     'attn_out_g': 6.04,
     'ssm_out_g': 6.48,
     'norm_mlp_g': 4.27}
    for name, times in wider.items():
        mean = out[name].mean()
        out[name] = (mean + times * (out[name] - mean)).astype(out[name].dtype)
    return out


def setup_inputs(seed=0):
    out = dict(first_inputs(seed))
    for name, value in second_inputs(seed + 1).items():
        if name != "x":
            out[name + "_2"] = value
    return out


def reference(
    x, attn_norm, w_in, q_a_norm, kv_a_norm, w_uq, w_ukv, lambda_q1, lambda_k1, lambda_q2,
    lambda_k2, diff_subln, rel_bias, w_o, mlp_norm, w_up, w_down, final_norm, meta_tokens_2,
    norm_mix_g_2, w_in_2, q_norm_g_2, k_norm_g_2, attn_sinks_2, ssm_lambda_re_2,
    ssm_lambda_im_2, ssm_log_step_2, ssm_b_re_2, ssm_b_im_2, ssm_c_re_2, ssm_c_im_2, ssm_d_2,
    w_glu_2, b_glu_2, attn_out_g_2, ssm_out_g_2, w_out_2, norm_mlp_g_2, w_up_2, w_down_2,
):
    x = first_block(
        x, attn_norm, w_in, q_a_norm, kv_a_norm, w_uq, w_ukv, lambda_q1, lambda_k1, lambda_q2,
        lambda_k2, diff_subln, rel_bias, w_o, mlp_norm, w_up, w_down, final_norm,
    )
    return second_block(
        x, meta_tokens_2, norm_mix_g_2, w_in_2, q_norm_g_2, k_norm_g_2, attn_sinks_2,
        ssm_lambda_re_2, ssm_lambda_im_2, ssm_log_step_2, ssm_b_re_2, ssm_b_im_2, ssm_c_re_2,
        ssm_c_im_2, ssm_d_2, w_glu_2, b_glu_2, attn_out_g_2, ssm_out_g_2, w_out_2, norm_mlp_g_2,
        w_up_2, w_down_2,
    )


_drawn_inputs = setup_inputs


def setup_inputs(seed=0):
    import zlib

    import numpy as np

    out = dict(_drawn_inputs(seed))
    spreads = {}
    factors = {'attn_norm': 3.108,
     'q_a_norm': 8.0,
     'kv_a_norm': 8.0,
     'lambda_q2': 5.735,
     'diff_subln': 4.989,
     'rel_bias': 6.687,
     'ssm_lambda_re_2': 200.0,
     'ssm_lambda_im_2': 38.464,
     'ssm_log_step_2': 41.728,
     'ssm_b_re_2': 52.624,
     'ssm_b_im_2': 53.128,
     'ssm_c_re_2': 54.672,
     'ssm_c_im_2': 53.616}
    for name, (base, spread) in spreads.items():
        noise = np.random.default_rng([zlib.crc32(name.encode()), seed]).standard_normal(out[name].shape)
        drawn = base * np.exp(spread * noise) if base else spread * noise
        out[name] = __import__('jax').numpy.asarray(drawn.astype(out[name].dtype))
    for name, factor in factors.items():
        out[name] = (out[name] * factor).astype(out[name].dtype)
    return out
```

```python
from contextlib import ExitStack

import numpy as np

import concourse.bass as bass
from concourse import mybir

F32 = mybir.dt.float32
F32R = mybir.dt.float32r
ALU = mybir.AluOpType
ACT = mybir.ActivationFunctionType
AX_X = mybir.AxisListType.X
RADD = bass.bass_isa.ReduceOp.add

P = 128
D = 2048
KT = D // P
S = 256
META = 16
L2 = META + S
DEPTH = 2
EPS = 1e-6
BIG = 1e30

HA, A_NOPE, A_ROPE, A_V = 8, 128, 64, 128
Q_RANK, KV_RANK = 384, 128
HB, HC = 4, 4
QT = Q_RANK // P
SCALE_A = (A_NOPE + A_ROPE) ** -0.5
SCALE_B = 64 ** -0.5
SCALE_C = 128 ** -0.5
SLOPES_B = [2.0 ** (-8.0 * (h + 1) / HB) for h in range(HB)]
CHUNK = 64
REL_CLIP = 256

H2, KV2, HD2 = 16, 4, 64
SLOPES_2 = [2.0 ** (-8.0 * (h + 1) / H2) for h in range(H2)]
SCALE_2 = HD2 ** -0.5
WINDOW = 128
W2 = 1024
T2 = W2 // P
PAIRS = 32
TWO_PI = 2.0 * np.pi
PI2_A, PI2_B, PI2_C = 6.28125, 1.9350051879882812e-3, 3.019915981956753e-7
MAGIC = 1.5 * 2.0 ** 23
MAGIC15 = 1.5 * 2.0 ** 8
SIN_MAX = 3.1415925
TURN_MAX = 0.4999999

C_IN = 15
C_MLA = 3
C_O = 8
C_UP = 8
FCH = 4
C_FFN = FCH * 2 * C_UP
C_LAYER = C_IN + C_MLA + C_O + C_FFN
R_LAYER = C_LAYER - C_MLA
C_IN2, C_GLU, C_O2 = 10, 2, 8
C_ALL = DEPTH * C_LAYER + C_IN2 + C_GLU + C_O2 + C_FFN
CW = 256
CE = KT * CW
assert C_LAYER % 2 == 0 and C_ALL % 2 == 0

COLS = {}
_at = 0
for _n, _w in [("attn_g", DEPTH * KT), ("mlp_g", DEPTH * KT), ("final_g", KT), ("qa_g", DEPTH * QT), ("kva_g", DEPTH),
               ("subln", DEPTH), ("mix2_g", KT), ("mlp2_g", KT), ("q2_g", 1), ("k2_g", 1), ("attn2_g", T2), ("ssm2_g", T2),
               ("ssm_d", T2), ("b_glu", T2), ("lamv", DEPTH * 4), ("lam_re", PAIRS), ("lam_im", PAIRS), ("log_step", PAIRS),
               ("sinks", H2), ("laminit", 2 * DEPTH)]:
    COLS[_n] = _at
    _at += _w
NPAR = _at

TABLES = {}
_at = 0
for _n, _w in [("ident", P), ("halves", P), ("cos", S), ("sin", S), ("mask", 384), ("dist", 384)]:
    TABLES[_n] = (_at, _w)
    _at += _w
NTAB = _at
NTAB2 = 416 + L2

DIFF0, CB0, MLA0 = 0, 8, 12
UNITS = 20
GROUPS = 16


def lam_init(l):
    return 0.8 - 0.6 * float(np.exp(-0.3 * l))


def group_of(u):
    return (u // 2, u % 2 == 1) if u < CB0 else (u - 4, True)


def mixed_tile(g):
    return g + 8 if g < 8 else g - 8


def build(nc, stream, params, tables, tables2, cbias, xT, metaT, bmat, cmat, out):
    at = [(nc.sbuf_base + 63) // 64 * 64]

    def place(name, shape, dt=F32, where=at):
        t = nc.alloc_sbuf_tensor_at(name, shape, dt, offset=where[0])
        where[0] += (int(np.prod(shape[1:])) * 4 + 31) // 32 * 32
        assert len(where) == 1 or where[0] <= where[1], (name, where)
        return t

    raw = [place(f"raw{i}", [P, KT, CW]) for i in range(2)]
    hi = [place(f"w_hi{i}", [P, KT, P], F32R) for i in range(2)]
    lo = [place(f"w_lo{i}", [P, KT, P], F32R) for i in range(2)]
    x = place("x", [P, KT, S])
    xg_at = at[0]
    xg_hi = place("xg_hi", [P, KT, L2], F32R)
    xg_lo = place("xg_lo", [P, KT, L2], F32R)
    act_at = at[0]
    act_hi = place("act_hi", [P, KT, S], F32R)
    act_lo = place("act_lo", [P, KT, S], F32R)
    act_end = at[0]
    ACT_HALF = (act_end - act_at) // 2
    par = place("par", [P, NPAR])
    tab = place("tab", [P, NTAB])
    ones = place("ones", [P, P])
    eps = place("eps", [P, 1])
    half_pi = place("half_pi", [P, 1])
    rstd = place("rstd", [P, L2])
    lamp = place("lamp", [P, DEPTH, 2])
    lams = place("lams", [P, DEPTH, 2])
    lame = place("lame", [P, DEPTH, 2])
    lamd = place("lamd", [P, DEPTH])
    nlam = place("nlam", [P, DEPTH])
    gsub = place("gsub", [P, DEPTH])
    scratch = place("scratch", [P, 1])
    magic = place("magic", [P, 1])
    eps16 = place("eps16", [P, 1])
    mag, freq, freq_hi, freq_lo, cre, cim, nre, nim, den = [
        place(f"ssm_{n}", [P, PAIRS]) for n in "mag freq freq_hi freq_lo cre cim nre nim den".split()]
    qk_g = place("qk_g", [P, 1])
    hb_glu = place("hb_glu", [P, T2])
    free_at, free_end = at[0], nc.sbuf_usable_end

    def par_at(name, i=0, n=1):
        return par[:, bass.ds(COLS[name] + i, n)]

    def table(name, a=0, b=None):
        o, w = TABLES[name]
        return tab[:, o + a:o + (w if b is None else b)]

    ident = table("ident")
    a2 = TABLES["mask"][0]
    tab2 = tab[:, a2:a2 + NTAB2]
    dist2, steps = tab2[:, 0:416], tab2[:, 416:NTAB2]
    a2 = TABLES["cos"][0]
    meta, mg = [tab[:, a2 + KT * META * i:a2 + KT * META * (i + 1)].rearrange("p (k n) -> p k n", k=KT) for i in range(2)]

    region = [free_at, free_end]
    sq = place("sq", [P, KT, L2], where=region)
    ssum = place("ssum", [P, L2], where=region)
    ssb = place("ssb", [P, L2], where=region)
    std = place("std", [P, L2], where=region)
    relu = [place(f"relu{i}", [P, S], where=region) for i in range(2)]
    rsq = [place(f"rsq{i}", [P, S], where=region) for i in range(2)]
    (dl, dr, th, turns, ang, angc, sn, cs, ab0, lb1, lbi, t0, t1) = [
        place(f"ssm_{n}", [P, PAIRS], where=region) for n in "dl dr th turns ang angc sn cs ab0 lb1 lbi t0 t1".split()]

    region = [free_at, free_end]
    proj = place("proj", [P, 30, S], where=region)
    QB, KB, VB, QC, KC, VC = range(6, 30, 4)
    sb1 = place("sb1", [P, 384], where=region)
    prob = [place(f"prob{i}", [P, 384], where=region) for i in range(4)]
    probT = [place(f"probT{i}", [P, 384], where=region) for i in range(2)]
    nmax = [place(f"nmax{i}", [P, 2], where=region) for i in range(2)]
    psums = [place(f"psums{i}", [P, 2], where=region) for i in range(2)]
    rsums = [place(f"rsums{i}", [P, 2], where=region) for i in range(2)]
    nlr = place("nlr", [P, 2], where=region)
    qr = place("qr", [P, 2, 2, S], where=region)
    cbias_sb = place("cbias_sb", [P, HC, 384], where=region)
    kr = proj[:, 4:6, :]
    region = [xg_at, act_at]
    qn = place("qn", [P, HA, S], where=region)
    kn = place("kn", [P, HA, S], where=region)
    va = place("va", [P, 2, HA * A_V], where=region)
    vb = place("vb", [P, 2, HB * P], where=region)
    vc = place("vc", [P, 2, HC * P], where=region)
    sb0 = place("sb0", [P, 384], where=region)
    sb = [sb0, sb1]
    region = [act_at, act_at + ACT_HALF // 2]
    rq = place("rq", [P, 2, 2, S], where=region)
    rkt = place("rkt", [P, 4, S], where=region)
    region = [act_at + ACT_HALF, act_at + ACT_HALF + ACT_HALF // 2]
    rt = place("rt", [P, 4, 2, S], where=region)
    region = [act_at + ACT_HALF // 2, act_at + ACT_HALF]
    csq = place("csq", [P, 4, S], where=region)
    cssb = place("cssb", [P, 2, S], where=region)
    cstd = place("cstd", [P, 2, S], where=region)
    region = [act_at + ACT_HALF + ACT_HALF // 2, act_end]
    crstd = place("crstd", [P, 2, S], where=region)
    csum = place("csum", [P, S], where=region)
    ob, osq, ostd, orstd = proj[:, VB:VB + 4, :], proj[:, VC:VC + 4, :], proj[:, 0:4, :], proj[:, KC:KC + 4, :]

    region = [free_at, free_end]
    u = place("u", [P, T2, L2], where=region)
    k2 = place("k2", [P, 2, L2], where=region)
    ks = place("ks", [P, 2, L2], where=region)
    v2 = place("v2", [P, 2, L2], where=region)
    q2 = place("q2", [P, T2, S], where=region)
    vt2 = place("vt2", [P, 2, 2 * P], where=region)
    vm2 = place("vm2", [META, 2 * P], where=region)
    rq2 = place("rq2", [P, 2, H2], where=region)
    sq2 = place("sq2", [P, 2, H2], where=region)
    ssm_at = region[0]
    km = [place(f"km{i}", [P, L2], where=region) for i in range(2)]
    ph = [place(f"ph{i}", [P, L2], where=region) for i in range(2)]
    sin2 = [place(f"sin2{i}", [P, L2], where=region) for i in range(2)]
    cos2 = [place(f"cos2{i}", [P, L2], where=region) for i in range(2)]
    mprod = [place(f"mprod{i}", [P, L2], where=region) for i in range(4)]
    zr = [place(f"zr{i}", [P, L2], where=region) for i in range(2)]
    zi = [place(f"zi{i}", [P, L2], where=region) for i in range(2)]
    pprod = [place(f"pprod{i}", [P, L2], where=region) for i in range(4)]
    wr = [place(f"wr{i}", [P, L2], where=region) for i in range(2)]
    wi = [place(f"wi{i}", [P, L2], where=region) for i in range(2)]
    region = [ssm_at, free_end]
    gbuf = place("gbuf", [P, T2, S], where=region)
    gate = [place(f"gate{i}", [P, S], where=region) for i in range(2)]
    region = [act_at, act_end]
    bm = place("bm", [P, 2, T2, P], where=region)
    cm = place("cm", [P, 2, PAIRS, 32], where=region)
    cn = place("cn", [P, 2, PAIRS, 32], where=region)
    ctmp = place("ctmp", [P, 2, PAIRS, 32], where=region)
    region = [xg_at, act_at]
    SBW = 418
    sb2 = [place(f"sb2{i}", [P, SBW], where=region) for i in range(2)]
    prob2 = [place(f"prob2{i}", [P, SBW], where=region) for i in range(4)]
    bias2 = [place(f"bias2{i}", [P, 416], where=region) for i in range(2)]
    pT2 = [place(f"pT2{i}", [P, 384], where=region) for i in range(2)]
    pM2 = [place(f"pM2{i}", [META, 256], where=region) for i in range(2)]
    nmax2 = [place(f"nmax2{i}", [P, 2], where=region) for i in range(2)]
    psums2 = [place(f"psums2{i}", [P, 2], where=region) for i in range(2)]
    rsums2 = [place(f"rsums2{i}", [P, 2], where=region) for i in range(2)]
    at2 = place("at2", [P, T2, S], where=region)
    nsum = place("nsum", [P, S], where=region)
    nsb = place("nsb", [P, S], where=region)
    nstd = place("nstd", [P, S], where=region)
    nrstd = place("nrstd", [P, S], where=region)
    region = [ssm_at + 4 * (T2 + 2) * S, free_end]
    sq8 = place("sq8", [P, T2, S], where=region)

    with ExitStack() as ctx:
        bank = [ctx.enter_context(nc.psum_tensor(f"bank{i}", [P, 512], F32)) for i in range(8)]

        def sem(name):
            return ctx.enter_context(nc.semaphore(name))

        par_landed = sem("par_landed")
        tab_landed = sem("tab_landed")
        x_landed = sem("x_landed")
        landed = [sem(f"landed{i}") for i in range(2)]
        hi_ready = sem("hi_ready")
        lo_ready = sem("lo_ready")
        tile_done = sem("tile_done")
        evac_done = sem("evac_done")
        const_ready = sem("const_ready")
        lam_chain = sem("lam_chain")
        lam_sum = sem("lam_sum")
        lam_exp = sem("lam_exp")
        xhi_ready = sem("xhi_ready")
        xlo_ready = sem("xlo_ready")
        sq_ready = sem("sq_ready")
        ss_ready = sem("ss_ready")
        ssb_ready = sem("ssb_ready")
        std_ready = sem("std_ready")
        rstd_ready = sem("rstd_ready")
        hhi_ready = sem("hhi_ready")
        rr_ready = sem("rr_ready")
        hlo_ready = sem("hlo_ready")
        cb_landed = sem("cb_landed")
        csq_ready = sem("csq_ready")
        csum_ready = sem("csum_ready")
        cssb_ready = sem("cssb_ready")
        cstd_ready = sem("cstd_ready")
        crstd_ready = sem("crstd_ready")
        cn_ready = sem("cn_ready")
        krt_ready = sem("krt_ready")
        kr_ready = sem("kr_ready")
        uq_done = sem("uq_done")
        uq_out = sem("uq_out")
        rt_ready = sem("rt_ready")
        qr_ready = sem("qr_ready")
        vt_done = sem("vt_done")
        vt_out = sem("vt_out")
        qb_ready = sem("qb_ready")
        score_done = sem("score_done")
        sb_ready = sem("sb_ready")
        nmax_ready = sem("nmax_ready")
        exp_done = sem("exp_done")
        rsum_ready = sem("rsum_ready")
        map_ready = sem("map_ready")
        pn_ready = sem("pn_ready")
        tr_done = sem("tr_done")
        pt_ready = sem("pt_ready")
        pv_done = sem("pv_done")
        ob_ready = sem("ob_ready")
        osq_ready = sem("osq_ready")
        oss_done = sem("oss_done")
        ostd_ready = sem("ostd_ready")
        orstd_ready = sem("orstd_ready")
        on_ready = sem("on_ready")
        onhi_ready = sem("onhi_ready")
        onlo_ready = sem("onlo_ready")
        ohi_ready = sem("ohi_ready")
        olo_ready = sem("olo_ready")
        second_landed = sem("second_landed")
        ssm_chain = sem("ssm_chain")
        ssm_exp = sem("ssm_exp")
        ssm_const = sem("ssm_const")
        ssm_div = sem("ssm_div")
        xn_ready = sem("xn_ready")
        mg_ready = sem("mg_ready")
        meta_hi = sem("meta_hi")
        mats_landed = sem("mats_landed")
        cmul_ready = sem("cmul_ready")
        cn2_ready = sem("cn2_ready")
        bu_done = sem("bu_done")
        angle_ready = sem("angle_ready")
        phase_chain = sem("phase_chain")
        phase_ready = sem("phase_ready")
        abs_ready = sem("abs_ready")
        trig_ready = sem("trig_ready")
        bu_out = sem("bu_out")
        drive_ready = sem("drive_ready")
        scan_ready = sem("scan_ready")
        turn_ready = sem("turn_ready")
        state_ready = sem("state_ready")
        y_done = sem("y_done")
        y_out = sem("y_out")
        ksq_ready = sem("ksq_ready")
        kss_done = sem("kss_done")
        kstd_ready = sem("kstd_ready")
        krstd_ready = sem("krstd_ready")
        kn_ready = sem("kn_ready")
        ks_done = sem("ks_done")
        ks_ready = sem("ks_ready")
        v2t_done = sem("v2t_done")
        v2t_out = sem("v2t_out")
        qsq_ready = sem("qsq_ready")
        qss_done = sem("qss_done")
        qstd_ready = sem("qstd_ready")
        rq2_ready = sem("rq2_ready")
        bias2_ready = sem("bias2_ready")
        score2_done = sem("score2_done")
        sb2_ready = sem("sb2_ready")
        nmax2_ready = sem("nmax2_ready")
        exp2_done = sem("exp2_done")
        rsum2_ready = sem("rsum2_ready")
        pn2_ready = sem("pn2_ready")
        tr2_done = sem("tr2_done")
        pt2_ready = sem("pt2_ready")
        pv2_done = sem("pv2_done")
        at2_ready = sem("at2_ready")
        gelu_sq = sem("gelu_sq")
        gelu_in = sem("gelu_in")
        gelu_tanh = sem("gelu_tanh")
        gelu_ready = sem("gelu_ready")
        ghi_ready = sem("ghi_ready")
        glo_ready = sem("glo_ready")
        gate_ready = sem("gate_ready")
        gated = sem("gated")
        nsq_ready = sem("nsq_ready")
        nss_ready = sem("nss_ready")
        nssb_ready = sem("nssb_ready")
        nstd_ready = sem("nstd_ready")
        nrstd_ready = sem("nrstd_ready")
        nx_ready = sem("nx_ready")
        nhi_ready = sem("nhi_ready")
        nlo_ready = sem("nlo_ready")
        stored = sem("stored")

        block = ctx.enter_context(nc.Block())

        TILES_LAYER = 2 * R_LAYER
        T_O = 2 * C_IN
        T_FFN = T_O + 2 * C_O
        T_UP = 2 * C_UP
        H_LAYER = FCH * T_UP
        C2_LAYER = C_LAYER // 2
        OTHERS = GROUPS - HB

        T_B2 = DEPTH * TILES_LAYER
        T_GLU, T_O2 = T_B2 + 20, T_B2 + 24
        T_FFN2 = T_O2 + 16
        C2_B2 = DEPTH * C2_LAYER
        H_B2 = DEPTH * H_LAYER

        def tiles_after(s):
            return range(12 * s // PAIRS, 12 * (s + 1) // PAIRS) if s < PAIRS else range(0)

        KSS, VT2, KSW = (13, 16), (19, 22), (25, 28)

        def evacuated(T):
            return T + 5

        def multiplied(T):
            return T + 3

        def lo_count(T, half):
            return 2 * T + half + 9

        def chunk_landed(c2):
            return 16 * c2 + 16

        @block.sync
        def _(sp):
            sp.dma_start(par[:], params).then_inc(par_landed, 16)
            sp.dma_start(x[:], xT).then_inc(x_landed, 16)

            def load(c, i):
                sp.dma_start(raw[i][:], stream[c].rearrange("p (k n) -> p k n", k=KT)).then_inc(landed[i], 16)

            def load_behind(R, c, i):
                sp.wait_ge(lo_ready, 4 * R + 12)
                load(c, i)

            with sp.Fori(0, DEPTH) as l:
                for i in range(2):
                    load_behind(l * R_LAYER + i - 2, l * C_LAYER + i, i)
                sp.dma_start(cbias_sb[:], cbias[l]).then_inc(cb_landed, 16)
                with sp.Fori(0, (C_IN - 1) // 2) as q:
                    for i in range(2):
                        load_behind(l * R_LAYER + 2 * q + i, l * C_LAYER + 2 * q + i + 2, i)
                load_behind(l * R_LAYER + C_IN - 1, l * C_LAYER + C_IN + 1, 0)
                for i, c, used in ((1, 17, 3), (0, 18, 6), (1, 19, 14)):
                    sp.wait_ge(uq_done, 14 * l + used)
                    load(l * C_LAYER + c, i)
                with sp.Fori(0, (C_LAYER - 20) // 2) as q:
                    for i in range(2):
                        load_behind(l * R_LAYER + C_IN + 2 * q + i, l * C_LAYER + 20 + 2 * q + i, i)
            B2, R2 = DEPTH * C_LAYER, DEPTH * R_LAYER
            with sp.Fori(0, (C_ALL - B2) // 2) as q:
                for i in range(2):
                    load_behind(R2 + 2 * q + i - 2, B2 + 2 * q + i, i)
            T_LAST = T_FFN2 + 2 * T_UP * FCH - T_UP
            for q in range(4):
                sp.wait_ge(evac_done, evacuated(T_LAST + 4 * q + 3))
                sp.dma_start(out[:, 4 * q:4 * q + 4, :], x[:, 4 * q:4 * q + 4, :]).then_inc(stored, 16)
            sp.wait_ge(stored, 64)

        @block.tensor
        def _(pe):
            pe.sem_inc(tile_done, 2)

            def mm(o, a, b, start, stop):
                return pe.matmul(o, a, b, start=start, stop=stop, skip_group_check=True)

            def tile(T, b, j, rhs_hi, rhs_lo, before=None):
                pe.wait_ge(evac_done, T + 1)
                n = rhs_hi.shape[2]
                for h in range(2):
                    pe.wait_ge(lo_ready, lo_count(T, h))
                    for k in range(8 * h, 8 * h + 8):
                        if before is not None:
                            before(k)
                        mm(bank[b][:, 0:n], hi[j][:, k, :], rhs_hi[:, k, :], k == 0, False)
                        mm(bank[b][:, 0:n], hi[j][:, k, :], rhs_lo[:, k, :], False, False)
                        last = mm(bank[b][:, 0:n], lo[j][:, k, :], rhs_hi[:, k, :], False, k == KT - 1)
                last.then_inc(tile_done, 1)

            xh, xl = xg_hi[:, :, META:], xg_lo[:, :, META:]

            def residual_ready(n):
                def wait(k):
                    if k % 4 == 0:
                        pe.wait_ge(xlo_ready, KT * n + k + 4)
                return wait

            def ffn(T0, H0, n):
                with pe.Fori(0, FCH) as f:
                    with pe.Fori(0, C_UP // 2) as q:
                        for t in range(4):
                            tile(T0 + 2 * T_UP * f + 4 * q + t, t, t % 2, xh, xl, residual_ready(n) if t == 0 else None)

                    def hidden_ready(k):
                        if k % 4 == 0:
                            pe.wait_ge(hlo_ready, H0 + T_UP * f + k + 6)
                    with pe.Fori(0, C_UP // 2) as q:
                        for t in range(4):
                            tile(T0 + 2 * T_UP * f + T_UP + 4 * q + t, t, t % 2, act_hi, act_lo, hidden_ready if t == 0 else None)

            pe.wait_ge(const_ready, 1)
            pe.wait_ge(tab_landed, 16)
            with pe.Fori(0, DEPTH) as l:
                T0 = l * TILES_LAYER
                for t in range(6):
                    tile(T0 + t, t % 4, t % 2, xh, xl, residual_ready(2 * l) if t == 0 else None)
                with pe.Fori(0, 6) as q:
                    for t in range(4):
                        tile(T0 + 6 + 4 * q + t, (2 + t) % 4, t % 2, xh, xl)

                pe.wait_ge(cn_ready, l + 1)
                flat = [raw[i][:].rearrange("p k n -> p (k n)") for i in range(2)]
                tiles = []
                for r in (1, 0):
                    w = flat[r][:, 0:QT * 768].rearrange("p (k n) -> p k n", k=QT)
                    tiles += [(15 if r else 16, [w[:, k, 128 * t:128 * t + 128] for k in range(QT)], 0) for t in range(6)]
                tiles += [(17, [flat[1][:, 128 * t:128 * t + 128]], QT) for t in range(HA)]
                for n, (c, ws, j0) in enumerate(tiles):
                    if n in (0, 6, 12):
                        pe.wait_ge(landed[c % 2], chunk_landed(l * C2_LAYER + c // 2))
                    if n % 2 == 0 and n >= 8:
                        pe.wait_ge(uq_out, 14 * l + n // 2 - 3)
                    for k, w in enumerate(ws):
                        last = mm(bank[4 + n // 2 % 4][:, 256 * (n % 2):256 * (n % 2) + 256], w, proj[:, j0 + k, :],
                                  k == 0, k == len(ws) - 1)
                    if n % 2 == 1:
                        last.then_inc(uq_done, 1)
                for g in range(4):
                    pe.wait_ge(uq_out, 14 * l + 10 + g - 3)
                    c0 = 1024 + 512 * (g % 2)
                    mm(bank[4 + (10 + g) % 4][:], proj[:, QT, 128 * (g // 2):128 * (g // 2) + 128], flat[1][:, c0:c0 + 512], True, True)\
                        .then_inc(uq_done, 1)
                pe.wait_ge(evac_done, evacuated(T0 + T_O - 1))
                pe.wait_ge(uq_out, 14 * l + 14)
                for g, v0 in enumerate((VB, VB, VC, VC)):
                    for h in range(4):
                        last = pe.transpose(bank[4 + g][:, 128 * h:128 * h + 128],
                                            proj[:, v0 + h, 128 * (g % 2):128 * (g % 2) + 128], ident)
                    last.then_inc(vt_done, 1)

                def scores(u):
                    s = bank[4 + u % 2]
                    if u >= 2:
                        pe.wait_ge(sb_ready, UNITS * l + u - 1)
                    else:
                        pe.wait_ge(vt_out, 4 * l + 4)
                        pe.wait_ge(qb_ready, l + 1)
                    if u < CB0:
                        r = slice(64 * (u % 2), 64 * (u % 2) + 64)
                        parts = [(proj[r, QB + u // 2, :], proj[r, KB + u // 2, :])]
                    elif u < MLA0:
                        parts = [(proj[:, QC + u - CB0, :], proj[:, KC + u - CB0, :])]
                    else:
                        h = u - MLA0
                        if h == 0:
                            pe.wait_ge(qr_ready, l + 1)
                            pe.wait_ge(kr_ready, l + 1)
                        r = slice(32 * (h % 4), 32 * (h % 4) + 32)
                        parts = [(qn[:, h, :], kn[:, h, :])] + [(qr[r, e, h // 4, :], kr[r, e, :]) for e in range(2)]
                    for i, (q, k) in enumerate(parts):
                        mm(s[:, 0:128], q[:, 0:128], k[:, 0:128], i == 0, i == len(parts) - 1)
                    for i, (q, k) in enumerate(parts):
                        last = mm(s[:, 128:384], q[:, 128:256], k, i == 0, i == len(parts) - 1)
                    last.then_inc(score_done, 1)

                def turn(g, u):
                    pe.wait_ge(pn_ready, GROUPS * l + g + 1)
                    if g >= 2:
                        pe.wait_ge(pt_ready, GROUPS * l + g - 1)
                    for i in range(3):
                        last = pe.transpose(bank[6 + g % 2][:, 128 * i:128 * i + 128], prob[u % 4][:, 128 * i:128 * i + 128], ident)
                    last.then_inc(tr_done, 1)

                def values(g):
                    pe.wait_ge(pt_ready, GROUPS * l + g + 1)
                    if 2 <= g < 2 + HB:
                        pe.wait_ge(osq_ready, HB * l + g - 1)
                    elif g >= 2:
                        pe.wait_ge(olo_ready, OTHERS * l + g - 1 - HB)
                    v, h = (vb, g) if g < 4 else (vc, g - 4) if g < 8 else (va, g - 8)
                    o = bank[g % 2]
                    mm(o[:, 0:256], v[:, 0, 128 * h:128 * h + 128], probT[g % 2][:, 0:256], True, False)
                    mm(o[:, 128:256], v[:, 1, 128 * h:128 * h + 128], probT[g % 2][:, 256:384], False, True).then_inc(pv_done, 1)

                for s in range(UNITS + 3):
                    if s < UNITS:
                        scores(s)
                    if 2 <= s < UNITS + 2 and group_of(s - 2)[1]:
                        turn(group_of(s - 2)[0], s - 2)
                    if 3 <= s and group_of(s - 3)[1]:
                        values(group_of(s - 3)[0])
                    if s == 13:
                        pe.wait_ge(osq_ready, HB * l + HB)
                        for h in range(HB):
                            last = mm(bank[2 + h // 2][:, 256 * (h % 2):256 * (h % 2) + 256], ones[:], osq[:, h, :], True, True)
                        last.then_inc(oss_done, 1)
                def mixed_ready(k):
                    if k == 0:
                        pe.wait_ge(olo_ready, OTHERS * l + OTHERS)
                        pe.wait_ge(onlo_ready, HB * l + HB)

                with pe.Fori(0, C_O // 2) as q:
                    for t in range(4):
                        tile(T0 + T_O + 4 * q + t, t, t % 2, act_hi, act_lo, mixed_ready if t == 0 else None)
                ffn(T0 + T_FFN, l * H_LAYER, 2 * l + 1)
            pe.wait_ge(evac_done, evacuated(T_B2 - 1))
            with pe.Fori(0, 2) as q:
                for t in range(4):
                    tile(T_B2 + 4 * q + t, t, t % 2, xg_hi, xg_lo, residual_ready(4) if t == 0 else None)
            pe.wait_ge(mats_landed, 32)

            def drive(j):
                pe.wait_ge(evac_done, evacuated(T_B2 + j // 4))
                if j >= 2:
                    pe.wait_ge(bu_out, j - 1)
                r = slice(32 * (j % 4), 32 * (j % 4) + 32)
                for e in range(2):
                    last = mm(bank[4 + 2 * (j % 2) + e][:, 0:L2], bm[r, e, j // 4, :], u[r, j // 4, :], True, True)
                last.then_inc(bu_done, 1)

            def read_out(j):
                if j % 4 == 0:
                    pe.wait_ge(y_out, j // 4) if j else pe.wait_ge(evac_done, evacuated(T_B2 + 7))
                if j == 0:
                    pe.wait_ge(cn2_ready, 1)
                pe.wait_ge(state_ready, j + 1)
                o = bank[2][32 * (j % 4):32 * (j % 4) + 32, 0:L2]
                mm(o, cn[:, 0, j, :], wr[j % 2][:], True, False)
                mm(o, cn[:, 1, j, :], wi[j % 2][:], False, True).then_inc(y_done, 1)

            for s in range(PAIRS + 3):
                if s < PAIRS:
                    drive(s)
                if s >= 3:
                    read_out(s - 3)
                for i in tiles_after(s):
                    T = T_B2 + 8 + i
                    pe.wait_ge(evac_done, T + 3)
                    tile(T, i % 2, i % 2, *((xg_hi, xg_lo) if i < 4 else (xh, xl)))
                if s in KSS:
                    a = KSS.index(s)
                    pe.wait_ge(ksq_ready, a + 1)
                    if a:
                        pe.wait_ge(kstd_ready, a)
                    mm(bank[3][:, 0:L2], table("halves"), ks[:, a, :], True, True).then_inc(kss_done, 1)
                if s in VT2:
                    a = VT2.index(s)
                    pe.wait_ge(kstd_ready, 2)
                    pe.wait_ge(evac_done, evacuated(T_B2 + 10 + a))
                    if a:
                        pe.wait_ge(v2t_out, a)
                    for i in range(2):
                        pe.transpose(bank[3][:, 128 * i:128 * i + 128], v2[:, a, META + 128 * i:META + 128 * i + 128], ident)
                    pe.transpose(bank[3][0:META, 256:384], v2[:, a, 0:META], ident).then_inc(v2t_done, 1)
                if s in KSW:
                    a = KSW.index(s)
                    pe.wait_ge(v2t_out, 2)
                    pe.wait_ge(kn_ready, a + 1)
                    if a:
                        pe.wait_ge(ks_ready, a)
                    mm(bank[3][0:64, 0:L2], ident[:, 64:128], k2[:, a, :], True, True)
                    mm(bank[3][64:128, 0:L2], ident[:, 0:64], k2[:, a, :], True, True).then_inc(ks_done, 1)
            pe.wait_ge(ks_ready, 2)
            pe.wait_ge(qsq_ready, 1)
            for a in range(2):
                for t in range(T2):
                    last = mm(bank[3][:, 16 * a + 2 * t:16 * a + 2 * t + 2], sq8[:, t, 128 * a:128 * a + 128],
                              table("halves")[:, 0:128:64], True, True)
            last.then_inc(qss_done, 1)

            def scores2(h):
                pe.wait_ge(sb2_ready, h - 1) if h >= 2 else pe.wait_ge(bu_out, PAIRS)
                g = h // 4
                k = (k2 if g % 2 == h % 2 else ks)[64 * (h % 2):64 * (h % 2) + 64, g // 2, :]
                q = q2[64 * (h % 2):64 * (h % 2) + 64, h // 2, :]
                mm(bank[4 + h % 2][:, 0:144], q[:, 0:128], k[:, 0:144], True, True)
                mm(bank[4 + h % 2][:, 144:416], q[:, 128:256], k, True, True).then_inc(score2_done, 1)

            def turn2(h):
                pe.wait_ge(pn2_ready, h + 1)
                if h >= 2:
                    pe.wait_ge(pt2_ready, h - 1)
                elif h == 0:
                    pe.wait_ge(y_out, T2)
                    pe.wait_ge(qstd_ready, 1)
                w = prob2[h % 4]
                for i, c in enumerate((17, 161, 289)):
                    pe.transpose(bank[6 + h % 2][:, 128 * i:128 * i + 128], w[:, c:c + 128], ident)
                for i, c in enumerate((1, 145)):
                    last = pe.transpose(bank[2 + h % 2][0:META, 128 * i:128 * i + 128], w[:, c:c + META], ident)
                last.then_inc(tr2_done, 1)

            def values2(h):
                pe.wait_ge(pt2_ready, h + 1)
                if h % 2 == 0:
                    pe.wait_ge(at2_ready, h // 2 - 1) if h >= 4 else pe.wait_ge(evac_done, evacuated(T_GLU - 1))
                o = bank[h // 2 % 2][64 * (h % 2):64 * (h % 2) + 64, :]
                c = 64 * (h // 4)
                mm(o[:, 0:256], vt2[:, 0, c:c + 64], pT2[h % 2][:, 0:256], True, False)
                mm(o[:, 128:256], vt2[:, 1, c:c + 64], pT2[h % 2][:, 256:384], False, False)
                mm(o[:, 0:256], vm2[:, c:c + 64], pM2[h % 2][:], False, True).then_inc(pv2_done, 1)

            pe.wait_ge(kn_ready, 2)
            for s in range(H2 + 3):
                if s < H2:
                    scores2(s)
                if 2 <= s < H2 + 2:
                    turn2(s - 2)
                if s >= 3:
                    values2(s - 3)
            pe.wait_ge(glo_ready, 1)
            pe.wait_ge(at2_ready, T2)
            for t in range(4):
                T = T_GLU + t
                for h in range(2):
                    pe.wait_ge(lo_ready, lo_count(T, h))
                for e in range(2):
                    o = bank[t][:, 256 * e:256 * e + 256]
                    for k in range(T2):
                        mm(o, hi[t % 2][:, 2 * k + e, :], act_hi[:, 8 + k, :], k == 0, False)
                        mm(o, hi[t % 2][:, 2 * k + e, :], act_lo[:, 8 + k, :], False, False)
                        last = mm(o, lo[t % 2][:, 2 * k + e, :], act_hi[:, 8 + k, :], False, k == T2 - 1)
                last.then_inc(tile_done, 1)
            pe.wait_ge(nlo_ready, 2 * T2)
            with pe.Fori(0, C_O2 // 2) as q:
                for t in range(4):
                    tile(T_O2 + 4 * q + t, t, t % 2, act_hi, act_lo)
            ffn(T_FFN2, H_B2, 5)

        @block.scalar
        def _(act):
            act.dma_start(tab[:], tables).then_inc(tab_landed, 16)

            def split(T, c2, r, j):
                if j == 0:
                    act.wait_ge(landed[r], chunk_landed(c2))
                act.wait_ge(tile_done, T + 1)
                for h in range(2):
                    act.activation(hi[j][:, 8 * h:8 * h + 8, :], raw[r][:, 8 * h:8 * h + 8, P * j:P * j + P], ACT.Copy)\
                        .then_inc(hi_ready, 1)

            def norm(n, gain, T):
                act.wait_ge(evac_done, T + 4)
                for k in range(KT):
                    act.activation(xg_hi[:, k, META:], x[:, k, :], ACT.Copy, scale=par_at(gain[0], gain[1] + k)).then_inc(xhi_ready, 1)
                act.activation(sq[:, :, 0:S], x[:], ACT.Square).then_inc(sq_ready, 1)
                act.wait_ge(ssb_ready, n + 1)
                act.activation(std[:, 0:S], ssb[:, 0:S], ACT.Sqrt, bias=eps[:], scale=1.0 / D).then_inc(std_ready, 1)

            def ffn(T0, c2, H0, last=False):
                def up(q, f, t):
                    T = T0 + 2 * T_UP * f + 4 * q + t
                    split(T + 2, c2 + C_UP * f + q + (t // 2 + 1) // 2, (1 + t // 2) % 2, t % 2)
                    act.wait_ge(evac_done, evacuated(T))
                    act.activation(act_hi[:, bass.ds(4 * q + t, 1), :], relu[t % 2][:].rearrange("p (a n) -> p a n", a=1), ACT.Square)\
                        .then_inc(hhi_ready, 1)

                def down(q, f, t):
                    split(T0 + 2 * T_UP * f + T_UP + 4 * q + t + 2, c2 + C_UP * f + C_UP // 2 + q + (t // 2 + 1) // 2,
                          (1 + t // 2) % 2, t % 2)

                def lot(f, end):
                    with act.Fori(0, C_UP // 2) as q:
                        for t in range(4):
                            up(q, f, t)
                    with act.Fori(0, C_UP // 2 - end) as q:
                        for t in range(4):
                            down(q, f, t)

                with act.Fori(0, FCH - last) as f:
                    lot(f, 0)
                if last:
                    lot(FCH - 1, 1)
                    for t in range(2):
                        down(C_UP // 2 - 1, FCH - 1, t)

            act.wait_ge(par_landed, 16)
            act.wait_ge(tab_landed, 16)
            act.wait_ge(x_landed, 16)
            act.wait_ge(const_ready, 1)
            act.activation(dl[:], par_at("log_step", 0, PAIRS), ACT.Exp).then_inc(ssm_exp, 1)
            act.wait_ge(lam_sum, 1)
            act.activation(lame[:], lams[:], ACT.Exp).then_inc(lam_exp, 1)
            for j in range(2):
                split(j, 0, 0, j)
            act.wait_ge(ssm_chain, 1)
            act.activation(mag[:], dr[:], ACT.Exp).then_inc(ssm_exp, 1)
            act.wait_ge(ssm_chain, 11)
            act.activation(ab0[:], angc[:], ACT.Abs).then_inc(ssm_exp, 1)
            act.activation(sn[:], angc[:], ACT.Sin).then_inc(ssm_exp, 1)
            act.wait_ge(ssm_exp, 4)
            act.activation(cs[:], ab0[:], ACT.Sin, scale=-1.0, bias=half_pi[:]).then_inc(ssm_exp, 1)
            with act.Fori(0, DEPTH) as l:
                T0, c0 = l * TILES_LAYER, l * C2_LAYER
                norm(2 * l, ("attn_g", l * KT), T0)
                for c in range(3):
                    for j in range(2):
                        split(T0 + 2 * c + j + 2, c0 + (c + 1) // 2, (c + 1) % 2, j)
                act.wait_ge(evac_done, evacuated(T0 + QT))
                act.activation(csq[:], proj[:, 0:4, :], ACT.Square).then_inc(csq_ready, 1)
                for j in range(2):
                    split(T0 + 8 + j, c0 + 2, 0, j)
                act.wait_ge(cssb_ready, l + 1)
                for i, n in enumerate((Q_RANK, KV_RANK)):
                    act.activation(cstd[:, i, :], cssb[:, i, :], ACT.Sqrt, bias=eps[:], scale=1.0 / n).then_inc(cstd_ready, 1)
                for j in range(2):
                    split(T0 + 10 + j, c0 + 2, 1, j)
                with act.Fori(0, 4) as q:
                    for c in range(2):
                        for j in range(2):
                            split(T0 + 12 + 4 * q + 2 * c + j, c0 + 3 + q, c, j)
                for j in range(2):
                    split(T0 + 28 + j, c0 + 7, 0, j)
                dst = [rq[:, 0], rq[:, 1]] + [qn[:, 2 * i:2 * i + 2, :] for i in range(4)] + [kn[:, 2 * i:2 * i + 2, :] for i in range(4)]
                dst = [d.rearrange("p a n -> p (a n)") for d in dst] + [va[:, g // 2, 512 * (g % 2):512 * (g % 2) + 512] for g in range(4)]
                for i, d in enumerate(dst):
                    act.wait_ge(uq_done, 14 * l + i + 1)
                    act.activation(d, bank[4 + i % 4][:], ACT.Copy).then_inc(uq_out, 1)
                for g in range(4):
                    act.wait_ge(vt_done, 4 * l + g + 1)
                    act.activation((vb, vc)[g // 2][:, g % 2, :], bank[4 + g][:], ACT.Copy).then_inc(vt_out, 1)
                for j in range(2):
                    split(T0 + T_O + j, c0 + 9, 0, j)

                def exps(u):
                    act.wait_ge(nmax_ready, UNITS * l + u + 1)
                    if u >= 4:
                        act.wait_ge(tr_done, GROUPS * l + group_of(u - 4)[0] + 1)
                    for i, r in enumerate((slice(0, 128), slice(128, 384))):
                        last = act.activation(prob[u % 4][:, r], sb[u % 2][:, r], ACT.Exp, bias=nmax[u % 2][:, i:i + 1],
                                              accum_out=psums[u % 2][:, i:i + 1])
                    last.then_inc(exp_done, 1)

                def weights_out(g):
                    act.wait_ge(tr_done, GROUPS * l + g + 1)
                    if g >= 2:
                        act.wait_ge(pv_done, GROUPS * l + g - 1)
                    act.activation(probT[g % 2][:], bank[6 + g % 2][:, 0:384], ACT.Copy).then_inc(pt_ready, 1)

                def output(g):
                    act.wait_ge(pv_done, GROUPS * l + g + 1)
                    if g < HB:
                        act.activation(ob[:, g, :], bank[g % 2][:, 0:256], ACT.Copy).then_inc(ob_ready, 1)
                        act.activation(osq[:, g, :], bank[g % 2][:, 0:256], ACT.Square).then_inc(osq_ready, 1)
                    else:
                        act.activation(act_hi[:, mixed_tile(g), :], bank[g % 2][:, 0:256], ACT.Copy).then_inc(ohi_ready, 1)

                for s in range(UNITS + 4):
                    if s < UNITS:
                        exps(s)
                    if 2 <= s < UNITS + 2 and group_of(s - 2)[1]:
                        weights_out(group_of(s - 2)[0])
                    if s >= 4 and group_of(s - 4)[1]:
                        output(group_of(s - 4)[0])
                    if s == 14:
                        act.wait_ge(oss_done, l + 1)
                        for i in range(2):
                            act.activation(ostd[:, 2 * i:2 * i + 2, :], bank[2 + i][:].rearrange("p (a n) -> p a n", a=2), ACT.Sqrt,
                                           bias=eps[:], scale=1.0 / P).then_inc(ostd_ready, 1)
                    if 16 <= s < 16 + HB:
                        act.wait_ge(on_ready, HB * l + s - 15)
                        act.activation(act_hi[:, 8 + s - 16, :], ob[:, s - 16, :], ACT.Copy).then_inc(onhi_ready, 1)
                with act.Fori(0, C_O // 2) as q:
                    for t in range(4):
                        split(T0 + T_O + 4 * q + t + 2, c0 + 9 + q + (t // 2 + 1) // 2, (1 + t // 2) % 2, t % 2)
                norm(2 * l + 1, ("mlp_g", l * KT), T0 + T_FFN)
                ffn(T0 + T_FFN, c0 + 13, l * H_LAYER)
            act.wait_ge(mg_ready, 1)
            act.activation(xg_hi[:, :, 0:META], mg, ACT.Copy).then_inc(meta_hi, 1)
            act.wait_ge(evac_done, evacuated(T_B2 - 1))
            act.activation(sq[:, :, 0:S], x[:], ACT.Square).then_inc(sq_ready, 1)
            act.wait_ge(ssb_ready, 5)
            act.activation(std[:, 0:S], ssb[:, 0:S], ACT.Sqrt, bias=eps[:], scale=1.0 / D).then_inc(std_ready, 1)
            for k in range(KT):
                act.wait_ge(xn_ready, k + 1)
                act.activation(xg_hi[:, k, META:], x[:, k, :], ACT.Copy, scale=par_at("mix2_g", k)).then_inc(xhi_ready, 1)
            act.activation(sq[:, :, 0:META], meta, ACT.Square)
            act.activation(sq[:, :, META:], x[:], ACT.Square).then_inc(sq_ready, 1)
            act.wait_ge(ssb_ready, 6)
            act.activation(std[:], ssb[:], ACT.Sqrt, bias=eps[:], scale=1.0 / D).then_inc(std_ready, 1)

            def split_after(T):
                c = (T + 2 - T_B2) // 2
                split(T + 2, C2_B2 + c // 2, c % 2, T % 2)

            for t in range(8):
                split_after(T_B2 + t)

            def angles(j):
                if j >= 2:
                    act.wait_ge(trig_ready, j - 1)
                    act.wait_ge(phase_ready, j - 1)
                act.activation(km[j % 2][:], steps, ACT.Identity, scale=freq[:, j:j + 1], bias=magic[:])
                act.activation(ph[j % 2][:], steps, ACT.Copy, scale=freq_hi[:, j:j + 1]).then_inc(angle_ready, 1)

            def trig(j):
                act.wait_ge(phase_ready, j + 1)
                if j >= 2:
                    act.wait_ge(state_ready, j - 1)
                act.activation(km[j % 2][:], ph[j % 2][:], ACT.Abs).then_inc(abs_ready, 1)
                act.activation(sin2[j % 2][:], ph[j % 2][:], ACT.Sin, scale=TWO_PI)
                act.wait_ge(abs_ready, j + 1)
                act.activation(cos2[j % 2][:], km[j % 2][:], ACT.Sin, scale=-TWO_PI, bias=half_pi[:]).then_inc(trig_ready, 1)

            act.wait_ge(ssm_const, 1)
            act.wait_ge(second_landed, 32)
            angles(0)
            for s in range(PAIRS + 3):
                if s + 1 < PAIRS:
                    angles(s + 1)
                if s < PAIRS:
                    trig(s)
                for i in tiles_after(s):
                    split_after(T_B2 + 8 + i)
                if s + 1 in KSS:
                    a = KSS.index(s + 1)
                    act.wait_ge(evac_done, evacuated(T_B2 + 8 + a))
                    act.activation(ks[:, a, :], k2[:, a, :], ACT.Square).then_inc(ksq_ready, 1)
                if s - 1 in KSS:
                    a = KSS.index(s - 1)
                    act.wait_ge(kss_done, a + 1)
                    act.activation(ks[:, a, :], bank[3][:, 0:L2], ACT.Sqrt, bias=eps[:], scale=1.0 / HD2).then_inc(kstd_ready, 1)
                if s - 1 in VT2:
                    a = VT2.index(s - 1)
                    act.wait_ge(v2t_done, a + 1)
                    act.activation(vt2[:, :, 128 * a:128 * a + 128], bank[3][:, 0:256].rearrange("p (i n) -> p i n", i=2), ACT.Copy)
                    act.activation(vm2[:, 128 * a:128 * a + 128], bank[3][0:META, 256:384], ACT.Copy).then_inc(v2t_out, 1)
                if s - 1 in KSW:
                    a = KSW.index(s - 1)
                    act.wait_ge(ks_done, a + 1)
                    act.activation(ks[:, a, :], bank[3][:, 0:L2], ACT.Copy).then_inc(ks_ready, 1)
            act.wait_ge(evac_done, evacuated(T_GLU - 1))
            act.wait_ge(state_ready, PAIRS)
            act.wait_ge(y_done, PAIRS)
            act.activation(sq8[:], q2[:], ACT.Square).then_inc(qsq_ready, 1)
            act.wait_ge(qss_done, 1)
            act.activation(sq2[:], bank[3][:, 0:2 * H2].rearrange("p (a h) -> p a h", a=2), ACT.Sqrt, bias=eps[:], scale=1.0 / HD2)\
                .then_inc(qstd_ready, 1)
            y = u[:, :, META:]
            act.wait_ge(y_out, T2)
            act.activation(gbuf[:], y, ACT.Square).then_inc(gelu_sq, 1)
            act.wait_ge(gelu_in, 2)
            act.activation(gbuf[:], gbuf[:], ACT.Tanh, scale=float(np.sqrt(2.0 / np.pi))).then_inc(gelu_tanh, 1)
            act.wait_ge(gelu_ready, 1)
            act.activation(act_hi[:, 8:16, :], y, ACT.Copy, scale=0.5).then_inc(ghi_ready, 1)

            def exps2(h):
                act.wait_ge(nmax2_ready, h + 1)
                if h >= 4:
                    act.wait_ge(tr2_done, h - 3)
                for i, r in enumerate((slice(0, 145), slice(145, SBW))):
                    last = act.activation(prob2[h % 4][:, r], sb2[h % 2][:, r], ACT.Exp, bias=nmax2[h % 2][:, i:i + 1],
                                          accum_out=psums2[h % 2][:, i:i + 1])
                last.then_inc(exp2_done, 1)

            def weights2_out(h):
                act.wait_ge(tr2_done, h + 1)
                if h >= 2:
                    act.wait_ge(pv2_done, h - 1)
                act.activation(pM2[h % 2][:], bank[2 + h % 2][0:META, 0:256], ACT.Copy)
                act.activation(pT2[h % 2][:], bank[6 + h % 2][:, 0:384], ACT.Copy).then_inc(pt2_ready, 1)

            for s in range(H2 + 4):
                if s < H2:
                    exps2(s)
                if 2 <= s < H2 + 2:
                    weights2_out(s - 2)
                if s >= 4 and s % 2 == 1:
                    act.wait_ge(pv2_done, s - 3)
                    act.activation(at2[:, (s - 4) // 2, :], bank[(s - 4) // 2 % 2][:, 0:256], ACT.Copy).then_inc(at2_ready, 1)

            def half_norm(i, src, t0, e):
                act.activation(sq8[:], src, ACT.Square).then_inc(nsq_ready, 1)
                act.wait_ge(nssb_ready, i + 1)
                act.activation(nstd[:], nsb[:], ACT.Sqrt, bias=e[:], scale=1.0 / W2).then_inc(nstd_ready, 1)
                for t in range(T2):
                    act.wait_ge(nx_ready, T2 * i + t + 1)
                    act.activation(act_hi[:, t0 + t, :], src[:, t, :], ACT.Copy).then_inc(nhi_ready, 1)

            act.wait_ge(at2_ready, T2)
            half_norm(0, at2[:], 0, eps)
            for t in range(4):
                act.wait_ge(tile_done, multiplied(T_GLU + t))
                for e in range(2):
                    n = 4 * (t // 2) + 2 * e + t % 2
                    if 2 * t + e >= 2:
                        act.wait_ge(gated, 2 * t + e - 1)
                    act.activation(gate[e][:], bank[t][:, 256 * e:256 * e + 256], ACT.Tanh, scale=0.5, bias=hb_glu[:, n:n + 1])\
                        .then_inc(gate_ready, 1)
                split_after(T_GLU + t)
            act.wait_ge(gated, 8)
            half_norm(1, gbuf[:], 8, eps16)
            with act.Fori(0, C_O2 // 2) as q:
                for t in range(4):
                    split(T_O2 + 4 * q + t + 2, C2_B2 + 6 + q + (t // 2 + 1) // 2, (1 + t // 2) % 2, t % 2)
            norm(6, ("mlp2_g", 0), T_FFN2)
            ffn(T_FFN2, C2_B2 + 10, H_B2, last=True)

        @block.vector
        def _(dve):
            dve.sem_inc(lo_ready, 8)
            dve.sem_inc(evac_done, 4)

            def split(T, r, j):
                for h in range(2):
                    dve.wait_ge(hi_ready, 2 * T + h + 1)
                    dve.tensor_tensor(lo[j][:, 8 * h:8 * h + 8, :], raw[r][:, 8 * h:8 * h + 8, P * j:P * j + P],
                                      hi[j][:, 8 * h:8 * h + 8, :].bitcast(F32), ALU.subtract).then_inc(lo_ready, 1)

            def norm(n, gain, m=None):
                m = n if m is None else m
                for k in range(KT):
                    dve.wait_ge(xhi_ready, KT * m + k + 1)
                    dve.scalar_tensor_tensor(out=xg_lo[:, k, META:], in0=x[:, k, :], scalar=par_at(gain[0], gain[1] + k),
                                             in1=xg_hi[:, k, META:].bitcast(F32), op0=ALU.mult, op1=ALU.subtract).then_inc(xlo_ready, 1)
                dve.wait_ge(sq_ready, n + 1)
                dve.tensor_reduce(ssum[:, 0:S], sq[:, :, 0:S].rearrange("p k n -> p n k"), AX_X, ALU.add).then_inc(ss_ready, 1)
                dve.wait_ge(std_ready, n + 1)
                dve.reciprocal(rstd[:, META:], std[:, 0:S]).then_inc(rstd_ready, 1)

            def add(T, b, j):
                dve.wait_ge(tile_done, multiplied(T))
                one = bank[b][:, 0:S].rearrange("p (a n) -> p a n", a=1)
                dve.tensor_tensor(x[:, bass.ds(j, 1), :], one, x[:, bass.ds(j, 1), :], ALU.add).then_inc(evac_done, 1)

            def ffn(T0, H0, n, last=False):
                def up(q, f, t):
                    T = T0 + 2 * T_UP * f + 4 * q + t
                    if t == 0:
                        dve.wait_ge(rstd_ready, n + 1)
                    dve.wait_ge(tile_done, multiplied(T))
                    dve.wait_ge(hlo_ready, H0 + T_UP * f + 4 * q + t + 1)
                    dve.scalar_tensor_tensor(out=relu[t % 2][:], in0=bank[t][:, 0:S], scalar=0.0, in1=rstd[:, META:],
                                             op0=ALU.max, op1=ALU.mult).then_inc(evac_done, 1)
                    split(T + 2, (1 + t // 2) % 2, t % 2)

                def down(q, f, t, ahead=True):
                    T = T0 + 2 * T_UP * f + T_UP + 4 * q + t
                    add(T, t, 4 * q + t)
                    if ahead:
                        split(T + 2, (1 + t // 2) % 2, t % 2)

                def lot(f, end):
                    with dve.Fori(0, C_UP // 2) as q:
                        for t in range(4):
                            up(q, f, t)
                    with dve.Fori(0, C_UP // 2 - end) as q:
                        for t in range(4):
                            down(q, f, t)

                with dve.Fori(0, FCH - last) as f:
                    lot(f, 0)
                if last:
                    lot(FCH - 1, 1)
                    for t in range(4):
                        down(C_UP // 2 - 1, FCH - 1, t, t < 2)

            dve.wait_ge(par_landed, 16)
            dve.wait_ge(x_landed, 16)
            pairs = par_at("lamv", 0, DEPTH * 4).rearrange("p (l e v) -> p l e v", l=DEPTH, e=2)
            dve.tensor_tensor(lamp[:], pairs[:, :, :, 0], pairs[:, :, :, 1], ALU.mult).then_inc(lam_chain, 1)
            dve.tensor_tensor(gsub[:], par_at("subln", 0, DEPTH), par_at("laminit", DEPTH, DEPTH), ALU.mult).then_inc(lam_chain, 1)
            dve.wait_ge(lam_exp, 1)
            dve.tensor_tensor(lamd[:], lame[:, :, 1], lame[:, :, 0], ALU.subtract).then_inc(lam_chain, 1)
            dve.wait_ge(lam_chain, 3)
            dve.tensor_tensor(nlam[:], lamd[:], par_at("laminit", 0, DEPTH), ALU.subtract).then_inc(lam_chain, 1)
            for j in range(2):
                split(j, 0, j)
            with dve.Fori(0, DEPTH) as l:
                T0 = l * TILES_LAYER

                def project(T, b, j):
                    dve.wait_ge(tile_done, multiplied(T))
                    one = bank[b][:, 0:S].rearrange("p (a n) -> p a n", a=1)
                    dve.tensor_tensor(proj[:, bass.ds(j, 1), :], one, rstd[:, META:].rearrange("p (a n) -> p a n", a=1), ALU.mult)\
                        .then_inc(evac_done, 1)

                norm(2 * l, ("attn_g", l * KT))
                dve.wait_ge(rstd_ready, 2 * l + 1)
                for t in range(6):
                    project(T0 + t, t % 4, t)
                    split(T0 + t + 2, (t // 2 + 1) % 2, t % 2)
                for t in range(6, 8):
                    project(T0 + t, t % 4, t)
                    split(T0 + t + 2, 0, t % 2)
                dve.wait_ge(cstd_ready, 2 * l + 2)
                dve.reciprocal(crstd[:], cstd[:]).then_inc(crstd_ready, 1)
                for t in range(8, 10):
                    project(T0 + t, t % 4, t)
                    split(T0 + t + 2, 1, t % 2)
                dve.wait_ge(crstd_ready, l + 1)
                for j in range(QT + 1):
                    g = par_at("qa_g", l * QT + j) if j < QT else par_at("kva_g", l)
                    last = dve.scalar_tensor_tensor(out=proj[:, j, :], in0=proj[:, j, :], scalar=g, in1=crstd[:, j // QT, :],
                                                    op0=ALU.mult, op1=ALU.mult)
                last.then_inc(cn_ready, 1)
                with dve.Fori(0, 4) as q:
                    for t in range(4):
                        project(T0 + 10 + 4 * q + t, (2 + t) % 4, 10 + 4 * q + t)
                        split(T0 + 12 + 4 * q + t, t // 2, t % 2)
                for t in range(26, 28):
                    project(T0 + t, t % 4, t)
                    split(T0 + t + 2, 0, t % 2)
                for t in range(28, 30):
                    project(T0 + t, t % 4, t)
                dve.wait_ge(evac_done, evacuated(T0 + T_O - 1))
                dve.tensor_scalar(proj[:, QB:QB + 4, :], proj[:, QB:QB + 4, :], SCALE_B, None, ALU.mult).then_inc(qb_ready, 1)
                for j in range(2):
                    split(T0 + T_O + j, 0, j)

                def biased(u):
                    dve.wait_ge(score_done, UNITS * l + u + 1)
                    if u >= 2:
                        dve.wait_ge(exp_done, UNITS * l + u - 1)
                    s = bank[4 + u % 2][:, 0:384]
                    if u < CB0:
                        dve.scalar_tensor_tensor(out=sb[u % 2][:], in0=table("dist"), scalar=-SLOPES_B[u // 2], in1=s,
                                                 op0=ALU.mult, op1=ALU.add).then_inc(sb_ready, 1)
                    elif u < MLA0:
                        dve.scalar_tensor_tensor(out=sb[u % 2][:], in0=s, scalar=SCALE_C, in1=cbias_sb[:, u - CB0, :],
                                                 op0=ALU.mult, op1=ALU.add).then_inc(sb_ready, 1)
                    else:
                        dve.scalar_tensor_tensor(out=sb[u % 2][:], in0=s, scalar=SCALE_A, in1=table("mask"),
                                                 op0=ALU.mult, op1=ALU.add).then_inc(sb_ready, 1)
                    dve.wait_ge(sb_ready, UNITS * l + u + 1)
                    dve.tensor_reduce(nmax[u % 2][:, 0:1], sb[u % 2][:, 0:128], AX_X, ALU.max, negate=True)
                    dve.tensor_reduce(nmax[u % 2][:, 1:2], sb[u % 2][:, 128:384], AX_X, ALU.max, negate=True).then_inc(nmax_ready, 1)

                def normed(u):
                    w = prob[u % 4]
                    halves = ((0, slice(0, 128)), (1, slice(128, 384)))
                    dve.wait_ge(exp_done, UNITS * l + u + 1)
                    dve.reciprocal(rsums[u % 2][:], psums[u % 2][:]).then_inc(rsum_ready, 1)
                    dve.wait_ge(rsum_ready, UNITS * l + u + 1)
                    if u < CB0 and u % 2 == 1:
                        dve.tensor_scalar(nlr[:], rsums[1][:], nlam[:, bass.ds(l, 1)], None, ALU.mult).then_inc(map_ready, 1)
                        dve.wait_ge(map_ready, CB0 * l + u + 1)
                        for i, r in halves:
                            last = dve.scalar_tensor_tensor(out=w[:, r], in0=w[:, r], scalar=nlr[:, i:i + 1], in1=prob[(u - 1) % 4][:, r],
                                                            op0=ALU.mult, op1=ALU.add)
                    else:
                        for i, r in halves:
                            last = dve.tensor_scalar(w[:, r], w[:, r], rsums[u % 2][:, i:i + 1], None, ALU.mult)
                    last.then_inc(pn_ready if group_of(u)[1] else map_ready, 1)

                for s in range(UNITS + 5):
                    if s == CB0:
                        dve.wait_ge(cb_landed, 16 * l + 16)
                    if s < UNITS:
                        biased(s)
                    if 1 <= s < UNITS + 1:
                        normed(s - 1)
                    if s >= 5 and group_of(s - 5)[1] and group_of(s - 5)[0] >= HB:
                        g = group_of(s - 5)[0]
                        dve.wait_ge(ohi_ready, OTHERS * l + g - HB + 1)
                        dve.tensor_tensor(act_lo[:, mixed_tile(g), :], bank[g % 2][:, 0:256], act_hi[:, mixed_tile(g), :].bitcast(F32),
                                          ALU.subtract).then_inc(olo_ready, 1)
                    if 15 <= s < 15 + HB:
                        h = s - 15
                        dve.wait_ge(ostd_ready, 2 * l + h // 2 + 1)
                        dve.reciprocal(orstd[:, h, :], ostd[:, h, :]).then_inc(orstd_ready, 1)
                        dve.wait_ge(orstd_ready, HB * l + h + 1)
                        dve.wait_ge(ob_ready, HB * l + h + 1)
                        dve.scalar_tensor_tensor(out=ob[:, h, :], in0=ob[:, h, :], scalar=gsub[:, bass.ds(l, 1)], in1=orstd[:, h, :],
                                                 op0=ALU.mult, op1=ALU.mult).then_inc(on_ready, 1)
                    if 17 <= s < 17 + HB:
                        h = s - 17
                        dve.wait_ge(onhi_ready, HB * l + h + 1)
                        dve.tensor_tensor(act_lo[:, 8 + h, :], ob[:, h, :], act_hi[:, 8 + h, :].bitcast(F32), ALU.subtract)\
                            .then_inc(onlo_ready, 1)
                with dve.Fori(0, C_O // 2) as q:
                    for t in range(4):
                        T = T0 + T_O + 4 * q + t
                        add(T, t, 4 * q + t)
                        split(T + 2, (1 + t // 2) % 2, t % 2)
                dve.wait_ge(evac_done, evacuated(T0 + T_FFN - 1))
                norm(2 * l + 1, ("mlp_g", l * KT))
                ffn(T0 + T_FFN, l * H_LAYER, 2 * l + 1)
                dve.wait_ge(evac_done, evacuated(T0 + TILES_LAYER - 1))
            dve.wait_ge(ssm_const, 1)
            dve.reciprocal(den[:], den[:]).then_inc(ssm_div, 1)
            dve.wait_ge(ssm_div, 1)
            dve.tensor_tensor(cre[:], nre[:], den[:], ALU.mult)
            dve.tensor_tensor(cim[:], nim[:], den[:], ALU.mult).then_inc(ssm_div, 1)
            dve.wait_ge(sq_ready, 5)
            dve.tensor_reduce(ssum[:, 0:S], sq[:, :, 0:S].rearrange("p k n -> p n k"), AX_X, ALU.add).then_inc(ss_ready, 1)
            dve.wait_ge(std_ready, 5)
            dve.reciprocal(rstd[:, META:], std[:, 0:S]).then_inc(rstd_ready, 1)
            dve.wait_ge(rstd_ready, 5)
            for k in range(KT):
                dve.scalar_tensor_tensor(out=x[:, k, :], in0=x[:, k, :], scalar=par_at("final_g", k), in1=rstd[:, META:],
                                         op0=ALU.mult, op1=ALU.mult).then_inc(xn_ready, 1)
            dve.wait_ge(meta_hi, 1)
            dve.tensor_tensor(xg_lo[:, :, 0:META], mg, xg_hi[:, :, 0:META].bitcast(F32), ALU.subtract)
            for k in range(KT):
                dve.wait_ge(xn_ready, k + 1)
                dve.wait_ge(xhi_ready, KT * 4 + k + 1)
                dve.scalar_tensor_tensor(out=xg_lo[:, k, META:], in0=x[:, k, :], scalar=par_at("mix2_g", k),
                                         in1=xg_hi[:, k, META:].bitcast(F32), op0=ALU.mult, op1=ALU.subtract).then_inc(xlo_ready, 1)
            dve.wait_ge(sq_ready, 6)
            dve.tensor_reduce(ssum[:], sq[:].rearrange("p k n -> p n k"), AX_X, ALU.add).then_inc(ss_ready, 1)
            dve.wait_ge(std_ready, 6)
            dve.reciprocal(rstd[:], std[:]).then_inc(rstd_ready, 1)
            dve.wait_ge(rstd_ready, 6)

            def split_after(T):
                split(T + 2, (T + 2 - T_B2) // 2 % 2, T % 2)

            def out_of_psum(T, b, dst, r):
                dve.wait_ge(tile_done, multiplied(T))
                dve.tensor_tensor(dst, bank[b][:, 0:dst.shape[1]], r, ALU.mult).then_inc(evac_done, 1)

            for t in range(8):
                out_of_psum(T_B2 + t, t % 4, u[:, t, :], rstd[:])
                split_after(T_B2 + t)

            def y_tile(i):
                dve.wait_ge(y_done, 4 * i + 4)
                dve.scalar_tensor_tensor(out=u[:, i, :], in0=u[:, i, :], scalar=par_at("ssm_d", i), in1=bank[2][:, 0:L2],
                                         op0=ALU.mult, op1=ALU.add).then_inc(y_out, 1)

            def phase(j):
                dve.wait_ge(angle_ready, j + 1)
                dve.scalar_tensor_tensor(out=ph[j % 2][:], in0=km[j % 2][:], scalar=MAGIC, in1=ph[j % 2][:], op0=ALU.subtract,
                                         op1=ALU.subtract).then_inc(phase_chain, 1)
                dve.wait_ge(phase_chain, 2 * j + 1)
                dve.scalar_tensor_tensor(out=ph[j % 2][:], in0=steps, scalar=freq_lo[:, j:j + 1], in1=ph[j % 2][:], op0=ALU.mult,
                                         op1=ALU.subtract).then_inc(phase_chain, 1)
                dve.wait_ge(phase_chain, 2 * j + 2)
                dve.tensor_scalar(ph[j % 2][:], ph[j % 2][:], TURN_MAX, -TURN_MAX, ALU.min, ALU.max).then_inc(phase_ready, 1)

            def states(j):
                dve.wait_ge(bu_done, j + 1)
                dve.wait_ge(trig_ready, j + 1)
                if j >= 1:
                    dve.wait_ge(scan_ready, j)
                re, im = (bank[4 + 2 * (j % 2) + e][:, 0:L2] for e in range(2))
                c, s = cos2[j % 2][:], sin2[j % 2][:]
                for i, (a, w) in enumerate(((re, c), (im, s), (im, c), (re, s))):
                    last = dve.tensor_tensor(mprod[i][:], a, w, ALU.mult)
                last.then_inc(bu_out, 1)
                dve.wait_ge(bu_out, j + 1)
                dve.tensor_tensor(mprod[0][:], mprod[0][:], mprod[1][:], ALU.add)
                dve.tensor_tensor(mprod[2][:], mprod[2][:], mprod[3][:], ALU.subtract).then_inc(drive_ready, 1)
                dve.wait_ge(drive_ready, j + 1)
                if j >= 2:
                    dve.wait_ge(state_ready, j - 1)
                decay = mag[:, j:j + 1].to_broadcast([P, L2])
                dve.tensor_tensor_scan(zr[j % 2][:], decay, mprod[0][:], 0.0, ALU.mult, ALU.add)
                dve.tensor_tensor_scan(zi[j % 2][:], decay, mprod[2][:], 0.0, ALU.mult, ALU.add).then_inc(scan_ready, 1)

            phase(0)
            for s in range(PAIRS + 3):
                if s + 1 < PAIRS:
                    phase(s + 1)
                if s < PAIRS:
                    states(s)
                for i in tiles_after(s):
                    T = T_B2 + 8 + i
                    dst, r = (k2[:, i, :], rstd[:]) if i < 2 else (v2[:, i - 2, :], rstd[:]) if i < 4 else (q2[:, i - 4, :], rstd[:, META:])
                    out_of_psum(T, i % 2, dst, r)
                    split_after(T)
                if s >= 6 and (s - 6) % 4 == 0 and (s - 6) // 4 < T2:
                    y_tile((s - 6) // 4)
                if s - 2 in KSS:
                    a = KSS.index(s - 2)
                    dve.wait_ge(kstd_ready, a + 1)
                    dve.reciprocal(ks[:, a, :], ks[:, a, :]).then_inc(krstd_ready, 1)
                    dve.wait_ge(krstd_ready, a + 1)
                    dve.scalar_tensor_tensor(out=k2[:, a, :], in0=k2[:, a, :], scalar=qk_g[:], in1=ks[:, a, :],
                                             op0=ALU.mult, op1=ALU.mult).then_inc(kn_ready, 1)
            dve.wait_ge(qstd_ready, 1)
            dve.reciprocal(rq2[:], sq2[:]).then_inc(rq2_ready, 1)
            y = u[:, :, META:]
            dve.wait_ge(gelu_sq, 1)
            dve.wait_ge(y_out, T2)
            dve.tensor_scalar(gbuf[:], gbuf[:], 0.044715, 1.0, ALU.mult, ALU.add).then_inc(gelu_in, 1)
            dve.wait_ge(gelu_in, 1)
            dve.tensor_tensor(gbuf[:], gbuf[:], y, ALU.mult).then_inc(gelu_in, 1)
            dve.wait_ge(gelu_tanh, 1)
            dve.scalar_tensor_tensor(out=y, in0=gbuf[:], scalar=1.0, in1=y, op0=ALU.add, op1=ALU.mult).then_inc(gelu_ready, 1)
            dve.wait_ge(ghi_ready, 1)
            dve.scalar_tensor_tensor(out=act_lo[:, 8:16, :], in0=y, scalar=0.5, in1=act_hi[:, 8:16, :].bitcast(F32), op0=ALU.mult,
                                     op1=ALU.subtract).then_inc(glo_ready, 1)

            def biased2(h):
                dve.wait_ge(score2_done, h + 1)
                dve.wait_ge(bias2_ready, h + 1)
                for a, r in enumerate((slice(0, 144), slice(144, 416))):
                    last = dve.scalar_tensor_tensor(out=sb2[h % 2][:, r.start + 1:r.stop + 1], in0=bank[4 + h % 2][:, r],
                                                    scalar=rq2[:, a, h:h + 1], in1=bias2[h % 2][:, r], op0=ALU.mult, op1=ALU.add)
                last.then_inc(sb2_ready, 1)
                dve.wait_ge(sb2_ready, h + 1)
                dve.tensor_reduce(nmax2[h % 2][:, 0:1], sb2[h % 2][:, 0:145], AX_X, ALU.max, negate=True)
                dve.tensor_reduce(nmax2[h % 2][:, 1:2], sb2[h % 2][:, 145:SBW], AX_X, ALU.max, negate=True).then_inc(nmax2_ready, 1)

            def normed2(h):
                dve.wait_ge(exp2_done, h + 1)
                dve.reciprocal(rsums2[h % 2][:], psums2[h % 2][:]).then_inc(rsum2_ready, 1)
                dve.wait_ge(rsum2_ready, h + 1)
                for i, r in enumerate((slice(1, 145), slice(145, 417))):
                    last = dve.tensor_scalar(prob2[h % 4][:, r], prob2[h % 4][:, r], rsums2[h % 2][:, i:i + 1], None, ALU.mult)
                last.then_inc(pn2_ready, 1)

            dve.wait_ge(rq2_ready, 1)
            for s in range(H2 + 1):
                if s < H2:
                    biased2(s)
                if s >= 1:
                    normed2(s - 1)

            def half_norm(i, src, t0, gain):
                dve.wait_ge(nsq_ready, i + 1)
                dve.tensor_reduce(nsum[:], sq8[:].rearrange("p k n -> p n k"), AX_X, ALU.add).then_inc(nss_ready, 1)
                dve.wait_ge(nstd_ready, i + 1)
                dve.reciprocal(nrstd[:], nstd[:]).then_inc(nrstd_ready, 1)
                dve.wait_ge(nrstd_ready, i + 1)
                for t in range(T2 + 2):
                    if t < T2:
                        dve.scalar_tensor_tensor(out=src[:, t, :], in0=src[:, t, :], scalar=par_at(gain, t), in1=nrstd[:],
                                                 op0=ALU.mult, op1=ALU.mult).then_inc(nx_ready, 1)
                    if t >= 2:
                        dve.wait_ge(nhi_ready, T2 * i + t - 1)
                        dve.tensor_tensor(act_lo[:, t0 + t - 2, :], src[:, t - 2, :], act_hi[:, t0 + t - 2, :].bitcast(F32), ALU.subtract)\
                            .then_inc(nlo_ready, 1)

            half_norm(0, at2[:], 0, "attn2_g")
            for t in range(4):
                for e in range(2):
                    n = 4 * (t // 2) + 2 * e + t % 2
                    dve.wait_ge(gate_ready, 2 * t + e + 1)
                    dve.scalar_tensor_tensor(out=gbuf[:, n, :], in0=gate[e][:], scalar=1.0, in1=y[:, n, :], op0=ALU.add, op1=ALU.mult)\
                        .then_inc(gated, 1)
                dve.wait_ge(gated, 2 * t + 2)
                dve.sem_inc(evac_done, 1)
                split_after(T_GLU + t)
            half_norm(1, gbuf[:], 8, "ssm2_g")
            with dve.Fori(0, C_O2 // 2) as q:
                for t in range(4):
                    T = T_O2 + 4 * q + t
                    add(T, t, 4 * q + t)
                    split(T + 2, (1 + t // 2) % 2, t % 2)
            dve.wait_ge(evac_done, evacuated(T_FFN2 - 1))
            norm(6, ("mlp2_g", 0), 5)
            ffn(T_FFN2, H_B2, 6, last=True)

        @block.gpsimd
        def _(pool):
            pool.sem_inc(hlo_ready, 2)
            pool.memset(ones[:], 1.0)
            pool.memset(half_pi[:], np.pi / 2)
            pool.memset(magic[:], MAGIC)
            pool.memset(eps16[:], 16 * EPS)
            pool.memset(eps[:], EPS).then_inc(const_ready, 1)
            pool.wait_ge(lam_chain, 1)
            pool.partition_all_reduce(lams[:].rearrange("p l e -> p (l e)"), lamp[:].rearrange("p l e -> p (l e)"), P, RADD).then_inc(lam_sum, 1)

            def step(ins):
                ssm_steps[0] += 1
                ins.then_inc(ssm_chain, 1)
                pool.wait_ge(ssm_chain, ssm_steps[0])

            def less(o, a, c, b):
                step(pool.tensor_scalar(t1[:], a[:], c, None, ALU.mult))
                step(pool.tensor_tensor(o[:], b[:], t1[:], ALU.subtract))

            ssm_steps = [0]
            pool.wait_ge(par_landed, 16)
            lre, lim = par_at("lam_re", 0, PAIRS), par_at("lam_im", 0, PAIRS)
            pool.wait_ge(ssm_exp, 1)
            step(pool.tensor_tensor(dr[:], lre, dl[:], ALU.mult))
            step(pool.tensor_tensor(th[:], lim, dl[:], ALU.mult))
            step(pool.tensor_scalar(turns[:], th[:], 1.0 / TWO_PI, MAGIC, ALU.mult, ALU.add))
            step(pool.tensor_scalar(turns[:], turns[:], MAGIC, None, ALU.subtract))
            less(ang, turns, PI2_A, th)
            less(ang, turns, PI2_B, ang)
            less(ang, turns, PI2_C, ang)
            step(pool.tensor_scalar(angc[:], ang[:], SIN_MAX, -SIN_MAX, ALU.min, ALU.max))
            step(pool.tensor_scalar(freq[:], ang[:], 1.0 / TWO_PI, None, ALU.mult))
            step(pool.tensor_scalar(freq_hi[:], freq[:], MAGIC15, MAGIC15, ALU.add, ALU.subtract))
            less(t0, freq_hi, PI2_A, ang)
            less(t0, freq_hi, PI2_B, t0)
            less(t0, freq_hi, PI2_C, t0)
            step(pool.tensor_scalar(freq_lo[:], t0[:], 1.0 / TWO_PI, None, ALU.mult))
            pool.wait_ge(ssm_exp, 5)
            step(pool.tensor_tensor(lb1[:], mag[:], cs[:], ALU.mult))
            step(pool.tensor_scalar(lb1[:], lb1[:], 1.0, None, ALU.subtract))
            step(pool.tensor_tensor(lbi[:], mag[:], sn[:], ALU.mult))
            step(pool.tensor_tensor(t0[:], lb1[:], lre, ALU.mult))
            step(pool.tensor_tensor(t1[:], lbi[:], lim, ALU.mult))
            step(pool.tensor_tensor(nre[:], t0[:], t1[:], ALU.add))
            step(pool.tensor_tensor(t0[:], lbi[:], lre, ALU.mult))
            step(pool.tensor_tensor(t1[:], lb1[:], lim, ALU.mult))
            step(pool.tensor_tensor(nim[:], t0[:], t1[:], ALU.subtract))
            step(pool.tensor_tensor(t0[:], lre, lre, ALU.mult))
            step(pool.tensor_tensor(t1[:], lim, lim, ALU.mult))
            step(pool.tensor_tensor(den[:], t0[:], t1[:], ALU.add))
            step(pool.tensor_tensor(qk_g[:], par_at("q2_g"), par_at("k2_g"), ALU.mult))
            step(pool.tensor_scalar(qk_g[:], qk_g[:], SCALE_2, None, ALU.mult))
            pool.tensor_scalar(hb_glu[:], par_at("b_glu", 0, T2), 0.5, None, ALU.mult).then_inc(ssm_const, 1)
            def norm(n):
                pool.wait_ge(ss_ready, n + 1)
                pool.tensor_tensor(scratch[:], eps[:], eps[:], ALU.add)
                pool.partition_all_reduce(ssb[:, 0:S], ssum[:, 0:S], P, RADD).then_inc(ssb_ready, 1)

            def ffn(T0, H0):
                with pool.Fori(0, FCH) as f:
                    with pool.Fori(0, C_UP // 2) as q:
                        for t in range(4):
                            H = H0 + T_UP * f + 4 * q + t
                            pool.wait_ge(evac_done, evacuated(T0 + 2 * T_UP * f + 4 * q + t))
                            pool.tensor_tensor(rsq[t % 2][:], relu[t % 2][:], relu[t % 2][:], ALU.mult).then_inc(rr_ready, 1)
                            pool.wait_ge(rr_ready, H + 1)
                            pool.wait_ge(hhi_ready, H + 1)
                            pool.tensor_tensor(act_lo[:, bass.ds(4 * q + t, 1), :], rsq[t % 2][:].rearrange("p (a n) -> p a n", a=1),
                                               act_hi[:, bass.ds(4 * q + t, 1), :].bitcast(F32), ALU.subtract).then_inc(hlo_ready, 1)

            pool.wait_ge(tab_landed, 16)
            with pool.Fori(0, DEPTH) as l:
                T0 = l * TILES_LAYER
                norm(2 * l)
                pool.wait_ge(csq_ready, l + 1)
                pool.tensor_tensor(csum[:], csq[:, 0, :], csq[:, 1, :], ALU.add).then_inc(csum_ready, 1)
                pool.wait_ge(csum_ready, 2 * l + 1)
                pool.tensor_tensor(csq[:, 2, :], csum[:], csq[:, 2, :], ALU.add).then_inc(csum_ready, 1)
                pool.wait_ge(csum_ready, 2 * l + 2)
                pool.tensor_tensor(scratch[:], eps[:], eps[:], ALU.add)
                pool.partition_all_reduce(cssb[:].rearrange("p a n -> p (a n)"), csq[:, 2:4, :].rearrange("p a n -> p (a n)"), P, RADD)\
                    .then_inc(cssb_ready, 1)

                def rotate(t, o, a, b, ready):
                    for i, (h, w) in enumerate(((a, "cos"), (b, "sin"), (b, "cos"), (a, "sin"))):
                        last = pool.tensor_tensor(t[i], h, table(w), ALU.mult)
                    last.then_inc(ready[0], 1)
                    pool.wait_ge(ready[0], ready[1])
                    pool.tensor_tensor(o[0], t[0], t[1], ALU.subtract)
                    return pool.tensor_tensor(o[1], t[2], t[3], ALU.add)

                pool.wait_ge(evac_done, evacuated(T0 + 5))
                rotate([rkt[:, i, :] for i in range(4)], [kr[:, 0, :], kr[:, 1, :]], kr[:, 0, :], kr[:, 1, :], (krt_ready, l + 1))\
                    .then_inc(kr_ready, 1)
                pool.wait_ge(uq_out, 14 * l + 2)
                for a in range(2):
                    last = rotate([rt[:, i, a, :] for i in range(4)], [qr[:, 0, a, :], qr[:, 1, a, :]], rq[:, 0, a, :], rq[:, 1, a, :],
                                  (rt_ready, 2 * l + a + 1))
                last.then_inc(qr_ready, 1)
                norm(2 * l + 1)
                ffn(T0 + T_FFN, l * H_LAYER)
            pool.dma_start(tab2, tables2).then_inc(second_landed, 16)
            pool.dma_start(meta, metaT).then_inc(second_landed, 16)
            pool.wait_ge(second_landed, 32)
            gains = par_at("mix2_g", 0, KT).rearrange("p (k a) -> p k a", a=1).to_broadcast([P, KT, META])
            pool.tensor_tensor(mg, meta, gains, ALU.mult).then_inc(mg_ready, 1)
            pool.wait_ge(evac_done, evacuated(T_B2 - 1))
            pool.dma_start(bm[:], bmat).then_inc(mats_landed, 16)
            pool.dma_start(cm[:], cmat).then_inc(mats_landed, 16)
            norm(4)
            pool.wait_ge(ss_ready, 6)
            pool.partition_all_reduce(ssb[:], ssum[:], P, RADD).then_inc(ssb_ready, 1)
            pool.wait_ge(mats_landed, 32)
            pool.wait_ge(ssm_div, 2)
            cr, ci = (v[:].rearrange("p (j a) -> p j a", a=1).to_broadcast([P, PAIRS, 32]) for v in (cre, cim))
            for i, (a, b) in enumerate(((0, cr), (1, ci), (0, ci), (1, cr))):
                dst = cn[:, i // 2] if i % 2 == 0 else ctmp[:, i // 2]
                last = pool.tensor_tensor(dst, cm[:, a], b, ALU.mult)
            last.then_inc(cmul_ready, 1)
            pool.wait_ge(cmul_ready, 1)
            pool.tensor_tensor(cn[:, 0], cn[:, 0], ctmp[:, 0], ALU.subtract)
            pool.tensor_tensor(cn[:, 1], cn[:, 1], ctmp[:, 1], ALU.add).then_inc(cmul_ready, 1)
            pool.wait_ge(cmul_ready, 2)
            pool.tensor_scalar(cn[:, 1], cn[:, 1], -1.0, 0.0, ALU.mult, ALU.add).then_inc(cn2_ready, 1)
            for j in range(PAIRS):
                c, s = cos2[j % 2][:], sin2[j % 2][:]
                pool.wait_ge(scan_ready, j + 1)
                if j >= 2:
                    pool.wait_ge(y_done, j - 1)
                if j >= 1:
                    pool.wait_ge(state_ready, j)
                for i, (w, z) in enumerate(((c, zr), (s, zi), (s, zr), (c, zi))):
                    last = pool.tensor_tensor(pprod[i][:], w, z[j % 2][:], ALU.mult)
                last.then_inc(turn_ready, 1)
                pool.wait_ge(turn_ready, j + 1)
                pool.tensor_tensor(wr[j % 2][:], pprod[0][:], pprod[1][:], ALU.subtract)
                pool.tensor_tensor(wi[j % 2][:], pprod[2][:], pprod[3][:], ALU.add).then_inc(state_ready, 1)

            pool.wait_ge(evac_done, evacuated(T_GLU - 1))
            for h in range(H2):
                if h >= 2:
                    pool.wait_ge(sb2_ready, h - 1)
                    pool.wait_ge(exp2_done, h - 1)
                pool.tensor_scalar(bias2[h % 2][:], dist2, -SLOPES_2[h], 0.0, ALU.mult, ALU.add)
                pool.tensor_copy(sb2[h % 2][:, 0:1], par_at("sinks", h))
                pool.tensor_copy(sb2[h % 2][:, SBW - 1:SBW], par_at("sinks", h)).then_inc(bias2_ready, 1)
            for i in range(2):
                pool.wait_ge(nss_ready, i + 1)
                pool.partition_all_reduce(nsb[:], nsum[:], P, RADD).then_inc(nssb_ready, 1)
            norm(6)
            ffn(T_FFN2, H_B2)


def feature_major(a):
    n, d = a.shape
    return a.T.reshape(d // P, P, n).transpose(1, 0, 2)


def columns(v):
    return v.reshape(-1, P).T


def chunks(w):
    return w.reshape(KT, P, -1, CW).transpose(2, 1, 0, 3).reshape(-1, P, CE)


def padded(w, k):
    c = np.zeros((1, P, CE), np.float32)
    c[0, :, 0:w.size // P] = w.reshape(k, P, -1).transpose(1, 0, 2).reshape(P, -1)
    return c


def ffn_chunks(up, down):
    f = D
    return [c for i in range(FCH) for c in (chunks(up[:, f * i:f * i + f]), chunks(down[f * i:f * i + f]))]


def weight_stream(a):
    parts = []
    r0, rh = Q_RANK + KV_RANK, A_ROPE // 2
    for l in range(DEPTH):
        w = a["w_in"][l]
        rotary = [np.tile(w[:, r0 + rh * e:r0 + rh * e + rh], (1, 4)) for e in range(2)]
        parts.append(chunks(np.concatenate([w[:, :r0]] + rotary + [w[:, r0 + A_ROPE:]], 1)))
        w = a["w_uq"][l].reshape(Q_RANK, HA, A_NOPE + A_ROPE)
        halves = [w[:, :, A_NOPE + rh * e:A_NOPE + rh * e + rh].reshape(Q_RANK, -1) for e in range(2)]
        w = np.concatenate(halves + [w[:, :, :A_NOPE].reshape(Q_RANK, -1)], 1)
        parts += [padded(w[:, :768], QT), padded(w[:, 768:], QT)]
        w = a["w_ukv"][l].reshape(KV_RANK, HA, A_NOPE + A_V)
        parts.append(padded(np.concatenate([w[:, :, :A_NOPE].reshape(P, -1), w[:, :, A_NOPE:].reshape(P, -1)], 1), 1))
        parts.append(chunks(a["w_o"][l]))
        parts += ffn_chunks(a["w_up"][l], a["w_down"][l])
    w = a["w_in_2"][0]
    q, k, v, u = np.split(w, [W2, W2 + KV2 * HD2, W2 + 2 * KV2 * HD2], 1)
    parts += [chunks(u), chunks(k), chunks(v), chunks(q)]
    parts.append(a["w_glu_2"][0].reshape(T2, P, 2, 512).transpose(2, 1, 0, 3).reshape(2, P, CE))
    parts.append(chunks(a["w_out_2"][0]))
    parts += ffn_chunks(a["w_up_2"][0], a["w_down_2"][0])
    s = np.concatenate(parts, 0)
    assert s.shape[0] == C_ALL
    return s


def small_params(a):
    m = np.zeros((P, NPAR), np.float32)

    def put(name, v, i=0):
        m[:v.shape[0], COLS[name] + i:COLS[name] + i + v.shape[1]] = v

    for l in range(DEPTH):
        put("attn_g", columns(a["attn_norm"][l]), l * KT)
        put("mlp_g", columns(a["mlp_norm"][l]), l * KT)
        put("qa_g", columns(a["q_a_norm"][l]), l * QT)
        put("kva_g", columns(a["kv_a_norm"][l]), l)
        put("subln", columns(a["diff_subln"][l]), l)
        for i, n in enumerate(("lambda_q1", "lambda_k1", "lambda_q2", "lambda_k2")):
            put("lamv", a[n][l][:, None], 4 * l + i)
        m[:, COLS["laminit"] + l] = lam_init(l)
        m[:, COLS["laminit"] + DEPTH + l] = 1.0 - lam_init(l)
    put("final_g", columns(a["final_norm"]))
    put("mix2_g", columns(a["norm_mix_g_2"][0]))
    put("mlp2_g", columns(a["norm_mlp_g_2"][0]))
    put("q2_g", np.tile(a["q_norm_g_2"][0], 2)[:, None])
    put("k2_g", np.tile(a["k_norm_g_2"][0], 2)[:, None])
    put("attn2_g", columns(a["attn_out_g_2"][0]))
    put("ssm2_g", columns(a["ssm_out_g_2"][0]))
    put("ssm_d", columns(a["ssm_d_2"][0]))
    put("b_glu", columns(a["b_glu_2"][0]))
    put("lam_re", a["ssm_lambda_re_2"][0].reshape(PAIRS, P).T)
    put("lam_im", a["ssm_lambda_im_2"][0].reshape(PAIRS, P).T)
    put("log_step", np.repeat(a["ssm_log_step_2"][0].reshape(PAIRS, 2), P // 2, axis=1).T)
    put("sinks", np.tile(a["attn_sinks_2"][0][None], (P, 1)))
    return m


def shape_tables():
    t = np.zeros((P, NTAB), np.float32)
    i = np.arange(P)

    def put(name, v):
        t[:, TABLES[name][0]:TABLES[name][0] + TABLES[name][1]] = v

    half = A_ROPE // 2
    freq = np.float32(10000.0) ** (-np.arange(half, dtype=np.float32) / np.float32(half))
    angle = np.arange(S, dtype=np.float32)[None, :] * freq[i % half][:, None]
    put("ident", np.eye(P))
    put("halves", (i[:, None] // 64 == i[None, :] // 64))
    put("cos", np.cos(angle))
    put("sin", np.sin(angle))
    q = np.concatenate([np.tile(i[:, None], (1, 128)), np.tile(i[:, None] + 128, (1, 256))], 1)
    k = np.concatenate([np.arange(128), np.arange(256)])[None, :]
    hidden = k // CHUNK > q // CHUNK
    put("mask", np.where(hidden, -BIG, 0.0))
    put("dist", np.where(hidden, BIG, np.abs(q - k)))
    t2 = np.zeros((P, NTAB2), np.float32)
    q = np.concatenate([np.tile(i[:, None] + META, (1, 144)), np.tile(i[:, None] + META + 128, (1, 272))], 1)
    k = np.concatenate([np.arange(144), np.arange(272)])[None, :]
    seen = (k <= q) & ((k < META) | (q - k < WINDOW))
    t2[:, 0:416] = np.where(seen, q - k, BIG)
    t2[:, 416:] = np.arange(L2)[None, :]
    return t, t2


def band_bias(rel):
    i = np.arange(P)
    q = np.concatenate([np.tile(i[:, None], (1, 128)), np.tile(i[:, None] + 128, (1, 256))], 1)
    k = np.concatenate([np.arange(128), np.arange(256)])[None, :]
    at = np.clip(q - k, 1 - CHUNK, REL_CLIP) + CHUNK - 1
    b = np.where((k // CHUNK > q // CHUNK)[None, None], np.float32(-BIG), rel[:, :, at])
    return np.ascontiguousarray(b.transpose(0, 2, 1, 3))


def ssm_matrices(a):
    b = np.zeros((P, 2, T2, P), np.float32)
    c = np.zeros((P, 2, PAIRS, 32), np.float32)
    for e, (bn, cn) in enumerate((("ssm_b_re_2", "ssm_c_re_2"), ("ssm_b_im_2", "ssm_c_im_2"))):
        for g in range(64):
            j, h = g // 2, g % 2
            r = 32 * (j % 4) + 16 * h
            b[r:r + 16, e, j // 4, 64 * h:64 * h + 64] = a[bn][0, g].T
            c[64 * h:64 * h + 64, e, j, 16 * h:16 * h + 16] = a[cn][0, g].T
    return b, c


def arrays_of(inputs):
    a = {k: np.asarray(v) for k, v in inputs.items()}
    t, t2 = shape_tables()
    b, c = ssm_matrices(a)
    return {
        "stream": weight_stream(a), "params": small_params(a), "tables": t, "tables2": t2, "cbias": band_bias(a["rel_bias"]),
        "xT": np.ascontiguousarray(feature_major(a["x"][0])), "metaT": np.ascontiguousarray(feature_major(a["meta_tokens_2"])),
        "bmat": b, "cmat": c,
    }


def kernel(**inputs):
    from concourse import bacc
    from concourse.bass_utils import run_bass_kernel_spmd

    arrays = arrays_of(inputs)
    nc = bacc.Bacc("TRN2", target_bir_lowering=False, num_devices=1)
    args = [nc.dram_tensor(n, v.shape, F32, kind="ExternalInput").ap() for n, v in arrays.items()]
    args.append(nc.dram_tensor("out", (P, KT, S), F32, kind="ExternalOutput").ap())
    build(nc, *args)
    got = run_bass_kernel_spmd(nc, [arrays], core_ids=[0]).results[0]["out"]
    return np.ascontiguousarray(got.transpose(2, 1, 0).reshape(1, S, D))
```

```python
from contextlib import ExitStack

import numpy as np

import concourse.bass as bass
from concourse import mybir

F32 = mybir.dt.float32
F32R = mybir.dt.float32r
ALU = mybir.AluOpType
ACT = mybir.ActivationFunctionType
AX_X = mybir.AxisListType.X
RADD = bass.bass_isa.ReduceOp.add

P = 128
D = 2048
KT = D // P
S = 256
META = 16
L2 = META + S
DEPTH = 2
EPS = 1e-6
BIG = 1e30

HA, A_NOPE, A_ROPE, A_V = 8, 128, 64, 128
Q_RANK, KV_RANK = 384, 128
HB, HC = 4, 4
QT = Q_RANK // P
SCALE_A = (A_NOPE + A_ROPE) ** -0.5
SCALE_B = 64 ** -0.5
SCALE_C = 128 ** -0.5
SLOPES_B = [2.0 ** (-8.0 * (h + 1) / HB) for h in range(HB)]
CHUNK = 64
REL_CLIP = 256

H2, KV2, HD2 = 16, 4, 64
SLOPES_2 = [2.0 ** (-8.0 * (h + 1) / H2) for h in range(H2)]
SCALE_2 = HD2 ** -0.5
WINDOW = 128
W2 = 1024
T2 = W2 // P
PAIRS = 32
TWO_PI = 2.0 * np.pi
PI2_A, PI2_B, PI2_C = 6.28125, 1.9350051879882812e-3, 3.019915981956753e-7
MAGIC = 1.5 * 2.0 ** 23
MAGIC15 = 1.5 * 2.0 ** 8
SIN_MAX = 3.1415925
TURN_MAX = 0.4999999

C_IN = 15
C_MLA = 3
C_O = 8
C_UP = 8
FCH = 4
C_FFN = FCH * 2 * C_UP
C_LAYER = C_IN + C_MLA + C_O + C_FFN
R_LAYER = C_LAYER - C_MLA
C_IN2, C_GLU, C_O2 = 10, 2, 8
C_ALL = DEPTH * C_LAYER + C_IN2 + C_GLU + C_O2 + C_FFN
CW = 256
CE = KT * CW
assert C_LAYER % 2 == 0 and C_ALL % 2 == 0

COLS = {}
_at = 0
for _n, _w in [("attn_g", (DEPTH + 1) * KT), ("mlp_g", DEPTH * KT), ("final_g", KT), ("qa_g", DEPTH * QT), ("kva_g", DEPTH),
               ("subln", DEPTH), ("mix2_g", KT), ("mlp2_g", KT), ("q2_g", 1), ("k2_g", 1), ("attn2_g", T2), ("ssm2_g", T2),
               ("ssm_d", T2), ("b_glu", T2), ("lamv", DEPTH * 4), ("lam_re", PAIRS), ("lam_im", PAIRS), ("log_step", PAIRS),
               ("sinks", H2), ("laminit", 2 * DEPTH)]:
    COLS[_n] = _at
    _at += _w
NPAR = _at

TABLES = {}
_at = 0
for _n, _w in [("ident", P), ("halves", P), ("cos", S), ("sin", S), ("mask", 384), ("dist", 384)]:
    TABLES[_n] = (_at, _w)
    _at += _w
NTAB = _at
NTAB2 = 416 + L2

DIFF0, CB0, MLA0 = 0, 8, 12
UNITS = 20
GROUPS = 16


def lam_init(l):
    return 0.8 - 0.6 * float(np.exp(-0.3 * l))


def group_of(u):
    return (u // 2, u % 2 == 1) if u < CB0 else (u - 4, True)


def mixed_tile(g):
    return g + 8 if g < 8 else g - 8


def build(nc, stream, params, tables, tables2, cbias, xT, metaT, bmat, cmat, out):
    at = [(nc.sbuf_base + 63) // 64 * 64]

    def place(name, shape, dt=F32, where=at):
        t = nc.alloc_sbuf_tensor_at(name, shape, dt, offset=where[0])
        where[0] += (int(np.prod(shape[1:])) * 4 + 31) // 32 * 32
        assert len(where) == 1 or where[0] <= where[1], (name, where)
        return t

    raw = [place(f"raw{i}", [P, KT, CW]) for i in range(2)]
    hi = [place(f"w_hi{i}", [P, KT, P], F32R) for i in range(2)]
    lo = [place(f"w_lo{i}", [P, KT, P], F32R) for i in range(2)]
    x = place("x", [P, KT, S])
    xg_at = at[0]
    xg_hi = place("xg_hi", [P, KT, L2], F32R)
    xg_lo = place("xg_lo", [P, KT, L2], F32R)
    act_at = at[0]
    act_hi = place("act_hi", [P, KT, S], F32R)
    act_lo = place("act_lo", [P, KT, S], F32R)
    act_end = at[0]
    ACT_HALF = (act_end - act_at) // 2
    par = place("par", [P, NPAR])
    tab = place("tab", [P, NTAB])
    ones = place("ones", [P, P])
    eps = place("eps", [P, 1])
    half_pi = place("half_pi", [P, 1])
    rstd = place("rstd", [P, L2])
    lamp = place("lamp", [P, DEPTH, 2])
    lams = place("lams", [P, DEPTH, 2])
    lame = place("lame", [P, DEPTH, 2])
    lamd = place("lamd", [P, DEPTH])
    nlam = place("nlam", [P, DEPTH])
    gsub = place("gsub", [P, DEPTH])
    scratch = place("scratch", [P, 1])
    mg = place("mg", [P, KT, META])
    msum = place("msum", [P, META])
    magic = place("magic", [P, 1])
    eps16 = place("eps16", [P, 1])
    mag, freq, freq_hi, freq_lo, cre, cim, nre, nim, den = [
        place(f"ssm_{n}", [P, PAIRS]) for n in "mag freq freq_hi freq_lo cre cim nre nim den".split()]
    qk_g = place("qk_g", [P, 1])
    hb_glu = place("hb_glu", [P, T2])
    free_at, free_end = at[0], nc.sbuf_usable_end

    def par_at(name, i=0, n=1):
        return par[:, bass.ds(COLS[name] + i, n)]

    def table(name, a=0, b=None):
        o, w = TABLES[name]
        return tab[:, o + a:o + (w if b is None else b)]

    ident = table("ident")
    a2 = TABLES["mask"][0]
    tab2 = tab[:, a2:a2 + NTAB2]
    dist2, steps = tab2[:, 0:416], tab2[:, 416:NTAB2]

    region = [free_at, free_end]
    sq = [place(f"sq{i}", [P, S], where=region) for i in range(4)]
    sqf = [place(f"sqf{i}", [P, S], where=region) for i in range(4)]
    ssum = place("ssum", [P, S + L2], where=region)
    ssb = place("ssb", [P, S + L2], where=region)
    std = place("std", [P, L2], where=region)
    xstd = place("xstd", [P, S], where=region)
    xrstd = place("xrstd", [P, S], where=region)
    meta = place("meta", [P, KT, META], where=region)
    relu = [place(f"relu{i}", [P, S], where=region) for i in range(2)]
    rsq = [place(f"rsq{i}", [P, S], where=region) for i in range(2)]
    (dl, dr, th, turns, ang, angc, sn, cs, ab0, lb1, lbi, t0, t1) = [
        place(f"ssm_{n}", [P, PAIRS], where=region) for n in "dl dr th turns ang angc sn cs ab0 lb1 lbi t0 t1".split()]

    region = [free_at, free_end]
    proj = place("proj", [P, 30, S], where=region)
    QB, KB, VB, QC, KC, VC = range(6, 30, 4)
    sb1 = place("sb1", [P, 384], where=region)
    prob = [place(f"prob{i}", [P, 384], where=region) for i in range(4)]
    probT = [place(f"probT{i}", [P, 384], where=region) for i in range(2)]
    qr = place("qr", [P, 2, 2, S], where=region)
    cbias_sb = place("cbias_sb", [P, HC, 384], where=region)
    kr = proj[:, 4:6, :]
    region = [xg_at, act_at]
    qn = place("qn", [P, HA, S], where=region)
    kn = place("kn", [P, HA, S], where=region)
    va = place("va", [P, 2, HA * A_V], where=region)
    vb = place("vb", [P, 2, HB * P], where=region)
    vc = place("vc", [P, 2, HC * P], where=region)
    sb0 = place("sb0", [P, 384], where=region)
    nmax = [place(f"nmax{i}", [P, 2], where=region) for i in range(2)]
    psums = [place(f"psums{i}", [P, 2], where=region) for i in range(2)]
    rsums = [place(f"rsums{i}", [P, 2], where=region) for i in range(2)]
    nlr = place("nlr", [P, 2], where=region)
    sb = [sb0, sb1]
    region = [act_at, act_at + ACT_HALF // 2]
    rq = place("rq", [P, 2, 2, S], where=region)
    rkt = place("rkt", [P, 4, S], where=region)
    region = [act_at + ACT_HALF, act_at + ACT_HALF + ACT_HALF // 2]
    rt = place("rt", [P, 4, 2, S], where=region)
    region = [act_at + ACT_HALF // 2, act_at + ACT_HALF]
    csq = place("csq", [P, 4, S], where=region)
    cssb = place("cssb", [P, 2, S], where=region)
    cstd = place("cstd", [P, 2, S], where=region)
    region = [act_at + ACT_HALF + ACT_HALF // 2, act_end]
    crstd = place("crstd", [P, 2, S], where=region)
    csum = place("csum", [P, S], where=region)
    ob, osq, ostd, orstd = proj[:, VB:VB + 4, :], proj[:, VC:VC + 4, :], proj[:, 0:4, :], proj[:, KC:KC + 4, :]

    region = [free_at, free_end]
    u = place("u", [P, T2, L2], where=region)
    k2 = place("k2", [P, 2, L2], where=region)
    ks = place("ks", [P, 2, L2], where=region)
    v2 = place("v2", [P, 2, L2], where=region)
    q2 = place("q2", [P, T2, S], where=region)
    vt2 = place("vt2", [P, 2, 2 * P], where=region)
    vm2 = place("vm2", [META, 2 * P], where=region)
    rq2 = place("rq2", [P, 2, H2], where=region)
    sq2 = place("sq2", [P, 2, H2], where=region)
    ssm_at = region[0]
    km = [place(f"km{i}", [P, L2], where=region) for i in range(2)]
    ph = [place(f"ph{i}", [P, L2], where=region) for i in range(2)]
    sin2 = [place(f"sin2{i}", [P, L2], where=region) for i in range(2)]
    cos2 = [place(f"cos2{i}", [P, L2], where=region) for i in range(2)]
    mprod = [place(f"mprod{i}", [P, L2], where=region) for i in range(4)]
    zr = [place(f"zr{i}", [P, L2], where=region) for i in range(2)]
    zi = [place(f"zi{i}", [P, L2], where=region) for i in range(2)]
    wr = [place(f"wr{i}", [P, L2], where=region) for i in range(2)]
    wi = [place(f"wi{i}", [P, L2], where=region) for i in range(2)]
    region = [ssm_at, free_end]
    gbuf = place("gbuf", [P, T2, S], where=region)
    gate = [place(f"gate{i}", [P, S], where=region) for i in range(2)]
    region = [act_at, act_end]
    bm = place("bm", [P, 2, T2, P], where=region)
    cm_at = region[0]
    cm = place("cm", [P, 2, PAIRS, 32], where=region)
    cn = place("cn", [P, 2, PAIRS, 32], where=region)
    ctmp_at = region[0]
    ctmp = place("ctmp", [P, 2, PAIRS, 32], where=region)
    region = [ctmp_at, act_end]
    pprod = [place(f"pprod{i}", [P, L2], where=region) for i in range(4)]
    sin2.append(place("sin22", [P, L2], where=region))
    cos2.append(place("cos22", [P, L2], where=region))
    region = [cm_at, ctmp_at]
    wr.append(place("wr2", [P, L2], where=region))
    wi.append(place("wi2", [P, L2], where=region))
    region = [xg_at, act_at]
    SBW = 418
    sb2 = [place(f"sb2{i}", [P, SBW], where=region) for i in range(2)]
    prob2 = [place(f"prob2{i}", [P, SBW], where=region) for i in range(4)]
    bias2 = [place(f"bias2{i}", [P, 416], where=region) for i in range(2)]
    pT2 = [place(f"pT2{i}", [P, 384], where=region) for i in range(2)]
    pM2 = [place(f"pM2{i}", [META, 256], where=region) for i in range(2)]
    nmax2 = [place(f"nmax2{i}", [P, 2], where=region) for i in range(2)]
    psums2 = [place(f"psums2{i}", [P, 2], where=region) for i in range(2)]
    rsums2 = [place(f"rsums2{i}", [P, 2], where=region) for i in range(2)]
    at2 = place("at2", [P, T2, S], where=region)
    nsum = place("nsum", [P, S], where=region)
    nsb = place("nsb", [P, S], where=region)
    nstd = place("nstd", [P, S], where=region)
    nrstd = place("nrstd", [P, S], where=region)
    region = [ssm_at + 4 * (T2 + 2) * S, free_end]
    sq8 = place("sq8", [P, T2, S], where=region)

    with ExitStack() as ctx:
        bank = [ctx.enter_context(nc.psum_tensor(f"bank{i}", [P, 512], F32)) for i in range(8)]

        def sem(name):
            return ctx.enter_context(nc.semaphore(name))

        par_landed = sem("par_landed")
        tab_landed = sem("tab_landed")
        x_landed = [sem(f"x_landed{i}") for i in range(4)]
        landed = [sem(f"landed{i}") for i in range(2)]
        hi_ready = sem("hi_ready")
        lo_ready = sem("lo_ready")
        tile_done = sem("tile_done")
        evac_done = sem("evac_done")
        const_ready = sem("const_ready")
        lam_chain = sem("lam_chain")
        lam_sum = sem("lam_sum")
        lam_exp = sem("lam_exp")
        xhi_ready = sem("xhi_ready")
        xlo_ready = sem("xlo_ready")
        sq_ready = sem("sq_ready")
        zeroed = sem("zeroed")
        acc_done = sem("acc_done")
        meta_ss = sem("meta_ss")
        gain_ready = sem("gain_ready")
        mean_chain = sem("mean_chain")
        mean_ready = sem("mean_ready")
        xstd_ready = sem("xstd_ready")
        xrstd_ready = sem("xrstd_ready")
        ssb_ready = sem("ssb_ready")
        std_ready = sem("std_ready")
        rstd_ready = sem("rstd_ready")
        hhi_ready = sem("hhi_ready")
        rr_ready = sem("rr_ready")
        hlo_ready = sem("hlo_ready")
        cb_landed = sem("cb_landed")
        csq_ready = sem("csq_ready")
        csum_ready = sem("csum_ready")
        cssb_ready = sem("cssb_ready")
        cstd_ready = sem("cstd_ready")
        crstd_ready = sem("crstd_ready")
        cn_ready = sem("cn_ready")
        krt_ready = sem("krt_ready")
        kr_ready = sem("kr_ready")
        uq_done = sem("uq_done")
        uq_out = sem("uq_out")
        rt_ready = sem("rt_ready")
        qr_ready = sem("qr_ready")
        vt_done = sem("vt_done")
        vt_out = sem("vt_out")
        qb_ready = sem("qb_ready")
        score_done = sem("score_done")
        sb_ready = sem("sb_ready")
        nmax_ready = sem("nmax_ready")
        exp_done = sem("exp_done")
        rsum_ready = sem("rsum_ready")
        map_ready = sem("map_ready")
        pn_ready = sem("pn_ready")
        tr_done = sem("tr_done")
        pt_ready = sem("pt_ready")
        pv_done = sem("pv_done")
        ob_ready = sem("ob_ready")
        osq_ready = sem("osq_ready")
        oss_done = sem("oss_done")
        ostd_ready = sem("ostd_ready")
        orstd_ready = sem("orstd_ready")
        on_ready = sem("on_ready")
        onhi_ready = sem("onhi_ready")
        onlo_ready = sem("onlo_ready")
        ohi_ready = sem("ohi_ready")
        olo_ready = sem("olo_ready")
        second_landed = sem("second_landed")
        ssm_chain = sem("ssm_chain")
        ssm_exp = sem("ssm_exp")
        ssm_const = sem("ssm_const")
        ssm_div = sem("ssm_div")
        meta_landed = sem("meta_landed")
        mg_ready = sem("mg_ready")
        xn_ready = sem("xn_ready")
        meta_hi = sem("meta_hi")
        mats_landed = sem("mats_landed")
        cmul_ready = sem("cmul_ready")
        cn2_ready = sem("cn2_ready")
        bu_done = sem("bu_done")
        angle_ready = sem("angle_ready")
        phase_chain = sem("phase_chain")
        phase_ready = sem("phase_ready")
        abs_ready = sem("abs_ready")
        trig_ready = sem("trig_ready")
        bu_out = sem("bu_out")
        drive_ready = sem("drive_ready")
        scan_ready = sem("scan_ready")
        turn_ready = sem("turn_ready")
        state_ready = sem("state_ready")
        y_done = sem("y_done")
        y_out = sem("y_out")
        ksq_ready = sem("ksq_ready")
        kss_done = sem("kss_done")
        kstd_ready = sem("kstd_ready")
        krstd_ready = sem("krstd_ready")
        kn_ready = sem("kn_ready")
        ks_done = sem("ks_done")
        ks_ready = sem("ks_ready")
        v2t_done = sem("v2t_done")
        v2t_out = sem("v2t_out")
        qsq_ready = sem("qsq_ready")
        qss_done = sem("qss_done")
        qstd_ready = sem("qstd_ready")
        rq2_ready = sem("rq2_ready")
        bias2_ready = sem("bias2_ready")
        score2_done = sem("score2_done")
        sb2_ready = sem("sb2_ready")
        nmax2_ready = sem("nmax2_ready")
        exp2_done = sem("exp2_done")
        rsum2_ready = sem("rsum2_ready")
        pn2_ready = sem("pn2_ready")
        tr2_done = sem("tr2_done")
        pt2_ready = sem("pt2_ready")
        pv2_done = sem("pv2_done")
        at2_ready = sem("at2_ready")
        gelu_sq = sem("gelu_sq")
        gelu_in = sem("gelu_in")
        gelu_tanh = sem("gelu_tanh")
        gelu_ready = sem("gelu_ready")
        ghi_ready = sem("ghi_ready")
        glo_ready = sem("glo_ready")
        gate_ready = sem("gate_ready")
        gated = sem("gated")
        nsq_ready = sem("nsq_ready")
        nss_ready = sem("nss_ready")
        nssb_ready = sem("nssb_ready")
        nstd_ready = sem("nstd_ready")
        nrstd_ready = sem("nrstd_ready")
        nx_ready = sem("nx_ready")
        nhi_ready = sem("nhi_ready")
        nlo_ready = sem("nlo_ready")
        stored = sem("stored")

        block = ctx.enter_context(nc.Block())

        TILES_LAYER = 2 * R_LAYER
        T_O = 2 * C_IN
        T_FFN = T_O + 2 * C_O
        T_UP = 2 * C_UP
        H_LAYER = FCH * T_UP
        T_FFN_LAST = 2 * T_UP * FCH - T_UP
        C2_LAYER = C_LAYER // 2
        OTHERS = GROUPS - HB

        T_B2 = DEPTH * TILES_LAYER
        T_GLU, T_O2 = T_B2 + 20, T_B2 + 24
        T_FFN2 = T_O2 + 16
        C2_B2 = DEPTH * C2_LAYER
        H_B2 = DEPTH * H_LAYER

        SLICES = 12 * KT // PAIRS

        def slices_of(s):
            return [divmod(g, KT) for g in range(SLICES * s, SLICES * s + SLICES)] if s < PAIRS else []

        def tiles_after(s):
            return [i for i, k in slices_of(s - 1) if k == KT - 1] if s else []

        GLU0 = 6

        def gate_at(s):
            t, odd = divmod(s - GLU0 - 2, 2)
            return [t] if 0 <= t < 4 and not odd else []

        KSS, VT2, KSW = (13, 16), (19, 22), (25, 28)

        def evacuated(T):
            return T + 5

        def multiplied(T):
            return T + 3

        def lo_count(T, half):
            return 2 * T + half + 9

        def chunk_landed(c2):
            return 16 * c2 + 16

        @block.sync
        def _(sp):
            sp.dma_start(par[:], params).then_inc(par_landed, 16)

            def load(c, i):
                sp.dma_start(raw[i][:], stream[c].rearrange("p (k n) -> p k n", k=KT)).then_inc(landed[i], 16)

            def load_behind(R, c, i):
                sp.wait_ge(lo_ready, 4 * R + 12)
                load(c, i)

            with sp.Fori(0, DEPTH) as l:
                for i in range(2):
                    if i:
                        sp.wait_ge(x_landed[3], 16)
                    load_behind(l * R_LAYER + i - 2, l * C_LAYER + i, i)
                sp.dma_start(cbias_sb[:], cbias[l]).then_inc(cb_landed, 16)
                with sp.Fori(0, (C_IN - 1) // 2) as q:
                    for i in range(2):
                        load_behind(l * R_LAYER + 2 * q + i, l * C_LAYER + 2 * q + i + 2, i)
                load_behind(l * R_LAYER + C_IN - 1, l * C_LAYER + C_IN + 1, 0)
                for i, c, used in ((1, 17, 3), (0, 18, 6), (1, 19, 14)):
                    sp.wait_ge(uq_done, 14 * l + used)
                    load(l * C_LAYER + c, i)
                with sp.Fori(0, (C_LAYER - 20) // 2) as q:
                    for i in range(2):
                        load_behind(l * R_LAYER + C_IN + 2 * q + i, l * C_LAYER + 20 + 2 * q + i, i)
            B2, R2 = DEPTH * C_LAYER, DEPTH * R_LAYER
            with sp.Fori(0, (C_ALL - B2) // 2) as q:
                for i in range(2):
                    load_behind(R2 + 2 * q + i - 2, B2 + 2 * q + i, i)
            T_LAST = T_FFN2 + 2 * T_UP * FCH - T_UP
            for q in range(4):
                sp.wait_ge(evac_done, evacuated(T_LAST + 4 * q + 3))
                sp.dma_start(out[:, 4 * q:4 * q + 4, :], x[:, 4 * q:4 * q + 4, :]).then_inc(stored, 16)
            sp.wait_ge(stored, 64)

        @block.tensor
        def _(pe):
            pe.sem_inc(tile_done, 2)

            def mm(o, a, b, start, stop):
                return pe.matmul(o, a, b, start=start, stop=stop, skip_group_check=True)

            def row_tile(b, j, rhs_hi, rhs_lo, k, first=0):
                n = rhs_hi.shape[2]
                mm(bank[b][:, 0:n], hi[j][:, k, :], rhs_hi[:, k, :], k == first, False)
                mm(bank[b][:, 0:n], hi[j][:, k, :], rhs_lo[:, k, :], False, False)
                return mm(bank[b][:, 0:n], lo[j][:, k, :], rhs_hi[:, k, :], False, k == (first - 1) % KT)

            def tile(T, b, j, rhs_hi, rhs_lo, before=None):
                pe.wait_ge(evac_done, T + 1)
                for h in range(2):
                    pe.wait_ge(lo_ready, lo_count(T, h))
                    for k in range(8 * h, 8 * h + 8):
                        if before is not None:
                            before(k)
                        last = row_tile(b, j, rhs_hi, rhs_lo, k)
                last.then_inc(tile_done, 1)

            xh, xl = xg_hi[:, :, META:], xg_lo[:, :, META:]

            def residual_ready(n):
                def wait(k):
                    if k % 4 == 0 or k > 12:
                        pe.wait_ge(xlo_ready, KT * n + (k + 4 if k < 12 else k + 1))
                return wait

            def ffn(T0, H0, n):
                with pe.Fori(0, FCH) as f:
                    with pe.Fori(0, C_UP // 2) as q:
                        for t in range(4):
                            tile(T0 + 2 * T_UP * f + 4 * q + t, t, t % 2, xh, xl, residual_ready(n) if t == 0 else None)

                    def hidden_ready(k):
                        if k % 4 == 0:
                            pe.wait_ge(hlo_ready, H0 + T_UP * f + k + 6)
                    with pe.Fori(0, C_UP // 2) as q:
                        for t in range(4):
                            tile(T0 + 2 * T_UP * f + T_UP + 4 * q + t, t, t % 2, act_hi, act_lo, hidden_ready if t == 0 else None)

            with pe.Fori(0, DEPTH) as l:
                T0 = l * TILES_LAYER
                for t in range(6):
                    tile(T0 + t, t % 4, t % 2, xh, xl, residual_ready(2 * l) if t == 0 else None)
                with pe.Fori(0, 6) as q:
                    for t in range(4):
                        tile(T0 + 6 + 4 * q + t, (2 + t) % 4, t % 2, xh, xl)

                pe.wait_ge(const_ready, 1)
                pe.wait_ge(tab_landed, 16)
                pe.wait_ge(cn_ready, l + 1)
                flat = [raw[i][:].rearrange("p k n -> p (k n)") for i in range(2)]
                tiles = []
                for r in (1, 0):
                    w = flat[r][:, 0:QT * 768].rearrange("p (k n) -> p k n", k=QT)
                    tiles += [(15 if r else 16, [w[:, k, 128 * t:128 * t + 128] for k in range(QT)], 0) for t in range(6)]
                tiles += [(17, [flat[1][:, 128 * t:128 * t + 128]], QT) for t in range(HA)]
                for n, (c, ws, j0) in enumerate(tiles):
                    if n in (0, 6, 12):
                        pe.wait_ge(landed[c % 2], chunk_landed(l * C2_LAYER + c // 2))
                    if n % 2 == 0 and n >= 8:
                        pe.wait_ge(uq_out, 14 * l + n // 2 - 3)
                    for k, w in enumerate(ws):
                        last = mm(bank[4 + n // 2 % 4][:, 256 * (n % 2):256 * (n % 2) + 256], w, proj[:, j0 + k, :],
                                  k == 0, k == len(ws) - 1)
                    if n % 2 == 1:
                        last.then_inc(uq_done, 1)
                for g in range(4):
                    pe.wait_ge(uq_out, 14 * l + 10 + g - 3)
                    c0 = 1024 + 512 * (g % 2)
                    mm(bank[4 + (10 + g) % 4][:], proj[:, QT, 128 * (g // 2):128 * (g // 2) + 128], flat[1][:, c0:c0 + 512], True, True)\
                        .then_inc(uq_done, 1)
                pe.wait_ge(evac_done, evacuated(T0 + T_O - 1))
                pe.wait_ge(uq_out, 14 * l + 14)
                for g, v0 in enumerate((VB, VB, VC, VC)):
                    for h in range(4):
                        last = pe.transpose(bank[4 + g][:, 128 * h:128 * h + 128],
                                            proj[:, v0 + h, 128 * (g % 2):128 * (g % 2) + 128], ident)
                    last.then_inc(vt_done, 1)

                def scores(u):
                    s = bank[4 + u % 2]
                    if u >= 2:
                        pe.wait_ge(sb_ready, UNITS * l + u - 1)
                    else:
                        pe.wait_ge(vt_out, 4 * l + 4)
                        pe.wait_ge(qb_ready, l + 1)
                    if u < CB0:
                        r = slice(64 * (u % 2), 64 * (u % 2) + 64)
                        parts = [(proj[r, QB + u // 2, :], proj[r, KB + u // 2, :])]
                    elif u < MLA0:
                        parts = [(proj[:, QC + u - CB0, :], proj[:, KC + u - CB0, :])]
                    else:
                        h = u - MLA0
                        if h == 0:
                            pe.wait_ge(qr_ready, l + 1)
                            pe.wait_ge(kr_ready, l + 1)
                        r = slice(32 * (h % 4), 32 * (h % 4) + 32)
                        parts = [(qn[:, h, :], kn[:, h, :])] + [(qr[r, e, h // 4, :], kr[r, e, :]) for e in range(2)]
                    for i, (q, k) in enumerate(parts):
                        mm(s[:, 0:128], q[:, 0:128], k[:, 0:128], i == 0, i == len(parts) - 1)
                    for i, (q, k) in enumerate(parts):
                        last = mm(s[:, 128:384], q[:, 128:256], k, i == 0, i == len(parts) - 1)
                    last.then_inc(score_done, 1)

                def turn(g, u):
                    pe.wait_ge(pn_ready, GROUPS * l + g + 1)
                    if g >= 2:
                        pe.wait_ge(pt_ready, GROUPS * l + g - 1)
                    for i in range(3):
                        last = pe.transpose(bank[6 + g % 2][:, 128 * i:128 * i + 128], prob[u % 4][:, 128 * i:128 * i + 128], ident)
                    last.then_inc(tr_done, 1)

                def values(g):
                    pe.wait_ge(pt_ready, GROUPS * l + g + 1)
                    if 2 <= g < 2 + HB:
                        pe.wait_ge(osq_ready, HB * l + g - 1)
                    elif g >= 2:
                        pe.wait_ge(olo_ready, OTHERS * l + g - 1 - HB)
                    v, h = (vb, g) if g < 4 else (vc, g - 4) if g < 8 else (va, g - 8)
                    o = bank[g % 2]
                    mm(o[:, 0:256], v[:, 0, 128 * h:128 * h + 128], probT[g % 2][:, 0:256], True, False)
                    mm(o[:, 128:256], v[:, 1, 128 * h:128 * h + 128], probT[g % 2][:, 256:384], False, True).then_inc(pv_done, 1)

                for s in range(UNITS + 3):
                    if s < UNITS:
                        scores(s)
                    if 2 <= s < UNITS + 2 and group_of(s - 2)[1]:
                        turn(group_of(s - 2)[0], s - 2)
                    if 3 <= s and group_of(s - 3)[1]:
                        values(group_of(s - 3)[0])
                    if s == 13:
                        pe.wait_ge(osq_ready, HB * l + HB)
                        for h in range(HB):
                            last = mm(bank[2 + h // 2][:, 256 * (h % 2):256 * (h % 2) + 256], ones[:], osq[:, h, :], True, True)
                        last.then_inc(oss_done, 1)
                def mixed_ready(k):
                    if k == 0:
                        pe.wait_ge(olo_ready, OTHERS * l + OTHERS)
                        pe.wait_ge(onlo_ready, HB * l + HB)

                with pe.Fori(0, C_O // 2) as q:
                    for t in range(4):
                        tile(T0 + T_O + 4 * q + t, t, t % 2, act_hi, act_lo, mixed_ready if t == 0 else None)
                ffn(T0 + T_FFN, l * H_LAYER, 2 * l + 1)
            pe.wait_ge(evac_done, evacuated(T_B2 - 1))
            with pe.Fori(0, 2) as q:
                for t in range(4):
                    tile(T_B2 + 4 * q + t, t, t % 2, xg_hi, xg_lo, residual_ready(4) if t == 0 else None)
            pe.wait_ge(mats_landed, 32)

            def drive(j):
                pe.wait_ge(evac_done, evacuated(T_B2 + j // 4))
                if j >= 2:
                    pe.wait_ge(bu_out, j - 1)
                r = slice(32 * (j % 4), 32 * (j % 4) + 32)
                for e in range(2):
                    last = mm(bank[4 + 2 * (j % 2) + e][:, 0:L2], bm[r, e, j // 4, :], u[r, j // 4, :], True, True)
                last.then_inc(bu_done, 1)

            def read_out(j):
                if j % 4 == 0:
                    pe.wait_ge(y_out, j // 4) if j else pe.wait_ge(evac_done, evacuated(T_B2 + 7))
                if j == 0:
                    pe.wait_ge(cn2_ready, 1)
                pe.wait_ge(state_ready, j + 1)
                o = bank[2][32 * (j % 4):32 * (j % 4) + 32, 0:L2]
                mm(o, cn[:, 0, j, :], wr[j % 3][:], True, False)
                mm(o, cn[:, 1, j, :], wi[j % 3][:], False, True).then_inc(y_done, 1)

            for s in range(PAIRS + 3):
                if s < PAIRS:
                    drive(s)
                for i, k in slices_of(s):
                    T = T_B2 + 8 + i
                    if k == 0:
                        pe.wait_ge(evac_done, T + 3)
                    if k % 8 == 0:
                        pe.wait_ge(lo_ready, lo_count(T, k // 8))
                    last = row_tile(i % 2, i % 2, *((xg_hi, xg_lo) if i < 4 else (xh, xl)), k)
                    if k == KT - 1:
                        last.then_inc(tile_done, 1)
                if s >= 3:
                    read_out(s - 3)
                if s in KSS:
                    a = KSS.index(s)
                    pe.wait_ge(ksq_ready, a + 1)
                    if a:
                        pe.wait_ge(kstd_ready, a)
                    mm(bank[3][:, 0:L2], table("halves"), ks[:, a, :], True, True).then_inc(kss_done, 1)
                if s in VT2:
                    a = VT2.index(s)
                    pe.wait_ge(kstd_ready, 2)
                    pe.wait_ge(evac_done, evacuated(T_B2 + 10 + a))
                    if a:
                        pe.wait_ge(v2t_out, a)
                    for i in range(2):
                        pe.transpose(bank[3][:, 128 * i:128 * i + 128], v2[:, a, META + 128 * i:META + 128 * i + 128], ident)
                    pe.transpose(bank[3][0:META, 256:384], v2[:, a, 0:META], ident).then_inc(v2t_done, 1)
                if s in KSW:
                    a = KSW.index(s)
                    pe.wait_ge(v2t_out, 2)
                    pe.wait_ge(kn_ready, a + 1)
                    if a:
                        pe.wait_ge(ks_ready, a)
                    mm(bank[3][0:64, 0:L2], ident[:, 64:128], k2[:, a, :], True, True)
                    mm(bank[3][64:128, 0:L2], ident[:, 0:64], k2[:, a, :], True, True).then_inc(ks_done, 1)
            pe.wait_ge(ks_ready, 2)
            pe.wait_ge(qsq_ready, 1)
            for a in range(2):
                for t in range(T2):
                    last = mm(bank[3][:, 16 * a + 2 * t:16 * a + 2 * t + 2], sq8[:, t, 128 * a:128 * a + 128],
                              table("halves")[:, 0:128:64], True, True)
            last.then_inc(qss_done, 1)

            def scores2(h):
                pe.wait_ge(sb2_ready, h - 1) if h >= 2 else pe.wait_ge(bu_out, PAIRS)
                g = h // 4
                k = (k2 if g % 2 == h % 2 else ks)[64 * (h % 2):64 * (h % 2) + 64, g // 2, :]
                q = q2[64 * (h % 2):64 * (h % 2) + 64, h // 2, :]
                mm(bank[4 + h % 2][:, 0:144], q[:, 0:128], k[:, 0:144], True, True)
                mm(bank[4 + h % 2][:, 144:416], q[:, 128:256], k, True, True).then_inc(score2_done, 1)

            def turn2(h):
                pe.wait_ge(pn2_ready, h + 1)
                if h >= 2:
                    pe.wait_ge(pt2_ready, h - 1)
                elif h == 0:
                    pe.wait_ge(bu_out, PAIRS)
                w = prob2[h % 4]
                for i, c in enumerate((17, 161, 289)):
                    pe.transpose(bank[6 + h % 2][:, 128 * i:128 * i + 128], w[:, c:c + 128], ident)
                for i, c in enumerate((1, 145)):
                    last = mm(bank[6 + h % 2][32 * i:32 * i + META, 384:512], w[:, c:c + META], ident, True, True)
                last.then_inc(tr2_done, 1)

            def values2(h):
                pe.wait_ge(pt2_ready, h + 1)
                if h % 2 == 0:
                    pe.wait_ge(at2_ready, h // 2 - 1) if h >= 4 else pe.wait_ge(evac_done, evacuated(T_GLU - 1))
                o = bank[h // 2 % 2][64 * (h % 2):64 * (h % 2) + 64, :]
                c = 64 * (h // 4)
                mm(o[:, 0:256], vt2[:, 0, c:c + 64], pT2[h % 2][:, 0:256], True, False)
                mm(o[:, 128:256], vt2[:, 1, c:c + 64], pT2[h % 2][:, 256:384], False, False)
                mm(o[:, 0:256], vm2[:, c:c + 64], pM2[h % 2][:], False, True).then_inc(pv2_done, 1)

            def gate_half(t, e):
                T = T_GLU + t
                if e == 0:
                    if t == 0:
                        pe.wait_ge(y_out, T2)
                        pe.wait_ge(qstd_ready, 1)
                        pe.wait_ge(glo_ready, 1)
                    if t >= 2:
                        pe.wait_ge(evac_done, evacuated(T - 2))
                    pe.wait_ge(lo_ready, lo_count(T, 1))
                o = bank[2 + t % 2][:, 256 * e:256 * e + 256]
                for k in range(T2):
                    mm(o, hi[t % 2][:, 2 * k + e, :], act_hi[:, 8 + k, :], k == 0, False)
                    mm(o, hi[t % 2][:, 2 * k + e, :], act_lo[:, 8 + k, :], False, False)
                    last = mm(o, lo[t % 2][:, 2 * k + e, :], act_hi[:, 8 + k, :], False, k == T2 - 1)
                if e == 1:
                    last.then_inc(tile_done, 1)

            pe.wait_ge(kn_ready, 2)
            for s in range(H2 + 3):
                if s < H2:
                    scores2(s)
                if 2 <= s < H2 + 2:
                    turn2(s - 2)
                if s >= 3:
                    values2(s - 3)
                if 0 <= s - GLU0 < 8:
                    gate_half((s - GLU0) // 2, (s - GLU0) % 2)
            with pe.Fori(0, C_O2 // 2) as q:
                for t in range(4):
                    T = T_O2 + 4 * q + t
                    pe.wait_ge(evac_done, T + 1)
                    pe.wait_ge(lo_ready, lo_count(T, 1))
                    for i in range(KT):
                        if t == 0 and i % T2 == 0:
                            pe.wait_ge(nlo_ready, T2 + i)
                        last = row_tile(t, t % 2, act_hi, act_lo, (T2 + i) % KT, T2)
                    last.then_inc(tile_done, 1)
            ffn(T_FFN2, H_B2, 5)

        @block.scalar
        def _(act):
            for i in range(4):
                act.dma_start(x[:, 4 * i:4 * i + 4, :], xT[:, 4 * i:4 * i + 4, :]).then_inc(x_landed[i], 16)
            act.dma_start(tab[:], tables).then_inc(tab_landed, 16)

            def split(T, c2, r, j):
                if j == 0:
                    act.wait_ge(landed[r], chunk_landed(c2))
                act.wait_ge(tile_done, T + 1)
                for h in range(2):
                    act.activation(hi[j][:, 8 * h:8 * h + 8, :], raw[r][:, 8 * h:8 * h + 8, P * j:P * j + P], ACT.Copy)\
                        .then_inc(hi_ready, 1)

            def gained(j, gain):
                act.activation(xg_hi[:, bass.ds(j, 1), META:], x[:, bass.ds(j, 1), :], ACT.Copy, scale=par_at(*gain)).then_inc(xhi_ready, 1)

            def squared(j, t, final=False):
                one = x[:, bass.ds(j, 1), :]
                last = act.activation(sq[t][:].rearrange("p (a n) -> p a n", a=1), one, ACT.Square)
                if final:
                    last = act.activation(sqf[t][:].rearrange("p (a n) -> p a n", a=1), one, ACT.Square, scale=par_at("final_g", j))
                last.then_inc(sq_ready, 1)

            def root(n):
                act.wait_ge(ssb_ready, n + 1)
                act.activation(std[:, 0:S], ssb[:, 0:S], ACT.Sqrt, bias=eps[:], scale=1.0 / D).then_inc(std_ready, 1)

            def ffn(T0, c2, H0, acc0=None, after=None):
                def up(q, f, t):
                    T = T0 + 2 * T_UP * f + 4 * q + t
                    split(T + 2, c2 + C_UP * f + q + (t // 2 + 1) // 2, (1 + t // 2) % 2, t % 2)
                    act.wait_ge(evac_done, evacuated(T))
                    act.activation(act_hi[:, bass.ds(4 * q + t, 1), :], relu[t % 2][:].rearrange("p (a n) -> p a n", a=1), ACT.Square)\
                        .then_inc(hhi_ready, 1)

                def down(q, f, t):
                    split(T0 + 2 * T_UP * f + T_UP + 4 * q + t + 2, c2 + C_UP * f + C_UP // 2 + q + (t // 2 + 1) // 2,
                          (1 + t // 2) % 2, t % 2)

                def ups(f):
                    with act.Fori(0, C_UP // 2) as q:
                        for t in range(4):
                            up(q, f, t)

                with act.Fori(0, FCH - 1) as f:
                    ups(f)
                    with act.Fori(0, C_UP // 2) as q:
                        for t in range(4):
                            down(q, f, t)
                ups(FCH - 1)
                if after is not None:
                    with act.Fori(0, C_UP // 2) as q:
                        for t in range(4):
                            down(q, FCH - 1, t)
                            act.wait_ge(acc_done, acc0 + 4 * q + t + 1)
                            act.wait_ge(evac_done, evacuated(T0 + T_FFN_LAST + 4 * q + t))
                            after(4 * q + t, t)
                else:
                    with act.Fori(0, C_UP // 2 - 1) as q:
                        for t in range(4):
                            down(q, FCH - 1, t)
                    for t in range(2):
                        down(C_UP // 2 - 1, FCH - 1, t)

            act.wait_ge(par_landed, 16)
            act.wait_ge(const_ready, 1)
            act.activation(dl[:], par_at("log_step", 0, PAIRS), ACT.Exp).then_inc(ssm_exp, 1)
            act.wait_ge(lam_sum, 1)
            act.activation(lame[:], lams[:], ACT.Exp).then_inc(lam_exp, 1)
            act.wait_ge(ssm_chain, 1)
            act.activation(mag[:], dr[:], ACT.Exp).then_inc(ssm_exp, 1)
            act.wait_ge(ssm_chain, 11)
            act.activation(ab0[:], angc[:], ACT.Abs).then_inc(ssm_exp, 1)
            act.activation(sn[:], angc[:], ACT.Sin).then_inc(ssm_exp, 1)
            act.wait_ge(ssm_exp, 4)
            act.activation(cs[:], ab0[:], ACT.Sin, scale=-1.0, bias=half_pi[:]).then_inc(ssm_exp, 1)
            split(0, 0, 0, 0)
            for j in range(KT):
                if j % 4 == 0:
                    act.wait_ge(x_landed[j // 4], 16)
                gained(j, ("attn_g", j))
                act.wait_ge(acc_done, j + 1)
                squared(j, j % 4)
                if j == 11:
                    split(1, 0, 0, 1)
            with act.Fori(0, DEPTH) as l:
                T0, c0 = l * TILES_LAYER, l * C2_LAYER
                root(2 * l)
                for c in range(3):
                    for j in range(2):
                        split(T0 + 2 * c + j + 2, c0 + (c + 1) // 2, (c + 1) % 2, j)
                act.wait_ge(evac_done, evacuated(T0 + QT))
                act.activation(csq[:], proj[:, 0:4, :], ACT.Square).then_inc(csq_ready, 1)
                for j in range(2):
                    split(T0 + 8 + j, c0 + 2, 0, j)
                act.wait_ge(cssb_ready, l + 1)
                for i, n in enumerate((Q_RANK, KV_RANK)):
                    act.activation(cstd[:, i, :], cssb[:, i, :], ACT.Sqrt, bias=eps[:], scale=1.0 / n).then_inc(cstd_ready, 1)
                for j in range(2):
                    split(T0 + 10 + j, c0 + 2, 1, j)
                with act.Fori(0, 4) as q:
                    for c in range(2):
                        for j in range(2):
                            split(T0 + 12 + 4 * q + 2 * c + j, c0 + 3 + q, c, j)
                for j in range(2):
                    split(T0 + 28 + j, c0 + 7, 0, j)
                dst = [rq[:, 0], rq[:, 1]] + [qn[:, 2 * i:2 * i + 2, :] for i in range(4)] + [kn[:, 2 * i:2 * i + 2, :] for i in range(4)]
                dst = [d.rearrange("p a n -> p (a n)") for d in dst] + [va[:, g // 2, 512 * (g % 2):512 * (g % 2) + 512] for g in range(4)]
                for i, d in enumerate(dst):
                    act.wait_ge(uq_done, 14 * l + i + 1)
                    act.activation(d, bank[4 + i % 4][:], ACT.Copy).then_inc(uq_out, 1)
                for g in range(4):
                    act.wait_ge(vt_done, 4 * l + g + 1)
                    act.activation((vb, vc)[g // 2][:, g % 2, :], bank[4 + g][:], ACT.Copy).then_inc(vt_out, 1)
                for j in range(2):
                    split(T0 + T_O + j, c0 + 9, 0, j)

                def exps(u):
                    act.wait_ge(nmax_ready, UNITS * l + u + 1)
                    if u >= 4:
                        act.wait_ge(tr_done, GROUPS * l + group_of(u - 4)[0] + 1)
                    for i, r in enumerate((slice(0, 128), slice(128, 384))):
                        last = act.activation(prob[u % 4][:, r], sb[u % 2][:, r], ACT.Exp, bias=nmax[u % 2][:, i:i + 1],
                                              accum_out=psums[u % 2][:, i:i + 1])
                    last.then_inc(exp_done, 1)

                def weights_out(g):
                    act.wait_ge(tr_done, GROUPS * l + g + 1)
                    if g >= 2:
                        act.wait_ge(pv_done, GROUPS * l + g - 1)
                    act.activation(probT[g % 2][:], bank[6 + g % 2][:, 0:384], ACT.Copy).then_inc(pt_ready, 1)

                def output(g):
                    act.wait_ge(pv_done, GROUPS * l + g + 1)
                    if g < HB:
                        act.activation(ob[:, g, :], bank[g % 2][:, 0:256], ACT.Copy).then_inc(ob_ready, 1)
                        act.activation(osq[:, g, :], bank[g % 2][:, 0:256], ACT.Square).then_inc(osq_ready, 1)
                    else:
                        act.activation(act_hi[:, mixed_tile(g), :], bank[g % 2][:, 0:256], ACT.Copy).then_inc(ohi_ready, 1)

                for s in range(UNITS + 4):
                    if s < UNITS:
                        exps(s)
                    if 2 <= s < UNITS + 2 and group_of(s - 2)[1]:
                        weights_out(group_of(s - 2)[0])
                    if s >= 4 and group_of(s - 4)[1]:
                        output(group_of(s - 4)[0])
                    if s == 14:
                        act.wait_ge(oss_done, l + 1)
                        for i in range(2):
                            act.activation(ostd[:, 2 * i:2 * i + 2, :], bank[2 + i][:].rearrange("p (a n) -> p a n", a=2), ACT.Sqrt,
                                           bias=eps[:], scale=1.0 / P).then_inc(ostd_ready, 1)
                    if 16 <= s < 16 + HB:
                        act.wait_ge(on_ready, HB * l + s - 15)
                        act.activation(act_hi[:, 8 + s - 16, :], ob[:, s - 16, :], ACT.Copy).then_inc(onhi_ready, 1)
                with act.Fori(0, C_O // 2) as q:
                    for t in range(4):
                        j = 4 * q + t
                        split(T0 + T_O + j + 2, c0 + 9 + q + (t // 2 + 1) // 2, (1 + t // 2) % 2, t % 2)
                        act.wait_ge(acc_done, KT * (2 * l + 1) + j + 1)
                        act.wait_ge(evac_done, evacuated(T0 + T_O + j))
                        gained(j, ("mlp_g", l * KT + j))
                        squared(j, t)
                root(2 * l + 1)
                act.activation(xg_hi[:, :, 0:META], mg[:], ACT.Copy).then_inc(meta_hi, 1)

                def after(j, t):
                    gained(j, ("attn_g", (l + 1) * KT + j))
                    squared(j, t, final=True)
                ffn(T0 + T_FFN, c0 + 13, l * H_LAYER, KT * (2 * l + 2), after)
            act.wait_ge(mean_ready, 1)
            act.activation(std[:], ssb[:, S:], ACT.Sqrt).then_inc(std_ready, 1)
            act.activation(xstd[:], ssb[:, 0:S], ACT.Sqrt, bias=eps[:], scale=1.0 / D).then_inc(xstd_ready, 1)

            def split_after(T):
                c = (T + 2 - T_B2) // 2
                split(T + 2, C2_B2 + c // 2, c % 2, T % 2)

            for t in range(8):
                split_after(T_B2 + t)

            def angles(j):
                if j >= 2:
                    act.wait_ge(trig_ready, j - 1)
                    act.wait_ge(phase_ready, j - 1)
                act.activation(km[j % 2][:], steps, ACT.Identity, scale=freq[:, j:j + 1], bias=magic[:])
                act.activation(ph[j % 2][:], steps, ACT.Copy, scale=freq_hi[:, j:j + 1]).then_inc(angle_ready, 1)

            def trig(j):
                act.wait_ge(phase_ready, j + 1)
                if j >= 3:
                    act.wait_ge(state_ready, j - 2)
                elif j == 2:
                    act.wait_ge(cn2_ready, 1)
                act.activation(km[j % 2][:], ph[j % 2][:], ACT.Abs).then_inc(abs_ready, 1)
                act.activation(sin2[j % 3][:], ph[j % 2][:], ACT.Sin, scale=TWO_PI)
                act.wait_ge(abs_ready, j + 1)
                act.activation(cos2[j % 3][:], km[j % 2][:], ACT.Sin, scale=-TWO_PI, bias=half_pi[:]).then_inc(trig_ready, 1)

            act.wait_ge(ssm_const, 1)
            act.wait_ge(second_landed, 16)
            angles(0)
            angles(1)
            for s in range(PAIRS + 3):
                if s < PAIRS:
                    trig(s)
                if s + 2 < PAIRS:
                    angles(s + 2)
                for i in tiles_after(s):
                    split_after(T_B2 + 8 + i)
                if s + 1 in KSS:
                    a = KSS.index(s + 1)
                    act.wait_ge(evac_done, evacuated(T_B2 + 8 + a))
                    act.activation(ks[:, a, :], k2[:, a, :], ACT.Square).then_inc(ksq_ready, 1)
                if s - 1 in KSS:
                    a = KSS.index(s - 1)
                    act.wait_ge(kss_done, a + 1)
                    act.activation(ks[:, a, :], bank[3][:, 0:L2], ACT.Sqrt, bias=eps[:], scale=1.0 / HD2).then_inc(kstd_ready, 1)
                if s - 1 in VT2:
                    a = VT2.index(s - 1)
                    act.wait_ge(v2t_done, a + 1)
                    act.activation(vt2[:, :, 128 * a:128 * a + 128], bank[3][:, 0:256].rearrange("p (i n) -> p i n", i=2), ACT.Copy)
                    act.activation(vm2[:, 128 * a:128 * a + 128], bank[3][0:META, 256:384], ACT.Copy).then_inc(v2t_out, 1)
                if s - 1 in KSW:
                    a = KSW.index(s - 1)
                    act.wait_ge(ks_done, a + 1)
                    act.activation(ks[:, a, :], bank[3][:, 0:L2], ACT.Copy).then_inc(ks_ready, 1)
            act.wait_ge(evac_done, evacuated(T_GLU - 1))
            act.wait_ge(state_ready, PAIRS)
            act.wait_ge(y_done, PAIRS)
            act.activation(sq8[:], q2[:], ACT.Square).then_inc(qsq_ready, 1)
            act.wait_ge(qss_done, 1)
            act.activation(sq2[:], bank[3][:, 0:2 * H2].rearrange("p (a h) -> p a h", a=2), ACT.Sqrt, bias=eps[:], scale=1.0 / HD2)\
                .then_inc(qstd_ready, 1)
            y = u[:, :, META:]

            def gelu_square():
                act.wait_ge(y_out, T2)
                act.activation(gbuf[:], y, ACT.Square).then_inc(gelu_sq, 1)

            def gelu_tangent():
                act.wait_ge(gelu_in, 2)
                act.activation(gbuf[:], gbuf[:], ACT.Tanh, scale=float(np.sqrt(2.0 / np.pi))).then_inc(gelu_tanh, 1)

            def gelu_high():
                act.wait_ge(gelu_ready, 1)
                act.activation(act_hi[:, 8:16, :], y, ACT.Copy, scale=0.5).then_inc(ghi_ready, 1)

            def gate_out(t):
                act.wait_ge(tile_done, multiplied(T_GLU + t))
                for e in range(2):
                    n = 4 * (t // 2) + 2 * e + t % 2
                    if 2 * t + e >= 2:
                        act.wait_ge(gated, 2 * t + e - 1)
                    act.activation(gate[e][:], bank[2 + t % 2][:, 256 * e:256 * e + 256], ACT.Tanh, scale=0.5, bias=hb_glu[:, n:n + 1])\
                        .then_inc(gate_ready, 1)
                split_after(T_GLU + t)

            def half_squares(i, src):
                if i:
                    act.wait_ge(nss_ready, i)
                act.activation(sq8[:], src, ACT.Square).then_inc(nsq_ready, 1)

            def half_root(i, e):
                act.wait_ge(nssb_ready, i + 1)
                act.activation(nstd[:], nsb[:], ACT.Sqrt, bias=e[:], scale=1.0 / W2).then_inc(nstd_ready, 1)

            def half_high(i, src, t0):
                for t in range(T2):
                    act.wait_ge(nx_ready, T2 * i + t + 1)
                    act.activation(act_hi[:, t0 + t, :], src[:, t, :], ACT.Copy).then_inc(nhi_ready, 1)

            def exps2(h):
                act.wait_ge(nmax2_ready, h + 1)
                if h >= 4:
                    act.wait_ge(tr2_done, h - 3)
                for i, r in enumerate((slice(0, 145), slice(145, SBW))):
                    last = act.activation(prob2[h % 4][:, r], sb2[h % 2][:, r], ACT.Exp, bias=nmax2[h % 2][:, i:i + 1],
                                          accum_out=psums2[h % 2][:, i:i + 1])
                last.then_inc(exp2_done, 1)

            def weights2_out(h):
                act.wait_ge(tr2_done, h + 1)
                if h >= 2:
                    act.wait_ge(pv2_done, h - 1)
                for i in range(2):
                    act.activation(pM2[h % 2][:, 128 * i:128 * i + 128], bank[6 + h % 2][32 * i:32 * i + META, 384:512], ACT.Copy)
                act.activation(pT2[h % 2][:], bank[6 + h % 2][:, 0:384], ACT.Copy).then_inc(pt2_ready, 1)

            for s in range(H2 + 4):
                if s < H2:
                    exps2(s)
                if 2 <= s < H2 + 2:
                    weights2_out(s - 2)
                if s >= 4 and s % 2 == 1:
                    act.wait_ge(pv2_done, s - 3)
                    act.activation(at2[:, (s - 4) // 2, :], bank[(s - 4) // 2 % 2][:, 0:256], ACT.Copy).then_inc(at2_ready, 1)
                if s == 0:
                    gelu_square()
                if s == 2:
                    gelu_tangent()
                if s == 4:
                    gelu_high()
                for t in gate_at(s):
                    gate_out(t)
                if s == H2:
                    act.wait_ge(gated, 8)
                    half_squares(0, gbuf[:])
                if s == H2 + 2:
                    half_root(0, eps16)

            act.wait_ge(at2_ready, T2)
            half_squares(1, at2[:])
            half_high(0, gbuf, 8)
            half_root(1, eps)
            half_high(1, at2, 0)
            with act.Fori(0, C_O2 // 2) as q:
                for t in range(4):
                    j = 4 * q + t
                    split(T_O2 + j + 2, C2_B2 + 6 + q + (t // 2 + 1) // 2, (1 + t // 2) % 2, t % 2)
                    act.wait_ge(acc_done, KT * 5 + j + 1)
                    act.wait_ge(evac_done, evacuated(T_O2 + j))
                    gained(j, ("mlp2_g", j))
                    squared(j, t)
            root(5)
            ffn(T_FFN2, C2_B2 + 10, H_B2)

        @block.vector
        def _(dve):
            dve.sem_inc(lo_ready, 8)
            dve.sem_inc(evac_done, 4)

            def split(T, r, j):
                for h in range(2):
                    dve.wait_ge(hi_ready, 2 * T + h + 1)
                    dve.tensor_tensor(lo[j][:, 8 * h:8 * h + 8, :], raw[r][:, 8 * h:8 * h + 8, P * j:P * j + P],
                                      hi[j][:, 8 * h:8 * h + 8, :].bitcast(F32), ALU.subtract).then_inc(lo_ready, 1)

            def gained(n, j, gain):
                dve.wait_ge(xhi_ready, KT * n + j + 1)
                dve.scalar_tensor_tensor(out=xg_lo[:, bass.ds(j, 1), META:], in0=x[:, bass.ds(j, 1), :], scalar=par_at(*gain),
                                         in1=xg_hi[:, bass.ds(j, 1), META:].bitcast(F32), op0=ALU.mult, op1=ALU.subtract).then_inc(xlo_ready, 1)

            def rooted(n):
                dve.wait_ge(std_ready, n + 1)
                dve.reciprocal(rstd[:, META:], std[:, 0:S]).then_inc(rstd_ready, 1)

            def add(T, b, j):
                dve.wait_ge(tile_done, multiplied(T))
                one = bank[b][:, 0:S].rearrange("p (a n) -> p a n", a=1)
                dve.tensor_tensor(x[:, bass.ds(j, 1), :], one, x[:, bass.ds(j, 1), :], ALU.add).then_inc(evac_done, 1)

            def ffn(T0, H0, n, after=None):
                def up(q, f, t):
                    T = T0 + 2 * T_UP * f + 4 * q + t
                    if t == 0:
                        dve.wait_ge(rstd_ready, n + 1)
                    dve.wait_ge(tile_done, multiplied(T))
                    dve.wait_ge(hlo_ready, H0 + T_UP * f + 4 * q + t + 1)
                    dve.scalar_tensor_tensor(out=relu[t % 2][:], in0=bank[t][:, 0:S], scalar=0.0, in1=rstd[:, META:],
                                             op0=ALU.max, op1=ALU.mult).then_inc(evac_done, 1)
                    split(T + 2, (1 + t // 2) % 2, t % 2)

                def down(q, f, t, ahead=True):
                    T = T0 + 2 * T_UP * f + T_UP + 4 * q + t
                    add(T, t, 4 * q + t)
                    if ahead:
                        split(T + 2, (1 + t // 2) % 2, t % 2)

                def ups(f):
                    with dve.Fori(0, C_UP // 2) as q:
                        for t in range(4):
                            up(q, f, t)

                with dve.Fori(0, FCH - 1) as f:
                    ups(f)
                    with dve.Fori(0, C_UP // 2) as q:
                        for t in range(4):
                            down(q, f, t)
                ups(FCH - 1)
                if after is not None:
                    with dve.Fori(0, C_UP // 2) as q:
                        for t in range(4):
                            down(q, FCH - 1, t)
                            after(4 * q + t)
                else:
                    with dve.Fori(0, C_UP // 2 - 1) as q:
                        for t in range(4):
                            down(q, FCH - 1, t)
                    for t in range(4):
                        down(C_UP // 2 - 1, FCH - 1, t, t < 2)

            dve.wait_ge(par_landed, 16)
            pairs = par_at("lamv", 0, DEPTH * 4).rearrange("p (l e v) -> p l e v", l=DEPTH, e=2)
            dve.tensor_tensor(lamp[:], pairs[:, :, :, 0], pairs[:, :, :, 1], ALU.mult).then_inc(lam_chain, 1)
            dve.tensor_tensor(gsub[:], par_at("subln", 0, DEPTH), par_at("laminit", DEPTH, DEPTH), ALU.mult).then_inc(lam_chain, 1)
            dve.wait_ge(lam_exp, 1)
            dve.tensor_tensor(lamd[:], lame[:, :, 1], lame[:, :, 0], ALU.subtract).then_inc(lam_chain, 1)
            dve.wait_ge(lam_chain, 3)
            dve.tensor_tensor(nlam[:], lamd[:], par_at("laminit", 0, DEPTH), ALU.subtract).then_inc(lam_chain, 1)
            dve.memset(ssum[:, 0:S], 0.0).then_inc(zeroed, 1)
            dve.wait_ge(zeroed, 1)
            split(0, 0, 0)
            for j in range(KT):
                if j % 4 == 0:
                    dve.wait_ge(x_landed[j // 4], 16)
                gained(0, j, ("attn_g", j))
                dve.wait_ge(sq_ready, j + 1)
                dve.wait_ge(acc_done, j + 4)
                dve.tensor_tensor(ssum[:, 0:S], ssum[:, 0:S], sq[j % 4][:], ALU.add).then_inc(acc_done, 1)
                if j == 11:
                    split(1, 0, 1)
            with dve.Fori(0, DEPTH) as l:
                T0 = l * TILES_LAYER

                def project(T, b, j):
                    dve.wait_ge(tile_done, multiplied(T))
                    one = bank[b][:, 0:S].rearrange("p (a n) -> p a n", a=1)
                    dve.tensor_tensor(proj[:, bass.ds(j, 1), :], one, rstd[:, META:].rearrange("p (a n) -> p a n", a=1), ALU.mult)\
                        .then_inc(evac_done, 1)

                rooted(2 * l)
                dve.wait_ge(rstd_ready, 2 * l + 1)
                for t in range(6):
                    project(T0 + t, t % 4, t)
                    split(T0 + t + 2, (t // 2 + 1) % 2, t % 2)
                for t in range(6, 8):
                    project(T0 + t, t % 4, t)
                    split(T0 + t + 2, 0, t % 2)
                dve.wait_ge(cstd_ready, 2 * l + 2)
                dve.reciprocal(crstd[:], cstd[:]).then_inc(crstd_ready, 1)
                for t in range(8, 10):
                    project(T0 + t, t % 4, t)
                    split(T0 + t + 2, 1, t % 2)
                dve.wait_ge(crstd_ready, l + 1)
                for j in range(QT + 1):
                    g = par_at("qa_g", l * QT + j) if j < QT else par_at("kva_g", l)
                    last = dve.scalar_tensor_tensor(out=proj[:, j, :], in0=proj[:, j, :], scalar=g, in1=crstd[:, j // QT, :],
                                                    op0=ALU.mult, op1=ALU.mult)
                last.then_inc(cn_ready, 1)
                with dve.Fori(0, 4) as q:
                    for t in range(4):
                        project(T0 + 10 + 4 * q + t, (2 + t) % 4, 10 + 4 * q + t)
                        split(T0 + 12 + 4 * q + t, t // 2, t % 2)
                for t in range(26, 28):
                    project(T0 + t, t % 4, t)
                    split(T0 + t + 2, 0, t % 2)
                for t in range(28, 30):
                    project(T0 + t, t % 4, t)
                dve.wait_ge(evac_done, evacuated(T0 + T_O - 1))
                dve.tensor_scalar(proj[:, QB:QB + 4, :], proj[:, QB:QB + 4, :], SCALE_B, None, ALU.mult).then_inc(qb_ready, 1)
                for j in range(2):
                    split(T0 + T_O + j, 0, j)

                def biased(u):
                    dve.wait_ge(score_done, UNITS * l + u + 1)
                    if u >= 2:
                        dve.wait_ge(exp_done, UNITS * l + u - 1)
                    s = bank[4 + u % 2][:, 0:384]
                    if u < CB0:
                        dve.scalar_tensor_tensor(out=sb[u % 2][:], in0=table("dist"), scalar=-SLOPES_B[u // 2], in1=s,
                                                 op0=ALU.mult, op1=ALU.add).then_inc(sb_ready, 1)
                    elif u < MLA0:
                        dve.scalar_tensor_tensor(out=sb[u % 2][:], in0=s, scalar=SCALE_C, in1=cbias_sb[:, u - CB0, :],
                                                 op0=ALU.mult, op1=ALU.add).then_inc(sb_ready, 1)
                    else:
                        dve.scalar_tensor_tensor(out=sb[u % 2][:], in0=s, scalar=SCALE_A, in1=table("mask"),
                                                 op0=ALU.mult, op1=ALU.add).then_inc(sb_ready, 1)
                    dve.wait_ge(sb_ready, UNITS * l + u + 1)
                    dve.tensor_reduce(nmax[u % 2][:, 0:1], sb[u % 2][:, 0:128], AX_X, ALU.max, negate=True)
                    dve.tensor_reduce(nmax[u % 2][:, 1:2], sb[u % 2][:, 128:384], AX_X, ALU.max, negate=True).then_inc(nmax_ready, 1)

                def normed(u):
                    w = prob[u % 4]
                    halves = ((0, slice(0, 128)), (1, slice(128, 384)))
                    dve.wait_ge(exp_done, UNITS * l + u + 1)
                    dve.reciprocal(rsums[u % 2][:], psums[u % 2][:]).then_inc(rsum_ready, 1)
                    dve.wait_ge(rsum_ready, UNITS * l + u + 1)
                    if u < CB0 and u % 2 == 1:
                        dve.tensor_scalar(nlr[:], rsums[1][:], nlam[:, bass.ds(l, 1)], None, ALU.mult).then_inc(map_ready, 1)
                        dve.wait_ge(map_ready, CB0 * l + u + 1)
                        for i, r in halves:
                            last = dve.scalar_tensor_tensor(out=w[:, r], in0=w[:, r], scalar=nlr[:, i:i + 1], in1=prob[(u - 1) % 4][:, r],
                                                            op0=ALU.mult, op1=ALU.add)
                    else:
                        for i, r in halves:
                            last = dve.tensor_scalar(w[:, r], w[:, r], rsums[u % 2][:, i:i + 1], None, ALU.mult)
                    last.then_inc(pn_ready if group_of(u)[1] else map_ready, 1)

                for s in range(UNITS + 5):
                    if s >= 5 and group_of(s - 5)[1] and group_of(s - 5)[0] >= HB:
                        g = group_of(s - 5)[0]
                        dve.wait_ge(ohi_ready, OTHERS * l + g - HB + 1)
                        dve.tensor_tensor(act_lo[:, mixed_tile(g), :], bank[g % 2][:, 0:256], act_hi[:, mixed_tile(g), :].bitcast(F32),
                                          ALU.subtract).then_inc(olo_ready, 1)
                    if s == CB0:
                        dve.wait_ge(cb_landed, 16 * l + 16)
                    if s < UNITS:
                        biased(s)
                    if 1 <= s < UNITS + 1:
                        normed(s - 1)
                    if 15 <= s < 15 + HB:
                        h = s - 15
                        dve.wait_ge(ostd_ready, 2 * l + h // 2 + 1)
                        dve.reciprocal(orstd[:, h, :], ostd[:, h, :]).then_inc(orstd_ready, 1)
                        dve.wait_ge(orstd_ready, HB * l + h + 1)
                        dve.wait_ge(ob_ready, HB * l + h + 1)
                        dve.scalar_tensor_tensor(out=ob[:, h, :], in0=ob[:, h, :], scalar=gsub[:, bass.ds(l, 1)], in1=orstd[:, h, :],
                                                 op0=ALU.mult, op1=ALU.mult).then_inc(on_ready, 1)
                    if 17 <= s < 17 + HB:
                        h = s - 17
                        dve.wait_ge(onhi_ready, HB * l + h + 1)
                        dve.tensor_tensor(act_lo[:, 8 + h, :], ob[:, h, :], act_hi[:, 8 + h, :].bitcast(F32), ALU.subtract)\
                            .then_inc(onlo_ready, 1)
                with dve.Fori(0, C_O // 2) as q:
                    for t in range(4):
                        T, j = T0 + T_O + 4 * q + t, 4 * q + t
                        add(T, t, j)
                        split(T + 2, (1 + t // 2) % 2, t % 2)
                        gained(2 * l + 1, j, ("mlp_g", l * KT + j))
                rooted(2 * l + 1)
                dve.wait_ge(meta_hi, l + 1)
                dve.tensor_tensor(xg_lo[:, :, 0:META], mg[:], xg_hi[:, :, 0:META].bitcast(F32), ALU.subtract)
                ffn(T0 + T_FFN, l * H_LAYER, 2 * l + 1, lambda j: gained(2 * l + 2, j, ("attn_g", (l + 1) * KT + j)))
            dve.wait_ge(ssm_const, 1)
            dve.reciprocal(den[:], den[:]).then_inc(ssm_div, 1)
            dve.wait_ge(ssm_div, 1)
            dve.tensor_tensor(cre[:], nre[:], den[:], ALU.mult)
            dve.tensor_tensor(cim[:], nim[:], den[:], ALU.mult).then_inc(ssm_div, 1)
            dve.wait_ge(ssb_ready, 5)
            dve.tensor_scalar(xrstd[:], ssb[:, 0:S], EPS / D, EPS * EPS, ALU.mult, ALU.add)
            dve.tensor_scalar(ssb[:, S:S + META], ssb[:, S:S + META], 1.0 / D, EPS, ALU.mult, ALU.add).then_inc(mean_chain, 1)
            dve.wait_ge(mean_chain, 1)
            dve.scalar_tensor_tensor(out=ssb[:, S + META:], in0=ssb[:, S + META:], scalar=1.0 / D, in1=xrstd[:], op0=ALU.mult, op1=ALU.add)\
                .then_inc(mean_ready, 1)
            dve.wait_ge(std_ready, 5)
            dve.reciprocal(rstd[:], std[:]).then_inc(rstd_ready, 1)
            dve.wait_ge(rstd_ready, 5)

            def split_after(T):
                split(T + 2, (T + 2 - T_B2) // 2 % 2, T % 2)

            def out_of_psum(T, b, dst, r):
                dve.wait_ge(tile_done, multiplied(T))
                dve.tensor_tensor(dst, bank[b][:, 0:dst.shape[1]], r, ALU.mult).then_inc(evac_done, 1)

            for t in range(8):
                out_of_psum(T_B2 + t, t % 4, u[:, t, :], rstd[:])
                split_after(T_B2 + t)
                if t == 0:
                    dve.wait_ge(xstd_ready, 1)
                    dve.reciprocal(xrstd[:], xstd[:]).then_inc(xrstd_ready, 1)
                    dve.wait_ge(xrstd_ready, 1)
                for k in range(2 * t, 2 * t + 2):
                    last = dve.scalar_tensor_tensor(out=x[:, k, :], in0=x[:, k, :], scalar=par_at("final_g", k), in1=xrstd[:],
                                                    op0=ALU.mult, op1=ALU.mult)
            last.then_inc(xn_ready, 1)

            def y_tile(i):
                dve.wait_ge(y_done, 4 * i + 4)
                dve.scalar_tensor_tensor(out=u[:, i, :], in0=u[:, i, :], scalar=par_at("ssm_d", i), in1=bank[2][:, 0:L2],
                                         op0=ALU.mult, op1=ALU.add).then_inc(y_out, 1)

            def rounded(j):
                dve.wait_ge(angle_ready, j + 1)
                dve.scalar_tensor_tensor(out=ph[j % 2][:], in0=km[j % 2][:], scalar=MAGIC, in1=ph[j % 2][:], op0=ALU.subtract,
                                         op1=ALU.subtract).then_inc(phase_chain, 1)

            def corrected(j):
                dve.wait_ge(phase_chain, 2 * j + 1)
                dve.scalar_tensor_tensor(out=ph[j % 2][:], in0=steps, scalar=freq_lo[:, j:j + 1], in1=ph[j % 2][:], op0=ALU.mult,
                                         op1=ALU.subtract).then_inc(phase_chain, 1)

            def bounded(j):
                dve.wait_ge(phase_chain, 2 * j + 2)
                dve.tensor_scalar(ph[j % 2][:], ph[j % 2][:], TURN_MAX, -TURN_MAX, ALU.min, ALU.max).then_inc(phase_ready, 1)

            def products(j):
                dve.wait_ge(bu_done, j + 1)
                dve.wait_ge(trig_ready, j + 1)
                if j >= 1:
                    dve.wait_ge(scan_ready, j)
                re, im = (bank[4 + 2 * (j % 2) + e][:, 0:L2] for e in range(2))
                c, s = cos2[j % 3][:], sin2[j % 3][:]
                for i, (a, w) in enumerate(((re, c), (im, s), (im, c), (re, s))):
                    last = dve.tensor_tensor(mprod[i][:], a, w, ALU.mult)
                last.then_inc(bu_out, 1)

            def driving(j):
                dve.wait_ge(bu_out, j + 1)
                dve.tensor_tensor(mprod[0][:], mprod[0][:], mprod[1][:], ALU.add)
                dve.tensor_tensor(mprod[2][:], mprod[2][:], mprod[3][:], ALU.subtract).then_inc(drive_ready, 1)

            def sums(j):
                dve.wait_ge(drive_ready, j + 1)
                if j >= 2:
                    dve.wait_ge(state_ready, j - 1)
                decay = mag[:, j:j + 1].to_broadcast([P, L2])
                dve.tensor_tensor_scan(zr[j % 2][:], decay, mprod[0][:], 0.0, ALU.mult, ALU.add)
                dve.tensor_tensor_scan(zi[j % 2][:], decay, mprod[2][:], 0.0, ALU.mult, ALU.add).then_inc(scan_ready, 1)

            for j in range(2):
                rounded(j)
                corrected(j)
                bounded(j)
            for s in range(PAIRS + 3):
                if s >= 7 and s % 4 == 3:
                    y_tile((s - 7) // 4)
                for now, ahead in ((products, rounded), (driving, corrected), (sums, bounded)):
                    if s < PAIRS:
                        now(s)
                    if s + 2 < PAIRS:
                        ahead(s + 2)
                for i in tiles_after(s):
                    T = T_B2 + 8 + i
                    dst, r = (k2[:, i, :], rstd[:]) if i < 2 else (v2[:, i - 2, :], rstd[:]) if i < 4 else (q2[:, i - 4, :], rstd[:, META:])
                    out_of_psum(T, i % 2, dst, r)
                    split_after(T)
                if s - 2 in KSS:
                    a = KSS.index(s - 2)
                    dve.wait_ge(kstd_ready, a + 1)
                    dve.reciprocal(ks[:, a, :], ks[:, a, :]).then_inc(krstd_ready, 1)
                    dve.wait_ge(krstd_ready, a + 1)
                    dve.scalar_tensor_tensor(out=k2[:, a, :], in0=k2[:, a, :], scalar=qk_g[:], in1=ks[:, a, :],
                                             op0=ALU.mult, op1=ALU.mult).then_inc(kn_ready, 1)
            y_tile(T2 - 1)
            dve.wait_ge(qstd_ready, 1)
            dve.reciprocal(rq2[:], sq2[:]).then_inc(rq2_ready, 1)
            y = u[:, :, META:]

            def gelu_argument():
                dve.wait_ge(gelu_sq, 1)
                dve.wait_ge(y_out, T2)
                dve.tensor_scalar(gbuf[:], gbuf[:], 0.044715, 1.0, ALU.mult, ALU.add).then_inc(gelu_in, 1)
                dve.wait_ge(gelu_in, 1)
                dve.tensor_tensor(gbuf[:], gbuf[:], y, ALU.mult).then_inc(gelu_in, 1)

            def gelu_twice():
                dve.wait_ge(gelu_tanh, 1)
                dve.scalar_tensor_tensor(out=y, in0=gbuf[:], scalar=1.0, in1=y, op0=ALU.add, op1=ALU.mult).then_inc(gelu_ready, 1)

            def gelu_low():
                dve.wait_ge(ghi_ready, 1)
                dve.scalar_tensor_tensor(out=act_lo[:, 8:16, :], in0=y, scalar=0.5, in1=act_hi[:, 8:16, :].bitcast(F32), op0=ALU.mult,
                                         op1=ALU.subtract).then_inc(glo_ready, 1)

            def gate_times(t):
                for e in range(2):
                    n = 4 * (t // 2) + 2 * e + t % 2
                    dve.wait_ge(gate_ready, 2 * t + e + 1)
                    dve.scalar_tensor_tensor(out=gbuf[:, n, :], in0=gate[e][:], scalar=1.0, in1=y[:, n, :], op0=ALU.add, op1=ALU.mult)\
                        .then_inc(gated, 1)
                dve.wait_ge(gated, 2 * t + 2)
                dve.sem_inc(evac_done, 1)
                split_after(T_GLU + t)

            def half_sums(i):
                dve.wait_ge(nsq_ready, i + 1)
                if i:
                    dve.wait_ge(nssb_ready, i)
                dve.tensor_reduce(nsum[:], sq8[:].rearrange("p k n -> p n k"), AX_X, ALU.add).then_inc(nss_ready, 1)

            def half_rooted(i):
                dve.wait_ge(nstd_ready, i + 1)
                dve.reciprocal(nrstd[:], nstd[:]).then_inc(nrstd_ready, 1)
                dve.wait_ge(nrstd_ready, i + 1)

            def half_scaled(src, t, gain):
                dve.scalar_tensor_tensor(out=src[:, t, :], in0=src[:, t, :], scalar=par_at(gain, t), in1=nrstd[:],
                                         op0=ALU.mult, op1=ALU.mult).then_inc(nx_ready, 1)

            def half_low(i, src, t, t0):
                dve.wait_ge(nhi_ready, T2 * i + t + 1)
                dve.tensor_tensor(act_lo[:, t0 + t, :], src[:, t, :], act_hi[:, t0 + t, :].bitcast(F32), ALU.subtract).then_inc(nlo_ready, 1)

            def biased2(h):
                dve.wait_ge(score2_done, h + 1)
                dve.wait_ge(bias2_ready, h + 1)
                for a, r in enumerate((slice(0, 144), slice(144, 416))):
                    last = dve.scalar_tensor_tensor(out=sb2[h % 2][:, r.start + 1:r.stop + 1], in0=bank[4 + h % 2][:, r],
                                                    scalar=rq2[:, a, h:h + 1], in1=bias2[h % 2][:, r], op0=ALU.mult, op1=ALU.add)
                last.then_inc(sb2_ready, 1)
                dve.wait_ge(sb2_ready, h + 1)
                dve.tensor_reduce(nmax2[h % 2][:, 0:1], sb2[h % 2][:, 0:145], AX_X, ALU.max, negate=True)
                dve.tensor_reduce(nmax2[h % 2][:, 1:2], sb2[h % 2][:, 145:SBW], AX_X, ALU.max, negate=True).then_inc(nmax2_ready, 1)

            def normed2(h):
                dve.wait_ge(exp2_done, h + 1)
                dve.reciprocal(rsums2[h % 2][:], psums2[h % 2][:]).then_inc(rsum2_ready, 1)
                dve.wait_ge(rsum2_ready, h + 1)
                for i, r in enumerate((slice(1, 145), slice(145, 417))):
                    last = dve.tensor_scalar(prob2[h % 4][:, r], prob2[h % 4][:, r], rsums2[h % 2][:, i:i + 1], None, ALU.mult)
                last.then_inc(pn2_ready, 1)

            dve.wait_ge(rq2_ready, 1)
            for s in range(H2 + 2):
                if s < H2:
                    biased2(s)
                if 1 <= s < H2 + 1:
                    normed2(s - 1)
                if s == 1:
                    gelu_argument()
                if s == 3:
                    gelu_twice()
                if s == 5:
                    gelu_low()
                for t in gate_at(s - 1):
                    gate_times(t)
                if s == H2 + 1:
                    half_sums(0)

            half_rooted(0)
            for t in range(T2):
                half_scaled(gbuf, t, "ssm2_g")
            half_sums(1)
            for t in range(T2):
                half_low(0, gbuf, t, 8)
            half_rooted(1)
            for t in range(T2 + 2):
                if t < T2:
                    half_scaled(at2, t, "attn2_g")
                if t >= 2:
                    half_low(1, at2, t - 2, 0)
            dve.wait_ge(xn_ready, 1)
            with dve.Fori(0, C_O2 // 2) as q:
                for t in range(4):
                    T, j = T_O2 + 4 * q + t, 4 * q + t
                    add(T, t, j)
                    split(T + 2, (1 + t // 2) % 2, t % 2)
                    gained(5, j, ("mlp2_g", j))
            rooted(5)
            ffn(T_FFN2, H_B2, 5)

        @block.gpsimd
        def _(pool):
            pool.sem_inc(hlo_ready, 2)
            pool.sem_inc(acc_done, 4)
            pool.dma_start(meta[:], metaT).then_inc(meta_landed, 16)
            pool.memset(ones[:], 1.0)
            pool.memset(half_pi[:], np.pi / 2)
            pool.memset(magic[:], MAGIC)
            pool.memset(eps16[:], 16 * EPS)
            pool.memset(eps[:], EPS).then_inc(const_ready, 1)
            pool.wait_ge(lam_chain, 1)
            pool.partition_all_reduce(lams[:].rearrange("p l e -> p (l e)"), lamp[:].rearrange("p l e -> p (l e)"), P, RADD).then_inc(lam_sum, 1)

            def step(ins):
                ssm_steps[0] += 1
                ins.then_inc(ssm_chain, 1)
                pool.wait_ge(ssm_chain, ssm_steps[0])

            def less(o, a, c, b):
                step(pool.tensor_scalar(t1[:], a[:], c, None, ALU.mult))
                step(pool.tensor_tensor(o[:], b[:], t1[:], ALU.subtract))

            ssm_steps = [0]
            pool.wait_ge(par_landed, 16)
            lre, lim = par_at("lam_re", 0, PAIRS), par_at("lam_im", 0, PAIRS)
            pool.wait_ge(ssm_exp, 1)
            step(pool.tensor_tensor(dr[:], lre, dl[:], ALU.mult))
            step(pool.tensor_tensor(th[:], lim, dl[:], ALU.mult))
            step(pool.tensor_scalar(turns[:], th[:], 1.0 / TWO_PI, MAGIC, ALU.mult, ALU.add))
            step(pool.tensor_scalar(turns[:], turns[:], MAGIC, None, ALU.subtract))
            less(ang, turns, PI2_A, th)
            less(ang, turns, PI2_B, ang)
            less(ang, turns, PI2_C, ang)
            step(pool.tensor_scalar(angc[:], ang[:], SIN_MAX, -SIN_MAX, ALU.min, ALU.max))
            step(pool.tensor_scalar(freq[:], ang[:], 1.0 / TWO_PI, None, ALU.mult))
            step(pool.tensor_scalar(freq_hi[:], freq[:], MAGIC15, MAGIC15, ALU.add, ALU.subtract))
            less(t0, freq_hi, PI2_A, ang)
            less(t0, freq_hi, PI2_B, t0)
            less(t0, freq_hi, PI2_C, t0)
            step(pool.tensor_scalar(freq_lo[:], t0[:], 1.0 / TWO_PI, None, ALU.mult))
            pool.wait_ge(meta_landed, 16)
            gains = par_at("mix2_g", 0, KT).rearrange("p (k a) -> p k a", a=1).to_broadcast([P, KT, META])
            pool.tensor_tensor(mg[:], meta[:], gains, ALU.mult).then_inc(mg_ready, 1)
            pool.wait_ge(mg_ready, 1)
            pool.tensor_tensor(meta[:], meta[:], meta[:], ALU.mult).then_inc(meta_ss, 1)
            for i, n in enumerate((8, 4, 2, 1)):
                pool.wait_ge(meta_ss, i + 1)
                dst = meta[:, 0:n, :] if n > 1 else msum[:].rearrange("p (a n) -> p a n", a=1)
                pool.tensor_tensor(dst, meta[:, 0:n, :], meta[:, n:2 * n, :], ALU.add).then_inc(meta_ss, 1)
            pool.wait_ge(meta_ss, 5)
            pool.tensor_tensor(par_at("attn_g", DEPTH * KT, KT), par_at("final_g", 0, KT), par_at("mix2_g", 0, KT), ALU.mult)\
                .then_inc(gain_ready, 1)

            def added(n, j, t, final=False):
                if t == 0:
                    pool.wait_ge(zeroed, n + 1)
                pool.wait_ge(sq_ready, KT * n + j + 1)
                pool.wait_ge(acc_done, KT * n + j + 4)
                last = pool.tensor_tensor(ssum[:, 0:S], ssum[:, 0:S], sq[t][:], ALU.add)
                if final:
                    last = pool.tensor_tensor(ssum[:, S + META:], ssum[:, S + META:], sqf[t][:], ALU.add)
                last.then_inc(acc_done, 1)

            def zero(n):
                pool.wait_ge(sq_ready, KT * n + 1)
                pool.tensor_tensor(scratch[:], eps[:], eps[:], ALU.add)
                pool.memset(ssum[:, 0:S], 0.0)
                pool.tensor_copy(ssum[:, S:S + META], msum[:])
                pool.memset(ssum[:, S + META:], 0.0).then_inc(zeroed, 1)

            def spread(n):
                pool.wait_ge(acc_done, KT * n + KT + 4)
                pool.tensor_tensor(scratch[:], eps[:], eps[:], ALU.add)
                pool.partition_all_reduce(ssb[:, 0:S], ssum[:, 0:S], P, RADD).then_inc(ssb_ready, 1)

            pool.wait_ge(ssm_exp, 5)
            step(pool.tensor_tensor(lb1[:], mag[:], cs[:], ALU.mult))
            step(pool.tensor_scalar(lb1[:], lb1[:], 1.0, None, ALU.subtract))
            step(pool.tensor_tensor(lbi[:], mag[:], sn[:], ALU.mult))
            step(pool.tensor_tensor(t0[:], lb1[:], lre, ALU.mult))
            step(pool.tensor_tensor(t1[:], lbi[:], lim, ALU.mult))
            step(pool.tensor_tensor(nre[:], t0[:], t1[:], ALU.add))
            step(pool.tensor_tensor(t0[:], lbi[:], lre, ALU.mult))
            step(pool.tensor_tensor(t1[:], lb1[:], lim, ALU.mult))
            step(pool.tensor_tensor(nim[:], t0[:], t1[:], ALU.subtract))
            step(pool.tensor_tensor(t0[:], lre, lre, ALU.mult))
            step(pool.tensor_tensor(t1[:], lim, lim, ALU.mult))
            step(pool.tensor_tensor(den[:], t0[:], t1[:], ALU.add))
            step(pool.tensor_tensor(qk_g[:], par_at("q2_g"), par_at("k2_g"), ALU.mult))
            step(pool.tensor_scalar(qk_g[:], qk_g[:], SCALE_2, None, ALU.mult))
            pool.tensor_scalar(hb_glu[:], par_at("b_glu", 0, T2), 0.5, None, ALU.mult).then_inc(ssm_const, 1)

            def ffn(T0, H0):
                with pool.Fori(0, FCH) as f:
                    with pool.Fori(0, C_UP // 2) as q:
                        for t in range(4):
                            H = H0 + T_UP * f + 4 * q + t
                            pool.wait_ge(evac_done, evacuated(T0 + 2 * T_UP * f + 4 * q + t))
                            pool.tensor_tensor(rsq[t % 2][:], relu[t % 2][:], relu[t % 2][:], ALU.mult).then_inc(rr_ready, 1)
                            pool.wait_ge(rr_ready, H + 1)
                            pool.wait_ge(hhi_ready, H + 1)
                            pool.tensor_tensor(act_lo[:, bass.ds(4 * q + t, 1), :], rsq[t % 2][:].rearrange("p (a n) -> p a n", a=1),
                                               act_hi[:, bass.ds(4 * q + t, 1), :].bitcast(F32), ALU.subtract).then_inc(hlo_ready, 1)

            pool.wait_ge(tab_landed, 16)
            with pool.Fori(0, DEPTH) as l:
                T0 = l * TILES_LAYER
                spread(2 * l)
                pool.wait_ge(csq_ready, l + 1)
                pool.tensor_tensor(csum[:], csq[:, 0, :], csq[:, 1, :], ALU.add).then_inc(csum_ready, 1)
                pool.wait_ge(csum_ready, 2 * l + 1)
                pool.tensor_tensor(csq[:, 2, :], csum[:], csq[:, 2, :], ALU.add).then_inc(csum_ready, 1)
                pool.wait_ge(csum_ready, 2 * l + 2)
                pool.tensor_tensor(scratch[:], eps[:], eps[:], ALU.add)
                pool.partition_all_reduce(cssb[:].rearrange("p a n -> p (a n)"), csq[:, 2:4, :].rearrange("p a n -> p (a n)"), P, RADD)\
                    .then_inc(cssb_ready, 1)

                def rotate(t, o, a, b, ready):
                    for i, (h, w) in enumerate(((a, "cos"), (b, "sin"), (b, "cos"), (a, "sin"))):
                        last = pool.tensor_tensor(t[i], h, table(w), ALU.mult)
                    last.then_inc(ready[0], 1)
                    pool.wait_ge(ready[0], ready[1])
                    pool.tensor_tensor(o[0], t[0], t[1], ALU.subtract)
                    return pool.tensor_tensor(o[1], t[2], t[3], ALU.add)

                pool.wait_ge(evac_done, evacuated(T0 + 5))
                rotate([rkt[:, i, :] for i in range(4)], [kr[:, 0, :], kr[:, 1, :]], kr[:, 0, :], kr[:, 1, :], (krt_ready, l + 1))\
                    .then_inc(kr_ready, 1)
                pool.wait_ge(uq_out, 14 * l + 2)
                for a in range(2):
                    last = rotate([rt[:, i, a, :] for i in range(4)], [qr[:, 0, a, :], qr[:, 1, a, :]], rq[:, 0, a, :], rq[:, 1, a, :],
                                  (rt_ready, 2 * l + a + 1))
                last.then_inc(qr_ready, 1)
                zero(2 * l + 1)
                with pool.Fori(0, C_O // 2) as q:
                    for t in range(4):
                        added(2 * l + 1, 4 * q + t, t)
                spread(2 * l + 1)
                ffn(T0 + T_FFN, l * H_LAYER)
                zero(2 * l + 2)
                with pool.Fori(0, KT // 4) as q:
                    for t in range(4):
                        added(2 * l + 2, 4 * q + t, t, final=True)
            pool.wait_ge(acc_done, KT * 5 + 4)
            pool.partition_all_reduce(ssb[:], ssum[:], P, RADD).then_inc(ssb_ready, 1)
            pool.dma_start(tab2, tables2).then_inc(second_landed, 16)
            pool.wait_ge(evac_done, evacuated(T_B2 - 1))
            pool.dma_start(bm[:], bmat).then_inc(mats_landed, 16)
            pool.dma_start(cm[:], cmat).then_inc(mats_landed, 16)
            pool.wait_ge(mats_landed, 32)
            pool.wait_ge(ssm_div, 2)
            cr, ci = (v[:].rearrange("p (j a) -> p j a", a=1).to_broadcast([P, PAIRS, 32]) for v in (cre, cim))
            for i, (a, b) in enumerate(((0, cr), (1, ci), (0, ci), (1, cr))):
                dst = cn[:, i // 2] if i % 2 == 0 else ctmp[:, i // 2]
                last = pool.tensor_tensor(dst, cm[:, a], b, ALU.mult)
            last.then_inc(cmul_ready, 1)
            pool.wait_ge(cmul_ready, 1)
            pool.tensor_tensor(cn[:, 0], cn[:, 0], ctmp[:, 0], ALU.subtract)
            pool.tensor_tensor(cn[:, 1], cn[:, 1], ctmp[:, 1], ALU.add).then_inc(cmul_ready, 1)
            pool.wait_ge(cmul_ready, 2)
            pool.tensor_scalar(cn[:, 1], cn[:, 1], -1.0, 0.0, ALU.mult, ALU.add).then_inc(cn2_ready, 1)
            for j in range(PAIRS):
                c, s = cos2[j % 3][:], sin2[j % 3][:]
                pool.wait_ge(scan_ready, j + 1)
                if j >= 3:
                    pool.wait_ge(y_done, j - 2)
                if j >= 1:
                    pool.wait_ge(state_ready, j)
                for i, (w, z) in enumerate(((c, zr), (s, zi), (s, zr), (c, zi))):
                    last = pool.tensor_tensor(pprod[i][:], w, z[j % 2][:], ALU.mult)
                last.then_inc(turn_ready, 1)
                pool.wait_ge(turn_ready, j + 1)
                pool.tensor_tensor(wr[j % 3][:], pprod[0][:], pprod[1][:], ALU.subtract)
                pool.tensor_tensor(wi[j % 3][:], pprod[2][:], pprod[3][:], ALU.add).then_inc(state_ready, 1)

            pool.wait_ge(evac_done, evacuated(T_GLU - 1))
            for h in range(H2):
                if h >= 2:
                    pool.wait_ge(sb2_ready, h - 1)
                    pool.wait_ge(exp2_done, h - 1)
                pool.tensor_scalar(bias2[h % 2][:], dist2, -SLOPES_2[h], 0.0, ALU.mult, ALU.add)
                pool.tensor_copy(sb2[h % 2][:, 0:1], par_at("sinks", h))
                pool.tensor_copy(sb2[h % 2][:, SBW - 1:SBW], par_at("sinks", h)).then_inc(bias2_ready, 1)
            for i in range(2):
                if i:
                    pool.wait_ge(nstd_ready, i)
                pool.wait_ge(nss_ready, i + 1)
                pool.partition_all_reduce(nsb[:], nsum[:], P, RADD).then_inc(nssb_ready, 1)
            zero(5)
            with pool.Fori(0, C_O2 // 2) as q:
                for t in range(4):
                    added(5, 4 * q + t, t)
            spread(5)
            ffn(T_FFN2, H_B2)


def feature_major(a):
    n, d = a.shape
    return a.T.reshape(d // P, P, n).transpose(1, 0, 2)


def columns(v):
    return v.reshape(-1, P).T


def chunks(w):
    return w.reshape(KT, P, -1, CW).transpose(2, 1, 0, 3).reshape(-1, P, CE)


def padded(w, k):
    c = np.zeros((1, P, CE), np.float32)
    c[0, :, 0:w.size // P] = w.reshape(k, P, -1).transpose(1, 0, 2).reshape(P, -1)
    return c


def ffn_chunks(up, down):
    f = D
    return [c for i in range(FCH) for c in (chunks(up[:, f * i:f * i + f]), chunks(down[f * i:f * i + f]))]


def weight_stream(a):
    parts = []
    r0, rh = Q_RANK + KV_RANK, A_ROPE // 2
    for l in range(DEPTH):
        w = a["w_in"][l]
        rotary = [np.tile(w[:, r0 + rh * e:r0 + rh * e + rh], (1, 4)) for e in range(2)]
        parts.append(chunks(np.concatenate([w[:, :r0]] + rotary + [w[:, r0 + A_ROPE:]], 1)))
        w = a["w_uq"][l].reshape(Q_RANK, HA, A_NOPE + A_ROPE)
        halves = [w[:, :, A_NOPE + rh * e:A_NOPE + rh * e + rh].reshape(Q_RANK, -1) for e in range(2)]
        w = np.concatenate(halves + [w[:, :, :A_NOPE].reshape(Q_RANK, -1)], 1)
        parts += [padded(w[:, :768], QT), padded(w[:, 768:], QT)]
        w = a["w_ukv"][l].reshape(KV_RANK, HA, A_NOPE + A_V)
        parts.append(padded(np.concatenate([w[:, :, :A_NOPE].reshape(P, -1), w[:, :, A_NOPE:].reshape(P, -1)], 1), 1))
        parts.append(chunks(a["w_o"][l]))
        parts += ffn_chunks(a["w_up"][l], a["w_down"][l])
    w = a["w_in_2"][0]
    q, k, v, u = np.split(w, [W2, W2 + KV2 * HD2, W2 + 2 * KV2 * HD2], 1)
    parts += [chunks(u), chunks(k), chunks(v), chunks(q)]
    parts.append(a["w_glu_2"][0].reshape(T2, P, 2, 512).transpose(2, 1, 0, 3).reshape(2, P, CE))
    parts.append(chunks(a["w_out_2"][0]))
    parts += ffn_chunks(a["w_up_2"][0], a["w_down_2"][0])
    s = np.concatenate(parts, 0)
    assert s.shape[0] == C_ALL
    return s


def small_params(a):
    m = np.zeros((P, NPAR), np.float32)

    def put(name, v, i=0):
        m[:v.shape[0], COLS[name] + i:COLS[name] + i + v.shape[1]] = v

    for l in range(DEPTH):
        put("attn_g", columns(a["attn_norm"][l]), l * KT)
        put("mlp_g", columns(a["mlp_norm"][l]), l * KT)
        put("qa_g", columns(a["q_a_norm"][l]), l * QT)
        put("kva_g", columns(a["kv_a_norm"][l]), l)
        put("subln", columns(a["diff_subln"][l]), l)
        for i, n in enumerate(("lambda_q1", "lambda_k1", "lambda_q2", "lambda_k2")):
            put("lamv", a[n][l][:, None], 4 * l + i)
        m[:, COLS["laminit"] + l] = lam_init(l)
        m[:, COLS["laminit"] + DEPTH + l] = 1.0 - lam_init(l)
    put("final_g", columns(a["final_norm"]))
    put("mix2_g", columns(a["norm_mix_g_2"][0]))
    put("mlp2_g", columns(a["norm_mlp_g_2"][0]))
    put("q2_g", np.tile(a["q_norm_g_2"][0], 2)[:, None])
    put("k2_g", np.tile(a["k_norm_g_2"][0], 2)[:, None])
    put("attn2_g", columns(a["attn_out_g_2"][0]))
    put("ssm2_g", columns(a["ssm_out_g_2"][0]))
    put("ssm_d", columns(a["ssm_d_2"][0]))
    put("b_glu", columns(a["b_glu_2"][0]))
    put("lam_re", a["ssm_lambda_re_2"][0].reshape(PAIRS, P).T)
    put("lam_im", a["ssm_lambda_im_2"][0].reshape(PAIRS, P).T)
    put("log_step", np.repeat(a["ssm_log_step_2"][0].reshape(PAIRS, 2), P // 2, axis=1).T)
    put("sinks", np.tile(a["attn_sinks_2"][0][None], (P, 1)))
    return m


def shape_tables():
    t = np.zeros((P, NTAB), np.float32)
    i = np.arange(P)

    def put(name, v):
        t[:, TABLES[name][0]:TABLES[name][0] + TABLES[name][1]] = v

    half = A_ROPE // 2
    freq = np.float32(10000.0) ** (-np.arange(half, dtype=np.float32) / np.float32(half))
    angle = np.arange(S, dtype=np.float32)[None, :] * freq[i % half][:, None]
    put("ident", np.eye(P))
    put("halves", (i[:, None] // 64 == i[None, :] // 64))
    put("cos", np.cos(angle))
    put("sin", np.sin(angle))
    q = np.concatenate([np.tile(i[:, None], (1, 128)), np.tile(i[:, None] + 128, (1, 256))], 1)
    k = np.concatenate([np.arange(128), np.arange(256)])[None, :]
    hidden = k // CHUNK > q // CHUNK
    put("mask", np.where(hidden, -BIG, 0.0))
    put("dist", np.where(hidden, BIG, np.abs(q - k)))
    t2 = np.zeros((P, NTAB2), np.float32)
    q = np.concatenate([np.tile(i[:, None] + META, (1, 144)), np.tile(i[:, None] + META + 128, (1, 272))], 1)
    k = np.concatenate([np.arange(144), np.arange(272)])[None, :]
    seen = (k <= q) & ((k < META) | (q - k < WINDOW))
    t2[:, 0:416] = np.where(seen, q - k, BIG)
    t2[:, 416:] = np.arange(L2)[None, :]
    return t, t2


def band_bias(rel):
    i = np.arange(P)
    q = np.concatenate([np.tile(i[:, None], (1, 128)), np.tile(i[:, None] + 128, (1, 256))], 1)
    k = np.concatenate([np.arange(128), np.arange(256)])[None, :]
    at = np.clip(q - k, 1 - CHUNK, REL_CLIP) + CHUNK - 1
    b = np.where((k // CHUNK > q // CHUNK)[None, None], np.float32(-BIG), rel[:, :, at])
    return np.ascontiguousarray(b.transpose(0, 2, 1, 3))


def ssm_matrices(a):
    b = np.zeros((P, 2, T2, P), np.float32)
    c = np.zeros((P, 2, PAIRS, 32), np.float32)
    for e, (bn, cn) in enumerate((("ssm_b_re_2", "ssm_c_re_2"), ("ssm_b_im_2", "ssm_c_im_2"))):
        for g in range(64):
            j, h = g // 2, g % 2
            r = 32 * (j % 4) + 16 * h
            b[r:r + 16, e, j // 4, 64 * h:64 * h + 64] = a[bn][0, g].T
            c[64 * h:64 * h + 64, e, j, 16 * h:16 * h + 16] = a[cn][0, g].T
    return b, c


def arrays_of(inputs):
    a = {k: np.asarray(v) for k, v in inputs.items()}
    t, t2 = shape_tables()
    b, c = ssm_matrices(a)
    return {
        "stream": weight_stream(a), "params": small_params(a), "tables": t, "tables2": t2, "cbias": band_bias(a["rel_bias"]),
        "xT": np.ascontiguousarray(feature_major(a["x"][0])), "metaT": np.ascontiguousarray(feature_major(a["meta_tokens_2"])),
        "bmat": b, "cmat": c,
    }


def kernel(**inputs):
    from concourse import bacc
    from concourse.bass_utils import run_bass_kernel_spmd

    arrays = arrays_of(inputs)
    nc = bacc.Bacc("TRN2", target_bir_lowering=False, num_devices=1)
    args = [nc.dram_tensor(n, v.shape, F32, kind="ExternalInput").ap() for n, v in arrays.items()]
    args.append(nc.dram_tensor("out", (P, KT, S), F32, kind="ExternalOutput").ap())
    build(nc, *args)
    got = run_bass_kernel_spmd(nc, [arrays], core_ids=[0]).results[0]["out"]
    return np.ascontiguousarray(got.transpose(2, 1, 0).reshape(1, S, D))
```
